# Optimizing a Trainium2 kernel written in Bass

```python
import math
import jax
import jax.numpy as jnp
from jax import lax
import numpy as np

D_MODEL = 1024
BATCH = 1
SEQ = 256
DEPTH = 1

NORM_EPS = 1e-6
GDN_HEADS = 4
GDN_HEAD_DIM = 128
GDN_WIDTH = GDN_HEADS * GDN_HEAD_DIM
GDN_CONV = 4
GDN_CHUNK = 64
NSA_HEADS = 8
NSA_KV_GROUPS = 2
NSA_GROUP_HEADS = NSA_HEADS // NSA_KV_GROUPS
NSA_HEAD_DIM = 64
NSA_WIDTH = NSA_HEADS * NSA_HEAD_DIM
NSA_KV_WIDTH = NSA_KV_GROUPS * NSA_HEAD_DIM
CMP_BLOCK = 32
CMP_STRIDE = 16
CMP_HIDDEN = 128
SEL_BLOCK = 64
SEL_COUNT = 16
WINDOW = 512
Q_BLOCK = 128
ROPE_THETA = 500000.0
ROPE_DIM = NSA_HEAD_DIM // 4
FORCED_SCORE = 1000.0
NEG_INF = -1e30
FFN_HIDDEN = -(-8 * D_MODEL // (3 * 256)) * 256
IN_SIZES = (3 * GDN_WIDTH, GDN_WIDTH, GDN_HEADS, GDN_HEADS,
            NSA_WIDTH, NSA_KV_WIDTH, NSA_KV_WIDTH, NSA_KV_WIDTH, NSA_KV_WIDTH, NSA_KV_WIDTH, NSA_KV_WIDTH,
            3 * NSA_HEADS, D_MODEL, D_MODEL)
IN_WIDTH = 4 * GDN_WIDTH + 2 * GDN_HEADS + NSA_WIDTH + 6 * NSA_KV_WIDTH + 3 * NSA_HEADS + 2 * D_MODEL


def rms_norm(x, gain):
    x32 = x.astype(jnp.float32)
    y = x32 * lax.rsqrt(jnp.mean(x32 * x32, axis=-1, keepdims=True) + NORM_EPS)
    return (y * gain.astype(jnp.float32)).astype(x.dtype)

def l2_normalize(x):
    return x * lax.rsqrt(jnp.sum(x * x, axis=-1, keepdims=True) + NORM_EPS)

def causal_depthwise_conv(x, w):
    k_len, ch = w.shape
    return lax.conv_general_dilated(x, w[:, None, :].astype(x.dtype), window_strides=(1,),
                                    padding=[(k_len - 1, 0)], dimension_numbers=('NWC', 'WIO', 'NWC'),
                                    feature_group_count=ch)

def partial_rope(x, pos):
    half = ROPE_DIM // 2
    inv_freq = ROPE_THETA ** (-jnp.arange(half, dtype=jnp.float32) / half)
    ang = pos.astype(jnp.float32)[:, None] * inv_freq
    bshape = (pos.shape[0],) + (1,) * (x.ndim - 3) + (half,)
    cos = jnp.cos(ang).reshape(bshape)
    sin = jnp.sin(ang).reshape(bshape)
    x1 = x[..., :half].astype(jnp.float32)
    x2 = x[..., half:ROPE_DIM].astype(jnp.float32)
    rot = jnp.concatenate([x1 * cos - x2 * sin, x2 * cos + x1 * sin], axis=-1).astype(x.dtype)
    return jnp.concatenate([rot, x[..., ROPE_DIM:]], axis=-1)

def gated_delta_rule_chunked(q, k, v, beta, g):
    b_, s_, h_, dk = q.shape
    dv = v.shape[-1]
    c = GDN_CHUNK
    n = s_ // c

    def to_chunks(a):
        return a.reshape(b_, n, c, h_, a.shape[-1]).transpose(0, 3, 1, 2, 4)

    q, k, v = to_chunks(q), to_chunks(k), to_chunks(v)
    beta = beta.reshape(b_, n, c, h_).transpose(0, 3, 1, 2)
    gc = jnp.cumsum(g.reshape(b_, n, c, h_).transpose(0, 3, 1, 2), axis=-1)
    causal = jnp.tril(jnp.ones((c, c), dtype=bool))
    strict = jnp.tril(jnp.ones((c, c), dtype=bool), -1)
    decay = jnp.exp(jnp.where(causal, gc[..., :, None] - gc[..., None, :], -jnp.inf))
    kb = k * beta[..., None]
    a_low = jnp.where(strict, jnp.einsum('bhnid,bhnjd->bhnij', kb, k) * decay, 0.0)
    ia = a_low + jnp.eye(c, dtype=q.dtype)
    u = lax.linalg.triangular_solve(ia, v * beta[..., None], left_side=True, lower=True, unit_diagonal=True)
    w = lax.linalg.triangular_solve(ia, kb * jnp.exp(gc)[..., None], left_side=True, lower=True, unit_diagonal=True)
    qk = jnp.einsum('bhnid,bhnjd->bhnij', q, k) * decay
    qg = q * jnp.exp(gc)[..., None]
    kd = k * jnp.exp(gc[..., -1:] - gc)[..., None]
    g_last = jnp.exp(gc[..., -1])

    def step(state, inp):
        qk_n, qg_n, kd_n, u_n, w_n, gl_n = inp
        v_new = u_n - jnp.einsum('bhcd,bhde->bhce', w_n, state)
        o_n = jnp.einsum('bhcd,bhde->bhce', qg_n, state) + jnp.einsum('bhij,bhje->bhie', qk_n, v_new)
        state = state * gl_n[..., None, None] + jnp.einsum('bhcd,bhce->bhde', kd_n, v_new)
        return state, o_n

    xs = tuple(jnp.moveaxis(a, 2, 0) for a in (qk, qg, kd, u, w, g_last))
    state0 = jnp.zeros((b_, h_, dk, dv), dtype=q.dtype)
    _, o = lax.scan(step, state0, xs)
    return o.transpose(1, 0, 3, 2, 4).reshape(b_, s_, h_, dv)

def compress_blocks(kv, pos_emb, w1, w2):
    s_ = kv.shape[1]
    n_cmp = (s_ - CMP_BLOCK) // CMP_STRIDE + 1
    idx = jnp.arange(n_cmp)[:, None] * CMP_STRIDE + jnp.arange(CMP_BLOCK)[None, :]
    blocks = kv[:, idx] + pos_emb[:, None, :]
    hid = jax.nn.silu(jnp.einsum('bnlgd,ldh->bgnh', blocks, w1))
    return jnp.einsum('bgnh,hd->bgnd', hid, w2)

def native_sparse_attention(q, k_cmp, v_cmp, k_slc, v_slc, k_win, v_win, gates,
                            cmp_pos_k, cmp_w1_k, cmp_w2_k, cmp_pos_v, cmp_w1_v, cmp_w2_v):
    b_, s_, g_, r_, dh = q.shape
    n_cmp = (s_ - CMP_BLOCK) // CMP_STRIDE + 1
    n_blk = s_ // SEL_BLOCK
    n_top = min(SEL_COUNT, n_blk)
    kc = compress_blocks(k_cmp, cmp_pos_k, cmp_w1_k, cmp_w2_k)
    vc = compress_blocks(v_cmp, cmp_pos_v, cmp_w1_v, cmp_w2_v)
    cmp_start = jnp.arange(n_cmp) * CMP_STRIDE
    cmp_end = cmp_start + CMP_BLOCK - 1
    blk_ids = jnp.arange(n_blk)
    sel_start = blk_ids * SEL_BLOCK
    overlap = ((cmp_start[:, None] <= sel_start[None, :] + SEL_BLOCK - 1)
               & (cmp_end[:, None] >= sel_start[None, :])).astype(jnp.float32)

    def to_blocks(a):
        return a.reshape(b_, n_blk, SEL_BLOCK, g_, dh).transpose(0, 3, 1, 2, 4).reshape(b_ * g_ * n_blk, SEL_BLOCK, dh)

    ks_flat = to_blocks(k_slc)
    vs_flat = to_blocks(v_slc)
    base = ((jnp.arange(b_)[:, None] * g_ + jnp.arange(g_)[None, :]) * n_blk)[:, :, None, None]
    pad = ((0, 0), (WINDOW, 0), (0, 0), (0, 0))
    kw_pad = jnp.pad(k_win, pad)
    vw_pad = jnp.pad(v_win, pad)
    span = WINDOW + Q_BLOCK
    q_off = jnp.arange(Q_BLOCK)
    sel_off = jnp.arange(SEL_BLOCK)
    win_off = jnp.arange(span) - WINDOW

    def query_block(qi):
        s0 = qi * Q_BLOCK
        t = s0 + q_off
        qb = lax.dynamic_slice_in_dim(q, s0, Q_BLOCK, axis=1)
        gb = lax.dynamic_slice_in_dim(gates, s0, Q_BLOCK, axis=1)
        vis = cmp_end[None, :] <= t[:, None]
        sc = jnp.einsum('bqgrd,bgnd->bgrqn', qb, kc).astype(jnp.float32)
        p_cmp = jnp.where(vis, jax.nn.softmax(jnp.where(vis, sc, NEG_INF), axis=-1), 0.0)
        o_cmp = jnp.einsum('bgrqn,bgnd->bqgrd', p_cmp.astype(vc.dtype), vc)
        imp = jnp.einsum('bgrqn,nj->bgqj', p_cmp, overlap)
        cur = (t // SEL_BLOCK)[:, None]
        valid = blk_ids[None, :] <= cur
        forced = (blk_ids[None, :] == 0) | (blk_ids[None, :] == cur) | (blk_ids[None, :] == cur - 1)
        score = jnp.where(valid, jnp.where(forced, FORCED_SCORE, imp), -1.0)
        _, top = lax.top_k(score, n_top)
        flat = base + top
        s_list = []
        for s in range(n_top):
            kg = ks_flat[flat[..., s]]
            kpos = top[..., s, None] * SEL_BLOCK + sel_off
            sc_s = jnp.einsum('bqgrd,bgqkd->bgrqk', qb, kg).astype(jnp.float32)
            s_list.append(jnp.where((kpos <= t[:, None])[:, :, None], sc_s, NEG_INF))
        p_sel = jax.nn.softmax(jnp.concatenate(s_list, axis=-1), axis=-1).astype(vs_flat.dtype)
        o_sel = sum(jnp.einsum('bgrqk,bgqkd->bqgrd', p_sel[..., s * SEL_BLOCK:(s + 1) * SEL_BLOCK],
                               vs_flat[flat[..., s]]) for s in range(n_top))
        kw = lax.dynamic_slice_in_dim(kw_pad, s0, span, axis=1)
        vw = lax.dynamic_slice_in_dim(vw_pad, s0, span, axis=1)
        kpos_w = s0 + win_off
        rel = t[:, None] - kpos_w[None, :]
        ok = (rel >= 0) & (rel < WINDOW) & (kpos_w[None, :] >= 0)
        sc_w = jnp.einsum('bqgrd,bkgd->bgrqk', qb, kw).astype(jnp.float32)
        p_w = jax.nn.softmax(jnp.where(ok, sc_w, NEG_INF), axis=-1)
        o_win = jnp.einsum('bgrqk,bkgd->bqgrd', p_w.astype(vw.dtype), vw)
        return gb[..., 0:1] * o_cmp + gb[..., 1:2] * o_sel + gb[..., 2:3] * o_win

    out = lax.map(query_block, jnp.arange(s_ // Q_BLOCK))
    return out.transpose(1, 0, 2, 3, 4, 5).reshape(b_, s_, g_ * r_ * dh)

def hybrid_layer(x, pos, mix_norm_gain, w_in, gdn_conv_w, gdn_a_log, gdn_dt_bias, gdn_out_norm_gain,
                 cmp_pos_k, cmp_w1_k, cmp_w2_k, cmp_pos_v, cmp_w1_v, cmp_w2_v,
                 w_branch_gdn, w_branch_nsa, w_out, ffn_norm_gain, w_gate_up, w_down):
    f32 = jnp.float32
    b_, s_, _ = x.shape
    h = rms_norm(x, mix_norm_gain)
    proj = jnp.einsum('bsd,de->bse', h, w_in)
    split_at = np.cumsum(IN_SIZES)[:-1].tolist()
    (qkv_a, z_a, beta_a, alpha_a, q_b, kc_b, vc_b, ks_b, vs_b, kw_b, vw_b,
     gate_b, merge_a, merge_b) = jnp.split(proj, split_at, axis=-1)

    qkv_a = jax.nn.silu(causal_depthwise_conv(qkv_a, gdn_conv_w))
    q_a, k_a, v_a = [a.reshape(b_, s_, GDN_HEADS, GDN_HEAD_DIM).astype(f32) for a in jnp.split(qkv_a, 3, axis=-1)]
    q_a = l2_normalize(q_a) * (GDN_HEAD_DIM ** -0.5)
    k_a = l2_normalize(k_a)
    beta = jax.nn.sigmoid(beta_a.astype(f32))
    log_decay = -jnp.exp(gdn_a_log.astype(f32)) * jax.nn.softplus(alpha_a.astype(f32) + gdn_dt_bias.astype(f32))
    o_a = gated_delta_rule_chunked(q_a, k_a, v_a, beta, log_decay)
    o_a = (o_a * lax.rsqrt(jnp.mean(o_a * o_a, axis=-1, keepdims=True) + NORM_EPS)
           * gdn_out_norm_gain.astype(f32)
           * jax.nn.silu(z_a.astype(f32).reshape(b_, s_, GDN_HEADS, GDN_HEAD_DIM)))
    o_a = o_a.reshape(b_, s_, GDN_WIDTH).astype(x.dtype)

    q_n = partial_rope(q_b.reshape(b_, s_, NSA_KV_GROUPS, NSA_GROUP_HEADS, NSA_HEAD_DIM), pos) * (NSA_HEAD_DIM ** -0.5)
    kv_shape = (b_, s_, NSA_KV_GROUPS, NSA_HEAD_DIM)
    k_cmp = partial_rope(kc_b.reshape(kv_shape), pos)
    k_slc = partial_rope(ks_b.reshape(kv_shape), pos)
    k_win = partial_rope(kw_b.reshape(kv_shape), pos)
    gates = jax.nn.sigmoid(gate_b.reshape(b_, s_, NSA_KV_GROUPS, NSA_GROUP_HEADS, 3))
    o_b = native_sparse_attention(q_n, k_cmp, vc_b.reshape(kv_shape), k_slc, vs_b.reshape(kv_shape),
                                  k_win, vw_b.reshape(kv_shape), gates,
                                  cmp_pos_k, cmp_w1_k, cmp_w2_k, cmp_pos_v, cmp_w1_v, cmp_w2_v)

    merged = (jax.nn.sigmoid(merge_a) * jnp.einsum('bse,ed->bsd', o_a, w_branch_gdn)
              + jax.nn.sigmoid(merge_b) * jnp.einsum('bse,ed->bsd', o_b, w_branch_nsa))
    x = x + jnp.einsum('bsd,de->bse', merged, w_out)

    h2 = rms_norm(x, ffn_norm_gain)
    gate, up = jnp.split(jnp.einsum('bsd,df->bsf', h2, w_gate_up), 2, axis=-1)
    return x + jnp.einsum('bsf,fd->bsd', jax.nn.silu(gate) * up, w_down)

def first_inputs(seed: int = 0) -> dict:
    key = jax.random.key(seed)
    ks = jax.random.split(key, 24)
    f32 = jnp.float32
    L = DEPTH

    def nrm(k, shape, scale):
        return jax.random.normal(k, shape, f32) * scale

    def gain(k, shape):
        return 1.0 + 0.02 * jax.random.normal(k, shape, f32)

    dt = jnp.exp(jax.random.uniform(ks[5], (L, GDN_HEADS), f32, math.log(1e-3), math.log(1e-1)))
    return {
        'x': nrm(ks[0], (BATCH, SEQ, D_MODEL), 1.0),
        'mix_norm_gain': gain(ks[1], (L, D_MODEL)),
        'w_in': nrm(ks[2], (L, D_MODEL, IN_WIDTH), D_MODEL ** -0.5),
        'gdn_conv_w': nrm(ks[3], (L, GDN_CONV, 3 * GDN_WIDTH), GDN_CONV ** -0.5),
        'gdn_a_log': jnp.log(jax.random.uniform(ks[4], (L, GDN_HEADS), f32, 1.0, 16.0)),
        'gdn_dt_bias': dt + jnp.log(-jnp.expm1(-dt)),
        'gdn_out_norm_gain': gain(ks[6], (L, GDN_HEAD_DIM)),
        'cmp_pos_k': nrm(ks[7], (L, CMP_BLOCK, NSA_HEAD_DIM), 0.02),
        'cmp_w1_k': nrm(ks[8], (L, CMP_BLOCK, NSA_HEAD_DIM, CMP_HIDDEN), (CMP_BLOCK * NSA_HEAD_DIM) ** -0.5),
        'cmp_w2_k': nrm(ks[9], (L, CMP_HIDDEN, NSA_HEAD_DIM), CMP_HIDDEN ** -0.5),
        'cmp_pos_v': nrm(ks[10], (L, CMP_BLOCK, NSA_HEAD_DIM), 0.02),
        'cmp_w1_v': nrm(ks[11], (L, CMP_BLOCK, NSA_HEAD_DIM, CMP_HIDDEN), (CMP_BLOCK * NSA_HEAD_DIM) ** -0.5),
        'cmp_w2_v': nrm(ks[12], (L, CMP_HIDDEN, NSA_HEAD_DIM), CMP_HIDDEN ** -0.5),
        'w_branch_gdn': nrm(ks[13], (L, GDN_WIDTH, D_MODEL), GDN_WIDTH ** -0.5),
        'w_branch_nsa': nrm(ks[14], (L, NSA_WIDTH, D_MODEL), NSA_WIDTH ** -0.5),
        'w_out': nrm(ks[15], (L, D_MODEL, D_MODEL), D_MODEL ** -0.5),
        'ffn_norm_gain': gain(ks[16], (L, D_MODEL)),
        'w_gate_up': nrm(ks[17], (L, D_MODEL, 2 * FFN_HIDDEN), D_MODEL ** -0.5),
        'w_down': nrm(ks[18], (L, FFN_HIDDEN, D_MODEL), FFN_HIDDEN ** -0.5),
        'final_norm_gain': gain(ks[19], (D_MODEL,)),
    }

def first_block(x, mix_norm_gain, w_in, gdn_conv_w, gdn_a_log, gdn_dt_bias, gdn_out_norm_gain,
              cmp_pos_k, cmp_w1_k, cmp_w2_k, cmp_pos_v, cmp_w1_v, cmp_w2_v,
              w_branch_gdn, w_branch_nsa, w_out, ffn_norm_gain, w_gate_up, w_down, final_norm_gain):
    pos = jnp.arange(x.shape[1])
    for layer in range(DEPTH):
        x = hybrid_layer(x, pos, mix_norm_gain[layer], w_in[layer], gdn_conv_w[layer], gdn_a_log[layer],
                         gdn_dt_bias[layer], gdn_out_norm_gain[layer],
                         cmp_pos_k[layer], cmp_w1_k[layer], cmp_w2_k[layer],
                         cmp_pos_v[layer], cmp_w1_v[layer], cmp_w2_v[layer],
                         w_branch_gdn[layer], w_branch_nsa[layer], w_out[layer],
                         ffn_norm_gain[layer], w_gate_up[layer], w_down[layer])
    return rms_norm(x, final_norm_gain)


D_MIX = D_MODEL
HEAD_DIM = 64
D_HYENA = D_MIX // 2
D_FOURIER = D_MIX - D_HYENA
N_HYENA_HEADS = D_HYENA // HEAD_DIM
N_FOURIER_GROUPS = D_FOURIER // HEAD_DIM
N_MIX_HEADS = N_HYENA_HEADS + N_FOURIER_GROUPS
D_IN_PROJ = 3 * D_HYENA + D_FOURIER
SHORT_CONV = 3
FILTER_EMB = 33
FILTER_BANDS = (FILTER_EMB - 1) // 2
FILTER_ORDER = 64
N_INNER_MLPS = 2
DECAY_FAST_PCT = 0.3
DECAY_SLOW_PCT = 1.5
DECAY_TARGET = 1e-2
N_GROUPS = 4
EXPERTS_PER_GROUP = 8
N_EXPERTS = N_GROUPS * EXPERTS_PER_GROUP
TOP_K = 2
D_EXPERT = D_MODEL // 2
MOE_BLOCK = 128
EPS = 1e-6


def rmsnorm(x, g):
    xf = x.astype(jnp.float32)
    y = xf * lax.rsqrt(jnp.mean(xf * xf, axis=-1, keepdims=True) + EPS)
    return (y * g.astype(jnp.float32)).astype(x.dtype)

def short_conv_centred(u, w, b):
    L = u.shape[1]
    half = SHORT_CONV // 2
    up = jnp.pad(u, ((0, 0), (half, half), (0, 0)))
    y = b
    for k in range(SHORT_CONV):
        y = y + up[:, k:k + L] * w[k]
    return y

def hyena_filters(L, f_w_in, f_b_in, f_w_mid, f_b_mid, f_freq, f_w_out):
    t = jnp.linspace(0.0, 1.0, L, dtype=jnp.float32)[:, None]
    w = (2.0 * math.pi / L) * jnp.arange(L, dtype=jnp.float32)[:, None]
    f = jnp.linspace(1e-4, FILTER_BANDS - 1, FILTER_BANDS, dtype=jnp.float32)[None, :]
    z = jnp.concatenate([t, jnp.cos(f * w), -jnp.sin(f * w)], axis=-1)
    h = jnp.sin(f_freq[0] * (z @ f_w_in + f_b_in))
    for i in range(N_INNER_MLPS):
        h = jnp.sin(f_freq[i + 1] * (h @ f_w_mid[i] + f_b_mid[i]))
    h = (h @ f_w_out).astype(jnp.float32).reshape(L, 2, D_HYENA)
    max_decay = math.log(DECAY_TARGET) / DECAY_FAST_PCT
    min_decay = math.log(DECAY_TARGET) / DECAY_SLOW_PCT
    deltas = jnp.abs(jnp.linspace(min_decay, max_decay, D_HYENA, dtype=jnp.float32))
    decay = jnp.exp(-t * deltas)
    h = h * decay[:, None, :]
    return h[:, 0], h[:, 1]

def bidirectional_long_conv(u, h_fwd, h_bwd):
    L = u.shape[1]
    k = jnp.concatenate([h_fwd, jnp.zeros_like(h_fwd[:1]), h_bwd[:0:-1]], axis=0)
    k = k / jnp.sum(jnp.abs(k), axis=0, keepdims=True)
    k_f = jnp.fft.rfft(k, n=2 * L, axis=0)
    u_f = jnp.fft.rfft(u, n=2 * L, axis=1)
    return jnp.fft.irfft(u_f * k_f[None], n=2 * L, axis=1)[:, :L]

def hyena_mixer(u, conv_w, conv_b, f_w_in, f_b_in, f_w_mid, f_b_mid, f_freq, f_w_out, f_bias):
    uc = short_conv_centred(u, conv_w, conv_b).astype(jnp.float32)
    x0, x1, v = jnp.split(uc, 3, axis=-1)
    h_fwd, h_bwd = hyena_filters(u.shape[1], f_w_in, f_b_in, f_w_mid, f_b_mid, f_freq, f_w_out)
    z = x1 * v
    z = bidirectional_long_conv(z, h_fwd, h_bwd) + z * f_bias.astype(jnp.float32)
    return x0 * z

def fourier_mixer(u):
    B, L, _ = u.shape
    ug = u.astype(jnp.float32).reshape(B, L, N_FOURIER_GROUPS, HEAD_DIM)
    y = jnp.fft.fftn(ug, axes=(1, 3), norm='ortho').real
    return y.reshape(B, L, D_FOURIER)

def head_rmsnorm(y, g):
    B, L, _ = y.shape
    yh = y.reshape(B, L, N_MIX_HEADS, HEAD_DIM)
    yh = yh * lax.rsqrt(jnp.mean(yh * yh, axis=-1, keepdims=True) + EPS)
    return yh.reshape(B, L, D_MIX) * g.astype(jnp.float32)

def mixer_sublayer(x, norm_g, w_in, conv_w, conv_b, f_w_in, f_b_in, f_w_mid, f_b_mid, f_freq, f_w_out,
                   f_bias, mix_g, w_out):
    h = rmsnorm(x, norm_g)
    proj = h @ w_in
    y_hyena = hyena_mixer(proj[..., :3 * D_HYENA], conv_w, conv_b, f_w_in, f_b_in, f_w_mid, f_b_mid,
                          f_freq, f_w_out, f_bias)
    y_fourier = fourier_mixer(proj[..., 3 * D_HYENA:])
    y = head_rmsnorm(jnp.concatenate([y_hyena, y_fourier], axis=-1), mix_g).astype(x.dtype)
    return x + y @ w_out

def hierarchical_moe(h, w_group, b_group, w_router, b_router, w_gate, w_up, w_down):
    B, L, D = h.shape
    T = B * L
    tok = h.reshape(T, D)
    g_logits = (tok @ w_group).astype(jnp.float32) + b_group.astype(jnp.float32)
    g_sel = jnp.argmax(g_logits, axis=-1)
    p_group = jnp.take_along_axis(jax.nn.softmax(g_logits, axis=-1), g_sel[:, None], axis=-1)[:, 0]
    e_logits = jnp.einsum('td,gde->tge', tok, w_router).astype(jnp.float32) + b_router.astype(jnp.float32)
    e_logits = jnp.take_along_axis(e_logits, g_sel[:, None, None], axis=1)[:, 0]
    top_l, top_i = lax.top_k(e_logits, TOP_K)
    weight = p_group[:, None] * jax.nn.softmax(top_l, axis=-1)
    expert = (g_sel[:, None] * EXPERTS_PER_GROUP + top_i).astype(jnp.int32)

    P = T * TOP_K
    flat_e = expert.reshape(P)
    flat_t = jnp.repeat(jnp.arange(T, dtype=jnp.int32), TOP_K)
    flat_w = weight.reshape(P)
    order = jnp.argsort(flat_e)
    se = flat_e[order]
    counts = jnp.bincount(flat_e, length=N_EXPERTS).astype(jnp.int32)
    starts = jnp.cumsum(counts) - counts
    padded = ((counts + MOE_BLOCK - 1) // MOE_BLOCK) * MOE_BLOCK
    pad_ends = jnp.cumsum(padded)
    pad_starts = pad_ends - padded
    dest = pad_starts[se] + (jnp.arange(P, dtype=jnp.int32) - starts[se])
    n_blocks = -(-P // MOE_BLOCK) + N_EXPERTS
    n_rows = n_blocks * MOE_BLOCK
    row_tok = jnp.zeros((n_rows,), jnp.int32).at[dest].set(flat_t[order])
    row_w = jnp.zeros((n_rows,), jnp.float32).at[dest].set(flat_w[order])
    block_start = jnp.arange(n_blocks, dtype=jnp.int32) * MOE_BLOCK
    block_e = jnp.minimum(jnp.searchsorted(pad_ends, block_start, side='right'), N_EXPERTS - 1)

    def expert_block(args):
        e, rows_tok, rows_w = args
        xb = tok[rows_tok]
        a = xb @ w_gate[e]
        u = xb @ w_up[e]
        y = (jax.nn.silu(a) * u) @ w_down[e]
        return (y * rows_w[:, None].astype(y.dtype)).astype(tok.dtype)

    ys = lax.map(expert_block, (block_e, row_tok.reshape(n_blocks, MOE_BLOCK), row_w.reshape(n_blocks, MOE_BLOCK)))
    out = jnp.zeros((T, D), tok.dtype).at[row_tok].add(ys.reshape(n_rows, D))
    return out.reshape(B, L, D)

def second_inputs(seed: int = 0) -> dict:
    key = jax.random.key(seed)
    ks = jax.random.split(key, 24)
    f32 = jnp.float32
    n = lambda k, shape, s: (jax.random.normal(k, shape, f32) * s)
    return {
        'x': n(ks[0], (BATCH, SEQ, D_MODEL), 1.0),
        'norm1_g': 1.0 + n(ks[1], (DEPTH, D_MODEL), 0.02),
        'w_in': n(ks[2], (DEPTH, D_MODEL, D_IN_PROJ), D_MODEL ** -0.5),
        'conv_w': n(ks[3], (DEPTH, SHORT_CONV, 3 * D_HYENA), SHORT_CONV ** -0.5),
        'conv_b': n(ks[4], (DEPTH, 3 * D_HYENA), 0.02),
        'f_w_in': n(ks[5], (DEPTH, FILTER_EMB, FILTER_ORDER), FILTER_EMB ** -0.5),
        'f_b_in': n(ks[6], (DEPTH, FILTER_ORDER), 0.1),
        'f_w_mid': n(ks[7], (DEPTH, N_INNER_MLPS, FILTER_ORDER, FILTER_ORDER), FILTER_ORDER ** -0.5),
        'f_b_mid': n(ks[8], (DEPTH, N_INNER_MLPS, FILTER_ORDER), 0.1),
        'f_freq': 1.0 + n(ks[9], (DEPTH, N_INNER_MLPS + 1, FILTER_ORDER), 0.1),
        'f_w_out': n(ks[10], (DEPTH, FILTER_ORDER, 2 * D_HYENA), FILTER_ORDER ** -0.5),
        'f_bias': n(ks[11], (DEPTH, D_HYENA), 1.0),
        'mix_g': 1.0 + n(ks[12], (DEPTH, D_MIX), 0.02),
        'w_out': n(ks[13], (DEPTH, D_MIX, D_MODEL), D_MIX ** -0.5),
        'norm2_g': 1.0 + n(ks[14], (DEPTH, D_MODEL), 0.02),
        'w_group': n(ks[15], (DEPTH, D_MODEL, N_GROUPS), D_MODEL ** -0.5),
        'b_group': n(ks[16], (DEPTH, N_GROUPS), 0.01),
        'w_router': n(ks[17], (DEPTH, N_GROUPS, D_MODEL, EXPERTS_PER_GROUP), D_MODEL ** -0.5),
        'b_router': n(ks[18], (DEPTH, N_GROUPS, EXPERTS_PER_GROUP), 0.01),
        'w_gate': n(ks[19], (DEPTH, N_EXPERTS, D_MODEL, D_EXPERT), D_MODEL ** -0.5),
        'w_up': n(ks[20], (DEPTH, N_EXPERTS, D_MODEL, D_EXPERT), D_MODEL ** -0.5),
        'w_down': n(ks[21], (DEPTH, N_EXPERTS, D_EXPERT, D_MODEL), D_EXPERT ** -0.5),
        'final_g': 1.0 + n(ks[22], (D_MODEL,), 0.02),
    }

def second_block(x, norm1_g, w_in, conv_w, conv_b, f_w_in, f_b_in, f_w_mid, f_b_mid, f_freq, f_w_out, f_bias,
              mix_g, w_out, norm2_g, w_group, b_group, w_router, b_router, w_gate, w_up, w_down, final_g):
    for i in range(DEPTH):
        x = mixer_sublayer(x, norm1_g[i], w_in[i], conv_w[i], conv_b[i], f_w_in[i], f_b_in[i], f_w_mid[i],
                           f_b_mid[i], f_freq[i], f_w_out[i], f_bias[i], mix_g[i], w_out[i])
        x = x + hierarchical_moe(rmsnorm(x, norm2_g[i]), w_group[i], b_group[i], w_router[i], b_router[i],
                                 w_gate[i], w_up[i], w_down[i])
    return rmsnorm(x, final_g)


def setup_inputs(seed=0):
    out = dict(first_inputs(seed))
    for name, value in second_inputs(seed + 1).items():
        if name != "x":
            out[name + "_2"] = value
    return out


def reference(
    x, mix_norm_gain, w_in, gdn_conv_w, gdn_a_log, gdn_dt_bias, gdn_out_norm_gain, cmp_pos_k,
    cmp_w1_k, cmp_w2_k, cmp_pos_v, cmp_w1_v, cmp_w2_v, w_branch_gdn, w_branch_nsa, w_out,
    ffn_norm_gain, w_gate_up, w_down, final_norm_gain, norm1_g_2, w_in_2, conv_w_2, conv_b_2,
    f_w_in_2, f_b_in_2, f_w_mid_2, f_b_mid_2, f_freq_2, f_w_out_2, f_bias_2, mix_g_2, w_out_2,
    norm2_g_2, w_group_2, b_group_2, w_router_2, b_router_2, w_gate_2, w_up_2, w_down_2,
    final_g_2,
):
    x = first_block(
        x, mix_norm_gain, w_in, gdn_conv_w, gdn_a_log, gdn_dt_bias, gdn_out_norm_gain,
        cmp_pos_k, cmp_w1_k, cmp_w2_k, cmp_pos_v, cmp_w1_v, cmp_w2_v, w_branch_gdn,
        w_branch_nsa, w_out, ffn_norm_gain, w_gate_up, w_down, final_norm_gain,
    )
    return second_block(
        x, norm1_g_2, w_in_2, conv_w_2, conv_b_2, f_w_in_2, f_b_in_2, f_w_mid_2, f_b_mid_2,
        f_freq_2, f_w_out_2, f_bias_2, mix_g_2, w_out_2, norm2_g_2, w_group_2, b_group_2,
        w_router_2, b_router_2, w_gate_2, w_up_2, w_down_2, final_g_2,
    )


_drawn_inputs = setup_inputs


def setup_inputs(seed=0):
    import zlib

    import numpy as np

    out = dict(_drawn_inputs(seed))
    spreads = {}
    factors = {'cmp_pos_k': 8.0,
     'cmp_pos_v': 5.399,
     'f_b_in_2': 2.828,
     'f_freq_2': 3.152,
     'norm2_g_2': 3.166,
     'b_group_2': 5.32,
     'b_router_2': 6.145,
     'final_g_2': 2.954}
    for name, (base, spread) in spreads.items():
        noise = np.random.default_rng([zlib.crc32(name.encode()), seed]).standard_normal(out[name].shape)
        drawn = base * np.exp(spread * noise) if base else spread * noise
        out[name] = jnp.asarray(drawn.astype(out[name].dtype))
    for name, factor in factors.items():
        out[name] = (out[name] * factor).astype(out[name].dtype)
    return out
```

```python
from contextlib import ExitStack

import concourse.bass as bass
from concourse import mybir

F32 = mybir.dt.float32
I32 = mybir.dt.int32
ALU = mybir.AluOpType
ACT = mybir.ActivationFunctionType
AX_X = mybir.AxisListType.X

P = 128
T = 256
NB = T // P
D = 1024
KT = D // P
H_GDN, DH_GDN = 4, 128
CHUNK = 64
N_CHUNK = T // CHUNK
QKV = 3 * H_GDN * DH_GDN
CT = QKV // P
TAPS = 4
NSA_H, NSA_G, NSA_D = 8, 2, 64
NSA_R = NSA_H // NSA_G
ROPE_HALF = NSA_D // 8
N_HEADS64 = NSA_H + 6 * NSA_G
CMP_BLOCK, CMP_STRIDE = 32, 16
N_CMP = (T - CMP_BLOCK) // CMP_STRIDE + 1
CMP_A = CMP_BLOCK // 2
FFN = 2816
FC = 256
N_FC = FFN // FC
DH2 = 512
NHT = DH2 // P
N_EXP, N_GRP, EPG = 32, 4, 8
DE = 512
CAP = 32
MAX_ITEMS = 2 * T // CAP + N_EXP
EPS = 1e-6
NEG = -1e30
SLOTS = 6
BANK = 512
TWO_PI = 6.283185307179586
ROUND_MAGIC = 12582912.0
TWO_PI_HI, TWO_PI_MID = 6.28125, 0.0019350051879882812
TWO_PI_LO = TWO_PI - TWO_PI_HI - TWO_PI_MID

(IDENT, CUM, SAME, STRICT, LEVEL0) = range(5)
N_LEVEL = 6
ONES = LEVEL0 + N_LEVEL
DFT_C, DFT_S, CAUSAL, RANK = range(ONES + 1, ONES + 5)
N_SQ = RANK + 1
C_MIX, C_FFN, C_N1, C_N2, C_MIXG = 0, 8, 16, 24, 32
C_CONV = 40
C_CONV2 = C_CONV + TAPS * CT
C_CONVB2 = C_CONV2 + 3 * CT
C_FBIAS = C_CONVB2 + CT
C_FB = C_FBIAS + NHT
C_FREQ = C_FB + 3
C_POS = C_FREQ + 3
C_ONE = C_POS + 2 * CMP_A
C_BLK = C_ONE + 2
C_FOLD = C_BLK + NSA_H
N_COLS = C_FOLD + CAP
R_ALOG, R_DT, R_ONORM = 0, 4, 8
R_FIN1 = R_ONORM + DH_GDN
R_FIN2 = R_FIN1 + D
R_BIAS = R_FIN2 + D
R_IOTA = R_BIAS + N_GRP + N_EXP
R_BIG = R_IOTA + 64
N_ROWS = R_BIG + N_EXP


SHARED = {
    "delta_vector": [("conv_ready", 1), ("y_ready", 1), ("g_spread", 2), ("gc_out", 2), ("roped", 1),
        ("beta_used", 1), ("sums_out", 1), ("kb_ready", 1), ("a_ready", 1), ("qk_ready", 1), ("kd_ready", 1)],
    "delta_scalar": [("softplus_ready", 1), ("qk_squared", 1), ("exp_gc_ready", 1), ("decays_ready", 1),
        ("norms_ready", 1)],
    "delta_tensor": [("gc_ready", 1), ("qk_summed", 1), ("kk_ready", 1), ("kv_turned", 2)],
    "rows_normed": [("x_normed", 2), ("x2_normed", 2), ("x3_normed", 2), ("x4_normed", 2)],
    "rows_turned": [("x_turned", 4), ("merge_turned", 4), ("x2_turned", 4), ("x3_turned", 4), ("x4_turned", 4)],
    "rows_ready": [("h_ready", 4), ("h2_ready", 4), ("h3_ready", 4), ("h4_ready", 4)],
    "attn_tensor": [("nq_turned", 2), ("nk_turned", 1), ("pairs_made", 1), ("hid_made", 2), ("kv_cmp_made", 1)],
    "attn_scalar": [("nq_ready", 2), ("nk_ready", 1), ("hid_ready", 2)],
    "attn_vector": [("pairs_ready", 1), ("hid_zeroed", 1), ("hid_rep_ready", 1), ("kv_cmp_ready", 1)],
    "filter_tensor": [("filt_layer", 3), ("filt_out_made", 1), ("kernF_made", 1), ("filter_turned", 1)],
    "filter_scalar": [("filt_sin", 3), ("kern_abs_ready", 1), ("kernF_ready", 1)],
    "filter_vector": [("arg_ready", 3), ("kern_ready", 1), ("filt_norm_ready", 1)],
    "mix_tensor": [("four_projected", 2), ("four1_made", 4), ("z_turned", 2), ("four2_made", 1), ("zF_made", 4),
        ("conv_made", 1), ("y_summed", 1), ("out2_made", 1)],
    "mix_scalar": [("four_ready", 2), ("four1_ready", 4), ("z_tok_ready", 2), ("y_fo_ready", 1), ("zF_ready", 4),
        ("y_squared", 2), ("y_root", 1)],
    "mix_vector": [("z_ready", 1), ("prod_ready", 1), ("y_hy_ready", 1), ("y_mean", 1), ("y_ready2", 2)],
    "route_tensor": [("logits_made", 1), ("ranks_made", 1)],
    "route_vector": [("zero_ready", 1), ("chosen_ready", 1), ("ex_ready", 1), ("table_ready", 1)],
}
PLACE = {stage: (name, sum(n for _, n in stages[:i])) for name, stages in SHARED.items() for i, (stage, _) in enumerate(stages)}


def since(stage, n):
    return PLACE.get(stage, (stage, 0))[1] + n


class Signals:

    def __init__(self, nc, ctx):
        self.nc, self.ctx, self.known = nc, ctx, {}

    def __call__(self, name):
        name = PLACE.get(name, (name, 0))[0]
        if name not in self.known:
            self.known[name] = self.ctx.enter_context(self.nc.semaphore(name))
        return self.known[name]


def spread(ap, axis, n):
    ap = ap.unsqueeze(axis)
    shape = list(ap.shape)
    shape[axis] = n
    return ap.broadcast_to(shape)


def two_layer_program(nc, dram, dump=None):
    with ExitStack() as ctx:
        sig = Signals(nc, ctx)

        def sb(name, *shape, dt=F32):
            return ctx.enter_context(nc.sbuf_tensor("sb_" + name, [P, *shape], dt))[:]

        ps = ctx.enter_context(nc.psum_tensor("ps", [P, 8, BANK], F32))[:]

        ring = sb("ring", SLOTS, 4096)
        squares = sb("squares", N_SQ, P)
        cols = sb("cols", N_COLS)
        rows = sb("rows", N_ROWS)
        x = sb("x", NB, D)
        hT = sb("hT", KT, T)
        stat = sb("stat", 16)
        own = sb("own", 6, 1024)
        raw = sb("raw", CT, T + TAPS - 1)
        silu_z = sb("silu_z", NB, 512)
        nsa = sb("nsa", NB, N_HEADS64, NSA_D)
        merge = sb("merge", NB, 2, D)
        ctl = sb("ctl", NB, 32)
        small = sb("small", 512)

        ring_units = ring[:, 4:6, :].rearrange("p s (u n) -> p (s u) n", n=1024)
        unit = [ring_units[:, u, :] for u in range(8)] + [own[:, u, :] for u in range(6)]
        raw_flat = raw.rearrange("p c t -> p (c t)")

        per_head = lambda u: u.rearrange("p (b h n) -> p b h n", b=NB, h=H_GDN)
        convT = ring_units[:, 0:3, :].rearrange("p u (c t) -> p (u c) t", t=T)
        qkT_sq = raw.rearrange("p c t -> p (c t)")[:, 0:2048].rearrange("p (c t) -> p c t", t=T)
        qT = ring_units[:, 0, :].rearrange("p (h b t) -> p b h t", h=H_GDN, b=NB)
        kT = ring_units[:, 1, :].rearrange("p (h b t) -> p b h t", h=H_GDN, b=NB)
        vT = ring_units[:, 2, :].rearrange("p (h b t) -> p b h t", h=H_GDN, b=NB)
        kbT, qgT = per_head(unit[3]), per_head(unit[4])
        g_lhs, beta_lhs = per_head(unit[5]), per_head(unit[6])
        decay_strict, qk_decay = per_head(unit[5]), per_head(unit[6])
        decayT, exp_gc = per_head(unit[7]), per_head(unit[8])
        aT, inv, invT, off, mid = (per_head(unit[u]) for u in (9, 10, 11, 12, 13))
        kbg, kd, vb = (per_head(raw_flat[:, u * 1024:(u + 1) * 1024]) for u in range(3))
        uu, wT, vnew = per_head(unit[12]), per_head(unit[13]), per_head(unit[9])
        state = unit[2].rearrange("p (s h n) -> p s h n", s=2, h=H_GDN)
        o_gdn, o_sq = per_head(unit[10]), per_head(unit[11])
        oaT = own[:, 2, :].rearrange("p (h t) -> p h t", t=T)
        piece = lambda n, w: small[:, n:n + w].rearrange("p (b h) -> p b h", b=NB)
        sp_y, sp_m, g_tok, gc, gl = (piece(8 * n, 8) for n in range(5))
        e_last, beta_g, o_ss = (piece(8 * n, 8) for n in range(5, 8))

        pair = lambda bank: ps[:, bank:bank + 2, :].rearrange("p b (h n) -> p b h n", h=H_GDN)
        sq = lambda n: squares[:, n, :]
        ident = sq(IDENT)

        rope = sb("rope", 2, NB, N_HEADS64, ROPE_HALF)
        vis = sb("vis", 2, NB, CMP_STRIDE)
        cmp_w2 = sb("cmp_w2", 2, NSA_D)
        soft = sb("soft", 96)
        nqT = own[:, 0, :].rearrange("p (r t) -> p r t", t=T)
        nkT = own[:, 1, 0:512].rearrange("p (s t) -> p s t", t=T)
        probs = [ring_units[:, 2 * n:2 * n + 2, :].rearrange("p u n -> p (u n)") for n in range(2)]
        probsT_all = ring_units[:, 4:6, :].rearrange("p u (h n) -> p (u h) n", n=P)
        pairs = own[:, 4, 0:960].rearrange("p (s a g n) -> p s a g n", s=2, a=CMP_A, g=NSA_G)
        hid = own[:, 5, 0:64].rearrange("p (s g n) -> p s g n", s=2, g=NSA_G)
        hid_rep = own[:, 5, 64:192].rearrange("p (g r n) -> p g r n", g=NSA_G, r=NSA_R)
        kcT = own[:, 5, 192:208]
        v_cmp = own[:, 5, 256:768].rearrange("p (h d) -> p h d", d=NSA_D)
        p_cmp = own[:, 5, 768:896].rearrange("p (h n) -> p h n", n=CMP_STRIDE)
        p_cmpT = own[:, 5, 896:1024]
        o_nsa = silu_z
        o_part = own[:, 1, 512:1024]
        obT = own[:, 3, :].rearrange("p (h t) -> p h t", t=T)
        JOBS = [(0, 0), (0, 1), (1, 0), (1, 1)]

        gated = nsa.rearrange("p b h d -> p (b h d)")[:, 0:1024].rearrange("p (i b n) -> p i b n", i=2, b=NB)
        gatedT = ctx.enter_context(nc.sbuf_tensor("sb_gatedT", [P, 2, NB, FC // P, P], F32))[:]

        class Step:

            def __init__(self, n=None, i=None, parity=None):
                self.n = n if i is None else 2 * i + parity + 1
                self.par = n % 2 if i is None else (parity + 1) % 2
                self.turns = n // 2 + 1 if i is None else i + 1 + (1 if self.par == 0 else 0)

        dft = [own[:, u, :].rearrange("p (b n) -> p b n", b=NB) for u in (0, 1, 3)]
        dft_fwd, dft_bwd, dft_time = dft
        dft_inv = own[:, 2, :].rearrange("p (f t) -> p f t", t=T)
        decay2 = own[:, 4, :].rearrange("p (b n) -> p b n", b=NB)
        filt_out = own[0:64, 5, :]
        kernF = own[:, 4:6, :].rearrange("p u (f n) -> p (u f) n", n=DH2)
        nsa_flat = nsa.rearrange("p b h d -> p (b h d)")
        emb, filt_in, filt_mid = nsa_flat[0:33, 1024:1280], nsa_flat[0:33, 1280:1344], nsa_flat[0:64, 1344:1472]
        w_route = sb("w_route", KT, N_GRP + N_EXP)
        kern = ring_units[:, 0:2, :].rearrange("p u (d n) -> p u d n", d=2)
        kern_abs = ring_units[:, 2:4, :].rearrange("p u (d n) -> p u d n", d=2)
        arg, turns_, act_a = (ring_units[0:64, 4, n * T:(n + 1) * T] for n in range(3))
        filt_norm = small[:, 72:76]
        u2 = raw_flat[:, 0:CT * (T + 2)].rearrange("p (c t) -> p c t", t=T + 2)
        merge_flat = merge.rearrange("p b i n -> p (b i n)")
        m_unit = [merge_flat[:, n * 1024:(n + 1) * 1024] for n in range(4)]
        conv2 = merge_flat[:, 0:CT * T].rearrange("p (c t) -> p c t", t=T)
        zT = m_unit[1].rearrange("p (c t) -> p c t", t=T)
        z_tok = m_unit[3].rearrange("p (b n) -> p b n", b=NB)
        u_four = silu_z
        four1 = nsa_flat[:, 0:2048].rearrange("p (c n) -> p c n", n=2 * T)
        zF = raw_flat[:, 0:2048].rearrange("p (f n) -> p f n", n=DH2)
        prodF = hT.rearrange("p k t -> p (k t)").rearrange("p (f n) -> p f n", n=DH2)
        cross = gatedT.rearrange("p i b f n -> p (i b f n)").rearrange("p (f n) -> p f n", n=DH2)
        y_hy = own[:, 1, :].rearrange("p (c t) -> p c t", t=T)
        y_fo = raw_flat[:, 2048:3072].rearrange("p (c t) -> p c t", t=T)
        y_sq = [m_unit[2], m_unit[3]]
        y_rs = merge_flat[:, 2048:4096]

        route = lambda n, w: raw_flat[:, n:n + w].rearrange("p (b e) -> p b e", b=NB)
        logits = route(0, 72)
        l_grp, l_exp = logits[:, :, 0:N_GRP], logits[:, :, N_GRP:]
        eq4, one_grp, eq, one1, one2, chosen = route(72, 8), route(80, 8), route(88, 64), route(152, 64), route(216, 64), route(280, 64)
        best = route(344, 2)
        ex = route(352, 10)
        shift, slot_of = route(368, 64), route(432, 64)
        vec = lambda n, w: raw_flat[:, n:n + w]
        over_ends = [vec(500, N_EXP), vec(532, N_EXP)]
        more, counts, base = vec(564, N_EXP), vec(596, N_EXP), vec(628, N_EXP)
        steps = vec(660, 7 * N_EXP).rearrange("p (e m) -> p e m", m=7)
        table_cmp = vec(900, 16 * N_EXP).rearrange("p (i e) -> p i e", e=N_EXP)
        table = vec(1420, 17)
        first, second = vec(1440, NB).rearrange("p (b e) -> p b e", e=1), vec(1442, NB).rearrange("p (b e) -> p b e", e=1)
        slots_of = vec(1444, 2 * NB)
        weights = vec(1448, 2 * NB)
        table_i = sb("table_i", 17, dt=I32)
        xn = merge[:, :, 0, :]
        part_gu = [own[:, n, :] for n in range(2)]
        part_d = own[:, 2, :]
        hgT = [own[:, 3, n * 256:(n + 1) * 256].rearrange("p (k c) -> p k c", c=CAP) for n in range(2)]
        pick = [own[:, 3, 512 + 64 * n:576 + 64 * n].rearrange("p (b c) -> p b c", b=NB) for n in range(2)]
        pick_tmp = [own[:, 3, 640 + 32 * n:672 + 32 * n] for n in range(3 * NB)]
        zero = own[:, 3, 832:960]
        pick4 = [own[:, 4, 256 * n:256 * (n + 1)].rearrange("p (b j c) -> p b j c", b=NB, j=4) for n in range(2)]
        pickT = own[:, 4, 512:768].rearrange("p (b t) -> p b t", b=NB)
        silu_g = own[:, 4, 768:896]
        actT = own[:, 4, 896:1024].rearrange("p (f c) -> p f c", c=CAP)
        ITEM_SLOTS = ((3, 4, 5), (0, 1, 2))

        def item_steps(pe):

            def gather(par):
                for k in range(KT):
                    for b in range(NB):
                        m = pe.matmul(ps[:, 0, k * CAP:(k + 1) * CAP], xn[:, b, k * P:(k + 1) * P], pick[par][:, b, :],
                                      start=(b == 0), stop=(b == NB - 1))
                return m

            def gate_up(par, slots):
                for n in range(2):
                    w = ring[:, slots[n], :].rearrange("p (k n) -> p k n", n=DE)
                    for kk in range(2):
                        for j in range(4):
                            k = 2 * j + kk
                            m = pe.matmul(ps[CAP * j:CAP * (j + 1), 1 + n, :], hgT[par][:, k, :], w[:, k, :],
                                          start=(kk == 0), stop=(kk == 1))
                return m

            def add_turn(par):
                fold = cols[:, C_FOLD:C_FOLD + CAP]
                for n in range(2):
                    for f in range(4):
                        at = n * P + f * CAP
                        pe.matmul(ps[:, 3, at:at + CAP], part_gu[par][:, n * DE + f * P:n * DE + (f + 1) * P], fold, start=True, stop=True)
                for b in range(NB):
                    m = pe.transpose(ps[:, 3, 256 + b * P:256 + (b + 1) * P], pick4[par][:, b].rearrange("p j c -> p (j c)"), ident)
                return m

            def down(slot):
                w = ring[:, slot, :].rearrange("p (f n) -> p f n", n=D)
                for half in range(2):
                    for j in range(4):
                        m = pe.matmul(ps[CAP * j:CAP * (j + 1), 1 + half, :], actT[:, j, :], w[:, j, half * BANK:(half + 1) * BANK],
                                      start=True, stop=True)
                return m

            def scatter(start, stop):
                for b in range(NB):
                    for half in range(2):
                        m = pe.matmul(ps[:, 4 + 2 * b + half, :], pickT[:, b, :], part_d[:, half * BANK:(half + 1) * BANK],
                                      start=start, stop=stop, skip_group_check=True)
                return m
            return gather, gate_up, add_turn, down, scatter

        def item_picks(dve, link, par):
            iota = rows[:, R_IOTA:R_IOTA + CAP]
            for b in range(NB):
                hit, hit_w, other_w = pick_tmp[3 * b:3 * b + 3]
                dve.tensor_scalar(hit, iota, slots_of[:, b:b + 1], None, ALU.is_equal)
                link(dve.tensor_scalar(hit_w, iota, slots_of[:, b:b + 1], weights[:, b:b + 1], ALU.is_equal, ALU.mult))
                at = NB + b
                dve.scalar_tensor_tensor(pick[par][:, b, :], iota, slots_of[:, at:at + 1], hit, ALU.is_equal, ALU.add)
                link(dve.tensor_scalar(other_w, iota, slots_of[:, at:at + 1], weights[:, at:at + 1], ALU.is_equal, ALU.mult))
                link(dve.tensor_tensor(hit_w, hit_w, other_w, ALU.add))
                dve.tensor_copy(pick4[par][:, b], spread(hit_w, 1, 4))
            return dve.tensor_scalar(slots_of, slots_of, -float(CAP), None, ALU.add)

        block = ctx.enter_context(nc.Block())
        IN2_SLOTS, OUT2_SLOTS = (3, 4, 5, 1), (0, 2)

        def chain(eng, name):
            count = [0]

            def link(ins):
                count[0] += 1
                ins.then_inc(sig(name), 1)
                eng.wait_ge(sig(name), count[0])
            return link

        stream = [("w_in", n) for n in range(11)] + [("cmp", 0), ("branch", 0), ("branch", 1), ("w_out", 0), ("w_out", 1)]
        where = {what: (n % 4, n // 4 + 1) for n, what in enumerate(stream)}

        def arrived(eng, what):
            slot, use = where[what]
            eng.wait_ge(sig(f"slot{slot}_loaded"), 16 * use)
            return ring[:, slot, :]

        @block.sync
        def _(sp):
            sp.dma_start(x, dram["x"]).then_inc(sig("x_loaded"), 16)
            sp.dma_start(squares, dram["squares"]).then_inc(sig("const_loaded"), 16)
            sp.dma_start(cols, dram["cols"]).then_inc(sig("const_loaded"), 16)
            for n, what in enumerate(stream):
                slot, use = where[what]
                if n >= 4:
                    sp.wait_ge(sig("slot_free"), n - 3)
                dst = ring[:, slot, :]
                kind, i = what
                if kind == "w_in" and i == 6:
                    dst = dst.rearrange("p (k n) -> p k n", n=BANK)[:, :, 0:288]
                    src = dram["w_in"][i][:, :, 0:288]
                elif kind == "w_in":
                    src = dram["w_in"][i].rearrange("p k n -> p (k n)")
                elif kind == "cmp":
                    src = dram["cmp_w1"].rearrange("p v a n -> p (v a n)")
                elif kind == "branch":
                    src = dram["w_branch"][i].rearrange("p k n -> p (k n)")
                else:
                    src = dram["w_out"][i].rearrange("p k n -> p (k n)")
                sp.dma_start(dst, src).then_inc(sig(f"slot{slot}_loaded"), 16)
                if n == 1:
                    sp.dma_start(rows, dram["rows"]).then_inc(sig("rows_loaded"), 16)
                    sp.dma_start(rope, dram["rope"]).then_inc(sig("nsa_const_loaded"), 16)
                    sp.dma_start(vis, dram["vis"]).then_inc(sig("nsa_const_loaded"), 16)
                    sp.dma_start(cmp_w2, dram["cmp_w2"]).then_inc(sig("nsa_const_loaded"), 16)
            sp.wait_ge(sig("slot_free"), 13)

            def load_gate_up(s):
                sp.dma_start(ring[:, s.par, :], dram["w_gu"][s.n].rearrange("p k h n -> p (k h n)"))\
                  .then_inc(sig(f"gu{s.par}_loaded"), 16)

            def load_down(s):
                sp.dma_start(ring[:, 2, s.par * 2048:(s.par + 1) * 2048], dram["w_dn"][s.n].rearrange("p f n -> p (f n)"))\
                  .then_inc(sig(f"dn{s.par}_loaded"), 16)

            load_gate_up(Step(0))
            sp.wait_ge(sig("slot_free"), 14)
            sp.wait_ge(sig("branch_made"), 2)
            for name, dst in (("dft_fwd", own[:, 0, :]), ("dft_bwd", own[:, 1, :]), ("dft_inv", own[:, 2, :]),
                              ("dft_time", own[:, 3, :]), ("decay", own[:, 4, :])):
                sp.dma_start(dst, dram[name].rearrange("p a n -> p (a n)")).then_inc(sig("mix_const_loaded"), 16)
            sp.dma_start(filt_out, dram["filt_out"]).then_inc(sig("mix_const_loaded"), 16)
            sp.dma_start(emb, dram["emb"]).then_inc(sig("mix_const_loaded"), 16)
            sp.dma_start(filt_in, dram["filt_in"]).then_inc(sig("mix_const_loaded"), 16)
            sp.dma_start(filt_mid, dram["filt_mid"].rearrange("p a n -> p (a n)")).then_inc(sig("mix_const_loaded"), 16)
            sp.dma_start(w_route, dram["w_route"]).then_inc(sig("mix_const_loaded"), 16)
            load_gate_up(Step(1))
            sp.wait_ge(sig("slot_free"), 15)
            load_down(Step(0))
            load_down(Step(1))
            with sp.Fori(0, (N_FC - 3) // 2) as i:
                for parity in range(2):
                    s = Step(i=i, parity=parity)
                    nxt = Step(i=i, parity=parity)
                    nxt.n, nxt.par = 2 * i + parity + 2, parity
                    sp.wait_ge(sig("gu_free"), 2 * i + parity + 1)
                    load_gate_up(nxt)
                    sp.wait_ge(sig("dn_free"), 2 * i + parity + 1)
                    load_down(nxt)
            s = Step(N_FC - 1)
            sp.wait_ge(sig("gu_free"), N_FC - 2)
            load_gate_up(s)
            sp.wait_ge(sig("dn_free"), N_FC - 2)
            load_down(s)
            sp.wait_ge(sig("slot_free"), 16)
            sp.wait_ge(sig("filter_turned"), since("filter_turned", 1))
            for c, slot in enumerate(IN2_SLOTS):
                if c == 3:
                    sp.wait_ge(sig("gu_free"), N_FC - 1)
                sp.dma_start(ring[:, slot, :], dram["w_in2"][c].rearrange("p k n -> p (k n)")).then_inc(sig(f"slot{slot}_loaded"), 16)
            for half, slot in enumerate(OUT2_SLOTS):
                sp.wait_ge(sig("gu_free" if half == 0 else "dn_free"), N_FC)
                sp.dma_start(ring[:, slot, :], dram["w_out2"][half].rearrange("p k n -> p (k n)")).then_inc(sig(f"slot{slot}_loaded"), 16)
            def load_item(par, expert, done=None):
                for n, slot in enumerate(ITEM_SLOTS[par]):
                    if done is not None and n == 0:
                        sp.wait_ge(sig("item_gu_made"), done)
                    if done is not None and n == 2:
                        sp.wait_ge(sig("item_down_made"), done)
                    src = dram["w_exp"][expert].rearrange("p i n -> p (i n)")[:, n * 4096:(n + 1) * 4096] if isinstance(expert, int) \
                        else dram["w_exp"][bass.ds(expert, 1)].rearrange("e p i n -> p (e i n)")[:, n * 4096:(n + 1) * 4096]
                    sp.dma_start(ring[:, slot, :], src).then_inc(sig(f"item{par}_{n}_loaded"), 16)

            sp.wait_ge(sig("u2_projected"), 6)
            load_item(0, 0)
            sp.wait_ge(sig("out2_made"), since("out2_made", 1))
            load_item(1, 1)
            with sp.Fori(0, N_EXP // 2 - 1) as i:
                for par in range(2):
                    load_item(par, 2 * i + par + 2, 2 * i + par + 1)
            sp.wait_ge(sig("table_ready"), since("table_ready", 1))
            sp.wait_ge(sig("item_down_made"), N_EXP)
            n_over = sp.value_load(table_i[0:1, 16:17], min_val=0, max_val=16)
            with sp.If(n_over > 0):
                with sp.Fori(0, n_over) as i:
                    sp.wait_ge(sig("over_next"), i + 1)
                    expert = sp.value_load(table_i[0:1, bass.ds(i, 1)], min_val=0, max_val=N_EXP - 1)
                    for n, slot in enumerate(ITEM_SLOTS[0]):
                        sp.dma_start(ring[:, slot, :], dram["w_exp"][bass.ds(expert, 1)].rearrange("e p i n -> p (e i n)")[:, n * 4096:(n + 1) * 4096])\
                          .then_inc(sig("over_loaded"), 16)
            sp.wait_ge(sig("out_ready"), NB)
            sp.dma_start(dram["out"], merge[:, :, 0, :]).then_inc(sig("out_stored"), 16)
            sp.wait_ge(sig("out_stored"), 16)

        @block.gpsimd
        def _(pool):
            pool.memset(raw[:, :, 0:TAPS - 1], 0.0).then_inc(sig("raw_padded"), 1)
            pool.wait_ge(sig("const_loaded"), 32)
            for t in (inv, invT):
                pool.tensor_copy(t.rearrange("p b h n -> p (b h) n"), spread(ident, 1, NB * H_GDN)).then_inc(sig("inverse_started"), 1)
            pool.wait_ge(sig("o_normed"), 1)
            pool.memset(u2[:, :, 0:1], 0.0)
            pool.memset(u2[:, :, T + 1:T + 2], 0.0).then_inc(sig("u2_padded"), 1)

        @block.tensor
        def _(pe):
            def transposes(bank, sources, signal):
                for n, s in enumerate(sources):
                    m = pe.transpose(ps[:, bank, n * P:(n + 1) * P], s, ident)
                m.then_inc(sig(signal), 1)

            def turn_rows(tok, ready, signal, first_free=None):
                for b in range(NB):
                    pe.wait_ge(sig(ready), since(ready, b + 1))
                    for half in range(2):
                        transposes(2 * b + half, [tok[:, b, (4 * half + n) * P:(4 * half + n + 1) * P] for n in range(4)], signal)

            def project(c):
                w = arrived(pe, ("w_in", c)).rearrange("p (k n) -> p k n", n=BANK)
                width = 288 if c == 6 else BANK
                for b in range(NB):
                    n = 2 * (c - 3) + b
                    if n >= 4:
                        pe.wait_ge(sig("projected_out"), n - 3)
                    for k in range(KT):
                        m = pe.matmul(ps[:, n % 4, 0:width], hT[:, k, b * P:(b + 1) * P], w[:, k, 0:width],
                                      start=(k == 0), stop=(k == KT - 1))
                    m.then_inc(sig("projected"), 1)
                pe.wait_ge(sig("projected"), 2 * (c - 3) + 2)
                pe.sem_inc(sig("slot_free"), 1)

            pe.wait_ge(sig("const_loaded"), 32)
            turn_rows(merge[:, :, 0, :], "x_normed", "x_turned")
            pe.wait_ge(sig("h_ready"), since("h_ready", 4))
            for c in range(3):
                w = arrived(pe, ("w_in", c)).rearrange("p (k n) -> p k n", n=BANK)
                for pr in range(2 * c, 2 * c + 2):
                    if pr >= 4:
                        pe.wait_ge(sig("qkv_out"), pr - 3)
                    for ct in (2 * pr, 2 * pr + 1):
                        for k in range(KT):
                            m = pe.matmul(ps[:, 4 + pr % 4, (ct % 2) * T:(ct % 2 + 1) * T],
                                          w[:, k, (ct % 4) * P:(ct % 4 + 1) * P], hT[:, k, :],
                                          start=(k == 0), stop=(k == KT - 1))
                    m.then_inc(sig("qkv_projected"), 1)
                pe.wait_ge(sig("qkv_projected"), 2 * c + 2)
                pe.sem_inc(sig("slot_free"), 1)
            for c in range(3, 7):
                project(c)

            pe.wait_ge(sig("qkv_out"), 6)
            pe.wait_ge(sig("g_spread"), since("g_spread", 2))
            for b in range(NB):
                for h in range(H_GDN):
                    pe.matmul(pair(4)[:, b, h, :], g_lhs[:, b, h, :], sq(CUM), start=True, stop=True)
                    pe.matmul(pair(6)[:, b, h, :], beta_lhs[:, b, h, :], ident, start=True, stop=True)
            pe.wait_ge(sig("projected_out"), 8)
            gt = g_tok.rearrange("p b h -> p (b h)")
            pe.matmul(ps[:, 0, 0:8], sq(CUM), gt, start=True, stop=True)
            pe.matmul(ps[:, 0, 8:16], sq(SAME), gt, start=True, stop=True).then_inc(sig("gc_ready"), 1)
            pe.wait_ge(sig("gc_out"), since("gc_out", 2))
            pe.wait_ge(sig("beta_used"), since("beta_used", 1))
            pe.wait_ge(sig("qk_squared"), since("qk_squared", 1))
            for n in range(4):
                m = pe.matmul(ps[:, 4 + n, :], sq(ONES), qkT_sq[:, 2 * n:2 * n + 2, :].rearrange("p c t -> p (c t)"),
                              start=True, stop=True)
            m.then_inc(sig("qk_summed"), 1)
            project(7)
            pe.wait_ge(sig("kb_ready"), since("kb_ready", 1))
            for b in range(NB):
                for h in range(H_GDN):
                    pe.matmul(pair(4)[:, b, h, :], kT[:, b, h, :], kbT[:, b, h, :], start=True, stop=True)
                    m = pe.matmul(pair(6)[:, b, h, :], kT[:, b, h, :], qT[:, b, h, :], start=True, stop=True)
            m.then_inc(sig("kk_ready"), 1)
            project(8)
            for n, (src, done) in enumerate(((kT, "a_ready"), (vT, "qk_ready"))):
                pe.wait_ge(sig(done), since(done, 1))
                for b in range(NB):
                    for h in range(H_GDN):
                        m = pe.transpose(pair(4 + 2 * n)[:, b, h, :], src[:, b, h, :], ident)
                m.then_inc(sig("kv_turned"), 1)
            project(9)
            project(10)
            pe.wait_ge(sig("projected_out"), 16)
            pe.wait_ge(sig("kd_ready"), since("kd_ready", 1))
            pe.wait_ge(sig("inverse_started"), 2)
            for n in range(N_LEVEL):
                pe.wait_ge(sig("off_ready"), n + 1)
                for b in range(NB):
                    for h in range(H_GDN):
                        m = pe.matmul(pair(0)[:, b, h, :], off[:, b, h, :], inv[:, b, h, :], start=True, stop=True)
                m.then_inc(sig("mid_made"), 1)
                pe.wait_ge(sig("mid_ready"), n + 1)
                for b in range(NB):
                    for h in range(H_GDN):
                        pe.matmul(pair(2)[:, b, h, :], invT[:, b, h, :], mid[:, b, h, :], start=True, stop=True)
                        m = pe.matmul(pair(4)[:, b, h, :], mid[:, b, h, :], invT[:, b, h, :], start=True, stop=True)
                m.then_inc(sig("step_made"), 1)
                pe.wait_ge(sig("inverse_ready"), n + 1)
            for b in range(NB):
                for h in range(H_GDN):
                    pe.matmul(pair(0)[:, b, h, :], invT[:, b, h, :], vb[:, b, h, :], start=True, stop=True)
                    m = pe.matmul(pair(2)[:, b, h, :], kbg[:, b, h, :], invT[:, b, h, :], start=True, stop=True)
            m.then_inc(sig("uw_made"), 1)
            for c in range(N_CHUNK):
                b, r = c // 2, slice(CHUNK * (c % 2), CHUNK * (c % 2) + CHUNK)
                heads = range(H_GDN)
                if c:
                    pe.wait_ge(sig("uw_ready"), 2)
                    pe.wait_ge(sig("state_ready"), c)
                    for h in heads:
                        m = pe.matmul(ps[r, 4, h * P:(h + 1) * P], wT[:, b, h, r], state[:, c % 2, h, :], start=True, stop=True)
                    m.then_inc(sig("ws_made"), 1)
                pe.wait_ge(sig("vnew_ready"), c + 1)
                if c < N_CHUNK - 1:
                    for h in heads:
                        m = pe.matmul(ps[:, 5, h * P:(h + 1) * P], kd[r, b, h, :], vnew[r, b, h, :], start=True, stop=True)
                    m.then_inc(sig("kv_made"), 1)
                for h in heads:
                    if c:
                        pe.matmul(pair(6)[r, b, h, :], qgT[:, b, h, r], state[:, c % 2, h, :], start=True, stop=False)
                    m = pe.matmul(pair(6)[r, b, h, :], qk_decay[r, b, h, r], vnew[r, b, h, :], start=(c == 0), stop=True)
                m.then_inc(sig("o_made"), 1)
            pe.wait_ge(sig("o_normed"), 1)
            for b in range(NB):
                for h in range(H_GDN):
                    m = pe.transpose(pair(0)[:, b, h, :], o_gdn[:, b, h, :], ident)
            m.then_inc(sig("o_turned"), 1)

            pe.wait_ge(sig("roped"), since("roped", 1))
            pe.wait_ge(sig("oa_ready"), 1)
            for b in range(NB):
                transposes(b, [nsa[:, b, 2 * r:2 * r + 2, :].rearrange("p h d -> p (h d)") for r in range(NSA_R)], "nq_turned")
            transposes(2, [nsa[:, b, h:h + 2, :].rearrange("p h d -> p (h d)") for h in (12, 16) for b in range(NB)], "nk_turned")
            for s in range(2):
                for g in range(NSA_G):
                    for b in range(NB):
                        for l2 in range(2):
                            at = (2 * s + g) * P + b * CHUNK
                            m = pe.matmul(ps[l2 * NSA_D:(l2 + 1) * NSA_D, 3, at:at + CHUNK], nsa[:, b, 8 + 2 * s + g, :],
                                          ident[:, l2::2], start=True, stop=True)
            m.then_inc(sig("pairs_made"), 1)
            w1 = arrived(pe, ("cmp", 0)).rearrange("p (s a n) -> p s a n", s=2, a=CMP_A)
            pe.wait_ge(sig("pairs_ready"), since("pairs_ready", 1))
            n = NSA_G * N_CMP
            for s in range(2):
                for a in range(CMP_A):
                    m = pe.matmul(ps[:, 4 + s, 0:n], w1[:, s, a, :], pairs[:, s, a, :, :].rearrange("p g n -> p (g n)"),
                                  start=(a == 0), stop=(a == CMP_A - 1))
                m.then_inc(sig("hid_made"), 1)
            pe.wait_ge(sig("hid_made"), since("hid_made", 2))
            pe.sem_inc(sig("slot_free"), 1)
            pe.wait_ge(sig("nsa_const_loaded"), 48)
            pe.wait_ge(sig("hid_ready"), since("hid_ready", 2))
            for g in range(NSA_G):
                pe.matmul(ps[g * NSA_D:(g + 1) * NSA_D, 4, 64:80], cmp_w2[:, 0, :], hid[:, 0, g, :], start=True, stop=True)
            pe.wait_ge(sig("hid_rep_ready"), since("hid_rep_ready", 1))
            pe.matmul(ps[:, 4, 128:192], hid_rep.rearrange("p g r n -> p (g r n)"), cmp_w2[:, 1, :], start=True, stop=True)\
              .then_inc(sig("kv_cmp_made"), 1)
            pe.wait_ge(sig("nq_ready"), since("nq_ready", 2))
            for b in range(NB):
                pe.wait_ge(sig("kv_cmp_ready"), since("kv_cmp_ready", 1))
                if b:
                    pe.wait_ge(sig("o_cmp_out"), b)
                for h in range(NSA_H):
                    r, g = h // NSA_G, h % NSA_G
                    gp = slice(g * NSA_D, (g + 1) * NSA_D)
                    m = pe.matmul(ps[:, 5 + g, r * CMP_STRIDE:(r + 1) * CMP_STRIDE], nqT[gp, r, b * P:(b + 1) * P], kcT[gp, :],
                                  start=True, stop=True)
                m.then_inc(sig("s_cmp_made"), 1)
                pe.wait_ge(sig("p_cmp_ready"), b + 1)
                pe.transpose(ps[:, 7, 0:128], p_cmp.rearrange("p h n -> p (h n)"), ident).then_inc(sig("p_cmp_turned"), 1)
                pe.wait_ge(sig("p_cmpT_ready"), b + 1)
                pe.matmul(ps[:, 4, :], p_cmpT, v_cmp.rearrange("p h d -> p (h d)"), start=True, stop=True)\
                  .then_inc(sig("o_cmp_made"), 1)
            pe.wait_ge(sig("nk_ready"), since("nk_ready", 1))
            pe.wait_ge(sig("o_cmp_out"), NB)
            for j, (b, s) in enumerate(JOBS):
                nk = (b + 1) * P
                if j:
                    pe.wait_ge(sig("scores_out"), j)
                for n in range(NSA_H):
                    r, g = n // NSA_G, n % NSA_G
                    h = g * NSA_R + r
                    gp = slice(g * NSA_D, (g + 1) * NSA_D)
                    m = pe.matmul(ps[:, h * nk // BANK, h * nk % BANK:h * nk % BANK + nk],
                                  nqT[gp, r, b * P:(b + 1) * P], nkT[gp, s, 0:nk], start=True, stop=True)
                m.then_inc(sig("scores_made"), 1)
                for half in range(b + 1):
                    pe.wait_ge(sig("probs_ready"), j + 1)
                    at = sum(bb + 1 for bb, _ in JOBS[:j]) + half
                    if at:
                        pe.wait_ge(sig("probsT_ready"), at)
                    for n in range(8):
                        src = probs[j % 2][:, (8 * half + n) * P:(8 * half + n + 1) * P]
                        m = pe.transpose(ps[:, 4 + n // 4, (n % 4) * P:(n % 4 + 1) * P], src, ident)
                    m.then_inc(sig("probs_turned"), 1)
                at = sum(bb + 1 for bb, _ in JOBS[:j + 1])
                pe.wait_ge(sig("probsT_ready"), at)
                if j:
                    pe.wait_ge(sig("o_job_out"), j)
                for h in range(NSA_H):
                    for kb in range(b + 1):
                        m = pe.matmul(ps[:, 6, h * NSA_D:(h + 1) * NSA_D], probsT_all[:, h * (b + 1) + kb, :],
                                      nsa[:, kb, 14 + 4 * s + h // NSA_R, :], start=(kb == 0), stop=(kb == b))
                m.then_inc(sig("o_job_made"), 1)
            pe.wait_ge(sig("o_nsa_ready"), NB)
            for b in range(NB):
                transposes(b, [o_nsa[:, b, n * P:(n + 1) * P] for n in range(4)], "ob_turned")

            pe.wait_ge(sig("ob_ready"), NB)
            for br, src in enumerate((oaT, obT)):
                w = arrived(pe, ("branch", br)).rearrange("p (k n) -> p k n", n=D)
                for b in range(NB):
                    for half in range(2):
                        for k in range(4):
                            m = pe.matmul(ps[:, 4 * b + 2 * br + half, :], src[:, k, b * P:(b + 1) * P],
                                          w[:, k, half * BANK:(half + 1) * BANK], start=(k == 0), stop=(k == 3))
                m.then_inc(sig("branch_made"), 1)
                pe.wait_ge(sig("branch_made"), br + 1)
                pe.sem_inc(sig("slot_free"), 1)
            for b in range(NB):
                pe.wait_ge(sig("merged"), NB)
                for half in range(2):
                    transposes(2 * b + half, [merge[:, b, 0, (4 * half + n) * P:(4 * half + n + 1) * P] for n in range(4)], "merge_turned")
            pe.wait_ge(sig("mergedT_ready"), 4)
            for half in range(2):
                w = arrived(pe, ("w_out", half)).rearrange("p (k n) -> p k n", n=BANK)
                for b in range(NB):
                    for k in range(KT):
                        m = pe.matmul(ps[:, 4 + 2 * b + half, :], hT[:, k, b * P:(b + 1) * P], w[:, k, :],
                                      start=(k == 0), stop=(k == KT - 1))
                m.then_inc(sig("w_out_made"), 1)
                pe.wait_ge(sig("w_out_made"), half + 1)
                pe.sem_inc(sig("slot_free"), 1)

            pe.wait_ge(sig("mix_const_loaded"), 160)
            pe.matmul(ps[0:64, 0, 0:T], filt_in, emb, start=True, stop=True).then_inc(sig("filt_layer"), 1)
            for n in range(2):
                pe.wait_ge(sig("filt_sin"), since("filt_sin", n + 1))
                pe.matmul(ps[0:64, 0, 0:T], filt_mid[:, n * 64:(n + 1) * 64], act_a, start=True, stop=True).then_inc(sig("filt_layer"), 1)
            pe.wait_ge(sig("filt_sin"), since("filt_sin", 3))
            for b in range(NB):
                for d in range(2):
                    m = pe.matmul(ps[:, 2 * b + d, :], act_a[:, b * P:(b + 1) * P], filt_out[:, d * DH2:(d + 1) * DH2], start=True, stop=True)
            m.then_inc(sig("filt_out_made"), 1)
            pe.wait_ge(sig("kern_ready"), since("kern_ready", 1))
            for f in range(4):
                for n, (mat, b, d) in enumerate(((dft_fwd, 0, 0), (dft_fwd, 1, 0), (dft_bwd, 0, 1), (dft_bwd, 1, 1))):
                    m = pe.matmul(ps[:, f, :], mat[:, b, f * P:(f + 1) * P], kern[:, b, d, :], start=(n == 0), stop=(n == 3))
            m.then_inc(sig("kernF_made"), 1)
            pe.wait_ge(sig("kern_abs_ready"), since("kern_abs_ready", 1))
            pe.wait_ge(sig("x2_added"), 1)
            for ct in range(NHT):
                for n in range(4):
                    b, d = n // 2, n % 2
                    one = C_ONE + (1 if (b, d) == (0, 1) else 0)
                    m = pe.matmul(ps[:, 4, ct:ct + 1], kern_abs[:, b, d, ct * P:(ct + 1) * P], cols[:, one:one + 1],
                                  start=(n == 0), stop=(n == 3))
            m.then_inc(sig("filter_turned"), 1)
            pe.wait_ge(sig("kernF_ready"), since("kernF_ready", 1))
            pe.wait_ge(sig("filt_norm_ready"), since("filt_norm_ready", 1))
            for b in range(NB):
                pe.wait_ge(sig("x2_normed"), since("x2_normed", b + 1))
                for half in range(2):
                    transposes(2 * b + half, [merge[:, b, 0, (4 * half + n) * P:(4 * half + n + 1) * P] for n in range(4)], "x2_turned")
            pe.wait_ge(sig("h2_ready"), since("h2_ready", 4))

            def gate_up(s, first=False):
                pe.wait_ge(sig(f"gu{s.par}_loaded"), 16 * s.turns)
                w = ring[:, s.par, :].rearrange("p (k n) -> p k n", n=BANK)
                if not first:
                    pe.wait_ge(sig("gatedT_ready"), s.n - 1)
                for b in range(NB):
                    for k in range(KT):
                        m = pe.matmul(ps[:, 2 * s.par + b, :], hT[:, k, b * P:(b + 1) * P], w[:, k, :],
                                      start=(k == 0), stop=(k == KT - 1))
                    m.then_inc(sig("gu_made"), 1)
                pe.wait_ge(sig("gu_made"), 2 * s.n + 2)
                pe.sem_inc(sig("gu_free"), 1)

            def down(s, start=False, stop=False):
                pe.wait_ge(sig("gated_ready"), s.n + 1)
                for b in range(NB):
                    for f in range(FC // P):
                        m = pe.transpose(ps[:, 2 * s.par + b, f * P:(f + 1) * P], gated[:, s.par, b, f * P:(f + 1) * P], ident)
                m.then_inc(sig("gated_turned"), 1)
                pe.wait_ge(sig(f"dn{s.par}_loaded"), 16 * s.turns)
                pe.wait_ge(sig("gatedT_ready"), s.n + 1)
                w = ring[:, 2, s.par * 2048:(s.par + 1) * 2048].rearrange("p (f n) -> p f n", n=D)
                for b in range(NB):
                    for half in range(2):
                        for f in range(FC // P):
                            m = pe.matmul(ps[:, 4 + 2 * b + half, :], gatedT[:, s.par, b, f, :], w[:, f, half * BANK:(half + 1) * BANK],
                                          start=start and f == 0, stop=stop and f == FC // P - 1, skip_group_check=True)
                m.then_inc(sig("down_made"), 1)
                pe.wait_ge(sig("down_made"), s.n + 1)
                pe.sem_inc(sig("dn_free"), 1)

            gate_up(Step(0), first=True)
            gate_up(Step(1), first=True)
            down(Step(0), start=True)
            with pe.Fori(0, (N_FC - 3) // 2) as i:
                for parity in range(2):
                    s, nxt = Step(i=i, parity=parity), Step(i=i, parity=parity)
                    nxt.n, nxt.par, nxt.turns = 2 * i + parity + 2, parity, i + 2
                    gate_up(nxt)
                    down(s)
            gate_up(Step(N_FC - 1))
            down(Step(N_FC - 2))
            down(Step(N_FC - 1), stop=True)

            def mix_weights(slot):
                pe.wait_ge(sig(f"slot{slot}_loaded"), 16 * (len(stream) // 4 + 1 if slot < 4 else 1))

            for b in range(NB):
                pe.wait_ge(sig("x3_normed"), since("x3_normed", b + 1))
                for half in range(2):
                    transposes(2 * b + half, [merge[:, b, 0, (4 * half + n) * P:(4 * half + n + 1) * P] for n in range(4)], "x3_turned")
            pe.wait_ge(sig("h3_ready"), since("h3_ready", 4))
            for c in range(3):
                mix_weights(IN2_SLOTS[c])
                w = ring[:, IN2_SLOTS[c], :].rearrange("p (k n) -> p k n", n=BANK)
                for pr in range(2 * c, 2 * c + 2):
                    if pr >= 4:
                        pe.wait_ge(sig("u2_out"), pr - 3)
                    for ct in (2 * pr, 2 * pr + 1):
                        for k in range(KT):
                            m = pe.matmul(ps[:, 4 + pr % 4, (ct % 2) * T:(ct % 2 + 1) * T],
                                          w[:, k, (ct % 4) * P:(ct % 4 + 1) * P], hT[:, k, :],
                                          start=(k == 0), stop=(k == KT - 1))
                    m.then_inc(sig("u2_projected"), 1)
            mix_weights(IN2_SLOTS[3])
            w = ring[:, IN2_SLOTS[3], :].rearrange("p (k n) -> p k n", n=BANK)
            for b in range(NB):
                for k in range(KT):
                    m = pe.matmul(ps[:, b, :], hT[:, k, b * P:(b + 1) * P], w[:, k, :], start=(k == 0), stop=(k == KT - 1))
                m.then_inc(sig("four_projected"), 1)
            pe.wait_ge(sig("four_ready"), since("four_ready", NB))
            for ct in range(NHT):
                for b in range(NB):
                    m = pe.matmul(ps[:, ct, :], u_four[:, b, ct * P:(ct + 1) * P], dft_time[:, b, :], start=(b == 0), stop=(b == NB - 1))
                m.then_inc(sig("four1_made"), 1)
            pe.wait_ge(sig("z_ready"), since("z_ready", 1))
            for b in range(NB):
                transposes(4 + b, [zT[:, ct, b * P:(b + 1) * P] for ct in range(NHT)], "z_turned")
            pe.wait_ge(sig("four1_ready"), since("four1_ready", NHT))
            for ct in range(NHT):
                at = ps[:, 6 + ct // 2, (ct % 2) * T:(ct % 2 + 1) * T]
                pe.matmul(at, sq(DFT_C), four1[:, ct, 0:T], start=True, stop=False)
                m = pe.matmul(at, sq(DFT_S), four1[:, ct, T:2 * T], start=False, stop=True)
            m.then_inc(sig("four2_made"), 1)
            pe.wait_ge(sig("z_tok_ready"), since("z_tok_ready", NB))
            for f in range(4):
                for b in range(NB):
                    m = pe.matmul(ps[:, f, :], dft_fwd[:, b, f * P:(f + 1) * P], z_tok[:, b, :], start=(b == 0), stop=(b == NB - 1))
                m.then_inc(sig("zF_made"), 1)
            pe.wait_ge(sig("prod_ready"), since("prod_ready", 1))
            for ct in range(NHT):
                for f in range(4):
                    m = pe.matmul(ps[:, 4 + ct // 2, (ct % 2) * T:(ct % 2 + 1) * T], prodF[:, f, ct * P:(ct + 1) * P],
                                  dft_inv[:, f, :], start=(f == 0), stop=(f == 3))
            m.then_inc(sig("conv_made"), 1)
            for n in range(2):
                pe.wait_ge(sig("y_squared"), since("y_squared", n + 1))
                for half in range(2):
                    m = pe.matmul(ps[:, 2 * n + half, :], sq(SAME), y_sq[n][:, half * BANK:(half + 1) * BANK], start=True, stop=True)
            m.then_inc(sig("y_summed"), 1)
            pe.wait_ge(sig("y_ready2"), since("y_ready2", 2))
            for half in range(2):
                mix_weights(OUT2_SLOTS[half])
                w = ring[:, OUT2_SLOTS[half], :].rearrange("p (k n) -> p k n", n=BANK)
                for b in range(NB):
                    for k in range(KT):
                        src = y_hy if k < NHT else y_fo
                        m = pe.matmul(ps[:, 4 + 2 * b + half, :], src[:, k % NHT, b * P:(b + 1) * P], w[:, k, :],
                                      start=(k == 0), stop=(k == KT - 1))
            m.then_inc(sig("out2_made"), 1)

            for b in range(NB):
                pe.wait_ge(sig("x4_normed"), since("x4_normed", b + 1))
                for half in range(2):
                    transposes(2 * b + half, [merge[:, b, 0, (4 * half + n) * P:(4 * half + n + 1) * P] for n in range(4)], "x4_turned")
            pe.wait_ge(sig("h4_ready"), since("h4_ready", 4))
            n = N_GRP + N_EXP
            for b in range(NB):
                for k in range(KT):
                    m = pe.matmul(ps[:, 4, b * n:(b + 1) * n], hT[:, k, b * P:(b + 1) * P], w_route[:, k, :], start=(k == 0), stop=(k == KT - 1))
            m.then_inc(sig("logits_made"), 1)
            pe.wait_ge(sig("chosen_ready"), since("chosen_ready", 1))
            pe.matmul(ps[:, 3, 0:32], sq(RANK), chosen[:, 0, :], start=True, stop=True)
            pe.matmul(ps[:, 3, 32:64], sq(ONES), chosen[:, 0, :], start=True, stop=False)
            pe.matmul(ps[:, 3, 32:64], sq(RANK), chosen[:, 1, :], start=False, stop=True)
            pe.matmul(ps[:, 3, 64:96], sq(ONES), chosen[:, 0, :], start=True, stop=False)
            pe.matmul(ps[:, 3, 64:96], sq(ONES), chosen[:, 1, :], start=False, stop=True).then_inc(sig("ranks_made"), 1)
            gather, item_gate_up, add_turn, item_down, scatter = item_steps(pe)
            pe.wait_ge(sig("zero_ready"), since("zero_ready", 1))
            for bank in range(4, 8):
                pe.matmul(ps[:, bank, :], zero, squares[:, 0:4, :].rearrange("p a n -> p (a n)"), start=True, stop=False, skip_group_check=True)

            def rows_and_gate_up(par, n, turn, before=None):
                pe.wait_ge(sig("picked"), n + 1)
                gather(par).then_inc(sig("gathered"), 1)
                if before:
                    before()
                pe.wait_ge(sig("hg_ready"), n + 1)
                for k in range(2):
                    pe.wait_ge(sig(f"item{par}_{k}_loaded"), 16 * turn)
                item_gate_up(par, ITEM_SLOTS[par]).then_inc(sig("item_gu_made"), 1)

            def to_tokens(n, stop=False):
                pe.wait_ge(sig("part_d_scalar"), n + 1)
                pe.wait_ge(sig("part_d_vector"), n + 1)
                scatter(False, stop).then_inc(sig("scattered"), 1)

            def down_rows(par, n, turn, last=False):
                pe.wait_ge(sig("part_g_ready"), n + 1)
                pe.wait_ge(sig("part_u_ready"), n + 1)
                add_turn(par).then_inc(sig("added"), 1)
                pe.wait_ge(sig("act_ready"), n + 1)
                if not last:
                    pe.wait_ge(sig("part_g_ready"), n + 2)
                    pe.wait_ge(sig("part_u_ready"), n + 2)
                pe.wait_ge(sig(f"item{par}_2_loaded"), 16 * turn)
                item_down(ITEM_SLOTS[par][2]).then_inc(sig("item_down_made"), 1)

            rows_and_gate_up(0, 0, 1)

            def first_parts_out():
                pe.wait_ge(sig("part_g_ready"), 1)
                pe.wait_ge(sig("part_u_ready"), 1)

            rows_and_gate_up(1, 1, 1, before=first_parts_out)
            down_rows(0, 0, 1)
            with pe.Fori(0, N_EXP // 2 - 1) as i:
                for par in (1, 0):
                    n = 2 * i + 2 - par
                    rows_and_gate_up(1 - par, n + 1, i + 2, before=lambda: to_tokens(n - 1))
                    down_rows(par, n, i + 1 if par else i + 2)
            to_tokens(N_EXP - 2)
            down_rows(1, N_EXP - 1, N_EXP // 2, last=True)
            to_tokens(N_EXP - 1, stop=True)
            pe.wait_ge(sig("table_ready"), since("table_ready", 1))
            n_over = pe.value_load(table_i[0:1, 16:17], min_val=0, max_val=16)
            with pe.If(n_over > 0):
                with pe.Fori(0, n_over) as i:
                    pe.wait_ge(sig("over_vector"), 5 * i + 1)
                    gather(0).then_inc(sig("over_tensor"), 1)
                    pe.wait_ge(sig("over_vector"), 5 * i + 2)
                    pe.wait_ge(sig("over_loaded"), 48 * i + 48)
                    item_gate_up(0, ITEM_SLOTS[0]).then_inc(sig("over_tensor"), 1)
                    pe.wait_ge(sig("over_vector"), 5 * i + 3)
                    add_turn(0).then_inc(sig("over_tensor"), 1)
                    pe.wait_ge(sig("over_vector"), 5 * i + 4)
                    item_down(ITEM_SLOTS[0][2]).then_inc(sig("over_tensor"), 1)
                    pe.wait_ge(sig("over_vector"), 5 * i + 5)
                    scatter(True, True).then_inc(sig("over_tensor"), 1)

        @block.scalar
        def _(act):
            link = chain(act, "act_chain")

            def root(values, ready, n, done):
                act.wait_ge(sig(ready), since(ready, n))
                act.activation(values, values, ACT.Sqrt).then_inc(sig(done), 1)

            root(stat[:, 0:NB], "row_mean", 1, "row_root")
            act.wait_ge(sig("raw_padded"), 1)
            for pr in range(6):
                act.wait_ge(sig("qkv_projected"), pr + 1)
                act.activation(raw[:, 2 * pr:2 * pr + 2, TAPS - 1:], ps[:, 4 + pr % 4, :].rearrange("p (c t) -> p c t", t=T),
                               ACT.Copy).then_inc(sig("qkv_out"), 1)

            def columns_out(n, out, func):
                act.wait_ge(sig("projected"), n + 1)
                return act.activation(out, ps[:, n % 4, 0:out.free_size()], func)

            for b in range(NB):
                columns_out(b, silu_z[:, b, :], ACT.Silu).then_inc(sig("projected_out"), 1)
            for b in range(NB):
                act.wait_ge(sig("projected"), 3 + b)
                act.activation(nsa[:, b, 0:NSA_H, :].rearrange("p (r g) d -> p g r d", g=NSA_G),
                               ps[:, 2 + b, :].rearrange("p (g r d) -> p g r d", g=NSA_G, d=NSA_D), ACT.Copy)\
                   .then_inc(sig("projected_out"), 1)
            flat = nsa.rearrange("p b h d -> p b (h d)")
            for b in range(NB):
                columns_out(4 + b, flat[:, b, 512:1024], ACT.Copy).then_inc(sig("projected_out"), 1)
            for b in range(NB):
                act.wait_ge(sig("projected"), 7 + b)
                act.activation(flat[:, b, 1024:1280], ps[:, 2 + b, 0:256], ACT.Copy)
                act.activation(ctl[:, b, 0:28], ps[:, 2 + b, 256:284], ACT.Sigmoid)
                act.activation(ctl[:, b, 28:32], ps[:, 2 + b, 284:288], ACT.Copy).then_inc(sig("projected_out"), 1)
            act.wait_ge(sig("y_ready"), since("y_ready", 1))
            link(act.activation(sp_m, sp_y, ACT.Abs))
            link(act.activation(sp_m, sp_m, ACT.Exp, scale=-1.0))
            link(act.activation(sp_m, sp_m, ACT.Ln, bias=1.0))
            act.activation(small[:, 64:68], rows[:, R_ALOG:R_ALOG + 4], ACT.Exp).then_inc(sig("softplus_ready"), 1)
            act.wait_ge(sig("conv_ready"), since("conv_ready", 1))
            link(act.activation(convT.rearrange("p c t -> p (c t)"), convT.rearrange("p c t -> p (c t)"), ACT.Silu))
            act.activation(qkT_sq.rearrange("p c t -> p (c t)"), convT[:, 0:8, :].rearrange("p c t -> p (c t)"),
                           ACT.Square).then_inc(sig("qk_squared"), 1)
            act.wait_ge(sig("gc_ready"), since("gc_ready", 1))
            act.activation(exp_gc.rearrange("p b h n -> p b (h n)"), ps[:, 4:6, :], ACT.Exp).then_inc(sig("exp_gc_ready"), 1)
            act.wait_ge(sig("gc_out"), since("gc_out", 2))
            link(act.activation(decayT.rearrange("p b h n -> p (b h n)"), decayT.rearrange("p b h n -> p (b h n)"), ACT.Exp))
            act.activation(e_last, e_last, ACT.Exp)
            act.activation(beta_g, gc, ACT.Exp).then_inc(sig("decays_ready"), 1)
            act.wait_ge(sig("sums_out"), since("sums_out", 1))
            norms = own[:, 4:6, :]
            act.activation(norms, norms, ACT.Sqrt).then_inc(sig("norms_ready"), 1)
            for n in range(8, 16):
                branch, half, b = (n - 8) // 4, (n - 8) // 2 % 2, n % 2
                columns_out(n, merge[:, b, branch, half * BANK:(half + 1) * BANK], ACT.Sigmoid).then_inc(sig("projected_out"), 1)
            for n in range(N_LEVEL):
                act.wait_ge(sig("mid_made"), n + 1)
                if n:
                    act.wait_ge(sig("inverse_ready"), n)
                act.activation(mid, pair(0), ACT.Copy).then_inc(sig("mid_ready"), 1)
            act.wait_ge(sig("uw_made"), 1)
            act.wait_ge(sig("inverse_ready"), N_LEVEL)
            act.activation(uu, pair(0), ACT.Copy).then_inc(sig("uw_ready"), 1)
            act.activation(wT, pair(2), ACT.Copy).then_inc(sig("uw_ready"), 1)
            act.wait_ge(sig("o_made"), N_CHUNK)
            link(act.activation(o_gdn, pair(6), ACT.Copy))
            act.activation(o_sq, o_gdn, ACT.Square).then_inc(sig("o_squared"), 1)
            root(o_ss, "o_mean", 1, "o_root")
            act.wait_ge(sig("o_turned"), 1)
            act.activation(oaT.rearrange("p h (b t) -> p b h t", b=NB), pair(0), ACT.Copy).then_inc(sig("oa_ready"), 1)

            for b in range(NB):
                act.wait_ge(sig("nq_turned"), since("nq_turned", b + 1))
                act.activation(nqT[:, :, b * P:(b + 1) * P], ps[:, b, :].rearrange("p (r t) -> p r t", t=P), ACT.Copy)\
                   .then_inc(sig("nq_ready"), 1)
            act.wait_ge(sig("nk_turned"), since("nk_turned", 1))
            act.activation(nkT.rearrange("p s t -> p (s t)"), ps[:, 2, :], ACT.Copy).then_inc(sig("nk_ready"), 1)
            act.wait_ge(sig("hid_zeroed"), since("hid_zeroed", 1))
            for s in range(2):
                act.wait_ge(sig("hid_made"), since("hid_made", s + 1))
                act.activation(hid[:, s, :, 0:N_CMP], ps[:, 4 + s, 0:NSA_G * N_CMP].rearrange("p (g n) -> p g n", n=N_CMP),
                               ACT.Silu).then_inc(sig("hid_ready"), 1)
            for b in range(NB):
                act.wait_ge(sig("s_cmp_ready"), b + 1)
                act.activation(p_cmp, p_cmp, ACT.Exp, scale=float(NSA_D) ** -0.5).then_inc(sig("exp_cmp_ready"), 1)
                act.wait_ge(sig("p_cmp_turned"), b + 1)
                act.activation(p_cmpT, ps[:, 7, 0:128], ACT.Copy).then_inc(sig("p_cmpT_ready"), 1)
            turned = 0
            for j, (b, s) in enumerate(JOBS):
                nk = (b + 1) * P
                p = probs[j % 2].rearrange("p (h n) -> p h n", n=nk) if b else probs[j % 2][:, 0:1024].rearrange("p (h n) -> p h n", n=nk)
                act.wait_ge(sig("maxima_ready"), j + 1)
                for h in range(NSA_H):
                    ins = act.activation(p[:, h, :], p[:, h, :], ACT.Exp, bias=soft[:, 8 * j + h:8 * j + h + 1],
                                         scale=float(NSA_D) ** -0.5, accum_out=soft[:, 32 + 8 * j + h:33 + 8 * j + h])
                ins.then_inc(sig("probs_ready"), 1)
                for half in range(b + 1):
                    turned += 1
                    act.wait_ge(sig("probs_turned"), turned)
                    if j and half == 0:
                        act.wait_ge(sig("o_job_made"), j)
                    act.activation(probsT_all[:, 8 * half:8 * half + 8, :], ps[:, 4:6, :].rearrange("p b (h n) -> p (b h) n", n=P),
                                   ACT.Copy).then_inc(sig("probsT_ready"), 1)
            for b in range(NB):
                act.wait_ge(sig("ob_turned"), b + 1)
                act.activation(obT[:, :, b * P:(b + 1) * P], ps[:, b, :].rearrange("p (h t) -> p h t", t=P), ACT.Copy)\
                   .then_inc(sig("ob_ready"), 1)

            def plain_out(signal_in, signal_out):
                for n in range(4):
                    b, half = n // 2, n % 2
                    act.wait_ge(sig(signal_in), since(signal_in, n + 1))
                    act.activation(hT[:, 4 * half:4 * half + 4, b * P:(b + 1) * P],
                                   ps[:, n, :].rearrange("p (k t) -> p k t", t=P), ACT.Copy).then_inc(sig(signal_out), 1)

            plain_out("merge_turned", "mergedT_ready")
            for n in range(3):
                act.wait_ge(sig("arg_ready"), since("arg_ready", n + 1))
                act.activation(act_a, arg, ACT.Sin).then_inc(sig("filt_sin"), 1)
            act.wait_ge(sig("kern_ready"), since("kern_ready", 1))
            act.activation(kern_abs.rearrange("p b d n -> p (b d n)"), kern.rearrange("p b d n -> p (b d n)"), ACT.Abs).then_inc(sig("kern_abs_ready"), 1)
            act.wait_ge(sig("kernF_made"), since("kernF_made", 1))
            act.activation(kernF.rearrange("p f n -> p (f n)"), ps[:, 0:4, :].rearrange("p f n -> p (f n)"), ACT.Copy).then_inc(sig("kernF_ready"), 1)
            root(stat[:, 0:NB], "row_mean", 2, "row_root")

            def ffn(s):
                for b in range(NB):
                    act.wait_ge(sig("gu_made"), 2 * s.n + b + 1)
                    act.activation(gated[:, s.par, b, :], ps[:, 2 * s.par + b, 0:FC], ACT.Silu).then_inc(sig("gate_ready"), 1)
                act.wait_ge(sig("gated_turned"), s.n + 1)
                act.activation(gatedT[:, s.par].rearrange("p b f n -> p b (f n)"), ps[:, 2 * s.par:2 * s.par + 2, 0:FC], ACT.Copy)\
                   .then_inc(sig("gatedT_ready"), 1)

            ffn(Step(0))
            with act.Fori(0, (N_FC - 1) // 2) as i:
                for parity in range(2):
                    ffn(Step(i=i, parity=parity))
            root(stat[:, 0:NB], "row_mean", 3, "row_root")
            root(stat[:, 0:NB], "row_mean", 4, "row_root")
            act.wait_ge(sig("u2_padded"), 1)
            for pr in range(6):
                act.wait_ge(sig("u2_projected"), pr + 1)
                act.activation(u2[:, 2 * pr:2 * pr + 2, 1:T + 1], ps[:, 4 + pr % 4, :].rearrange("p (c t) -> p c t", t=T),
                               ACT.Copy).then_inc(sig("u2_out"), 1)
            for b in range(NB):
                act.wait_ge(sig("four_projected"), since("four_projected", b + 1))
                act.activation(u_four[:, b, :], ps[:, b, :], ACT.Copy).then_inc(sig("four_ready"), 1)
            for ct in range(NHT):
                act.wait_ge(sig("four1_made"), since("four1_made", ct + 1))
                act.activation(four1[:, ct, :], ps[:, ct, :], ACT.Copy).then_inc(sig("four1_ready"), 1)
            for b in range(NB):
                act.wait_ge(sig("z_turned"), since("z_turned", b + 1))
                act.activation(z_tok[:, b, :], ps[:, 4 + b, :], ACT.Copy).then_inc(sig("z_tok_ready"), 1)
            act.wait_ge(sig("four2_made"), since("four2_made", 1))
            act.activation(y_fo, ps[:, 6:8, :].rearrange("p b (c t) -> p (b c) t", t=T), ACT.Copy).then_inc(sig("y_fo_ready"), 1)
            for f in range(4):
                act.wait_ge(sig("zF_made"), since("zF_made", f + 1))
                act.activation(zF[:, f, :], ps[:, f, :], ACT.Copy).then_inc(sig("zF_ready"), 1)
            act.wait_ge(sig("y_fo_ready"), since("y_fo_ready", 1))
            act.activation(y_sq[1], y_fo.rearrange("p c t -> p (c t)"), ACT.Square)
            act.wait_ge(sig("y_hy_ready"), since("y_hy_ready", 1))
            act.activation(y_sq[0], y_hy.rearrange("p c t -> p (c t)"), ACT.Square).then_inc(sig("y_squared"), 2)
            act.wait_ge(sig("y_mean"), since("y_mean", 1))
            act.activation(y_rs, y_rs, ACT.Sqrt).then_inc(sig("y_root"), 1)
            root(stat[:, 0:NB], "row_mean", 5, "row_root")
            act.wait_ge(sig("ex_ready"), since("ex_ready", 1))
            act.activation(ex, ex, ACT.Exp).then_inc(sig("ex_out"), 1)

            def part_g(par, n):
                act.wait_ge(sig("item_gu_made"), n + 1)
                act.activation(part_gu[par][:, 0:DE], ps[:, 1, :], ACT.Copy).then_inc(sig("part_g_ready"), 1)

            def silu_and_down(n):
                act.wait_ge(sig("added"), n + 1)
                act.activation(silu_g, ps[:, 3, 0:P], ACT.Silu).then_inc(sig("silu_g_ready"), 1)
                act.wait_ge(sig("item_down_made"), n + 1)
                act.activation(part_d[:, 0:BANK], ps[:, 1, :], ACT.Copy).then_inc(sig("part_d_scalar"), 1)

            part_g(0, 0)
            part_g(1, 1)
            silu_and_down(0)
            with act.Fori(0, N_EXP // 2 - 1) as i:
                for par in (1, 0):
                    n = 2 * i + 2 - par
                    part_g(1 - par, n + 1)
                    silu_and_down(n)
            silu_and_down(N_EXP - 1)
            act.wait_ge(sig("table_ready"), since("table_ready", 1))
            n_over = act.value_load(table_i[0:1, 16:17], min_val=0, max_val=16)
            with act.If(n_over > 0):
                with act.Fori(0, n_over) as i:
                    act.wait_ge(sig("over_tensor"), 5 * i + 3)
                    act.activation(silu_g, ps[:, 3, 0:P], ACT.Silu).then_inc(sig("over_scalar"), 1)
            root(stat[:, 0:NB], "row_mean", 6, "row_root")

        @block.vector
        def _(dve):
            link = chain(dve, "dve_chain")

            rows_scaled = [0]

            def row_scales(src, junk, ready=None):
                for b in range(NB):
                    if ready:
                        dve.wait_ge(sig(ready[0]), ready[1] + b)
                    link(dve.tensor_tensor_reduce(junk, src[:, b, :], src[:, b, :], 1.0, 0.0, ALU.mult, ALU.add, stat[:, b:b + 1]))
                dve.tensor_scalar(stat[:, 0:NB], stat[:, 0:NB], 1.0 / D, EPS, ALU.mult, ALU.add).then_inc(sig("row_mean"), 1)
                rows_scaled[0] += 1
                dve.wait_ge(sig("row_root"), rows_scaled[0])
                link(dve.reciprocal(stat[:, 0:NB], stat[:, 0:NB]))

            def turned_out(first, signal_in, signal_out, gains):
                for n in range(4):
                    b, half = n // 2, n % 2
                    dve.wait_ge(sig(signal_in), since(signal_in, n + 1))
                    dve.tensor_tensor(hT[:, 4 * half:4 * half + 4, b * P:(b + 1) * P],
                                      ps[:, n, :].rearrange("p (k t) -> p k t", t=P),
                                      spread(cols[:, gains + 4 * half:gains + 4 * half + 4], 2, P), ALU.mult)\
                       .then_inc(sig(signal_out), 1)

            dve.wait_ge(sig("x_loaded"), 16)
            row_scales(x, merge[:, 0, 1, :])
            for b in range(NB):
                dve.tensor_scalar(merge[:, b, 0, :], x[:, b, :], stat[:, b:b + 1], None, ALU.mult).then_inc(sig("x_normed"), 1)
            dve.wait_ge(sig("const_loaded"), 32)
            turned_out(0, "x_turned", "h_ready", C_MIX)

            dve.wait_ge(sig("qkv_out"), 6)
            for k in range(TAPS):
                for ct in range(CT):
                    tap = cols[:, C_CONV + k * CT + ct:C_CONV + k * CT + ct + 1]
                    src = raw[:, ct, k:k + T]
                    if k == 0:
                        ins = dve.tensor_scalar(convT[:, ct, :], src, tap, None, ALU.mult)
                    else:
                        ins = dve.scalar_tensor_tensor(convT[:, ct, :], src, tap, convT[:, ct, :], ALU.mult, ALU.add)
                if k < TAPS - 1:
                    link(ins)
            ins.then_inc(sig("conv_ready"), 1)
            dve.wait_ge(sig("projected_out"), 8)
            dve.wait_ge(sig("rows_loaded"), 16)
            dve.tensor_tensor(sp_y, ctl[:, :, 28:32], spread(rows[:, R_DT:R_DT + 4], 1, NB), ALU.add).then_inc(sig("y_ready"), 1)
            dve.wait_ge(sig("y_ready"), since("y_ready", 1))
            dve.wait_ge(sig("softplus_ready"), since("softplus_ready", 1))
            link(dve.scalar_tensor_tensor(sp_y, sp_y, 0.0, sp_m, ALU.max, ALU.add))
            link(dve.scalar_tensor_tensor(g_tok, sp_y, -1.0, spread(small[:, 64:68], 1, NB), ALU.mult, ALU.mult))
            dve.tensor_copy(g_lhs, spread(g_tok, 3, P)).then_inc(sig("g_spread"), 1)
            beta = ctl[:, :, 24:28]
            dve.tensor_copy(beta_lhs, spread(beta, 3, P)).then_inc(sig("g_spread"), 1)
            dve.wait_ge(sig("gc_ready"), since("gc_ready", 1))
            link(dve.tensor_copy(small[:, 24:40], ps[:, 0, 0:16]))
            dve.tensor_tensor(e_last, gl, gc, ALU.subtract).then_inc(sig("gc_out"), 1)
            dve.wait_ge(sig("exp_gc_ready"), since("exp_gc_ready", 1))
            for b in range(NB):
                for h in range(H_GDN):
                    ins = dve.tensor_scalar(decayT[:, b, h, :], pair(4)[:, b, h, :], gc[:, b, h:h + 1], 0.0,
                                            ALU.subtract, ALU.min)
            ins.then_inc(sig("gc_out"), 1)
            dve.wait_ge(sig("nsa_const_loaded"), 48)
            dve.wait_ge(sig("projected_out"), 8)
            tmp = [own[:, 4:6, :].rearrange("p u n -> p (u n)")[:, 320 * n:320 * n + 320]
                   .rearrange("p (b h d) -> p b h d", b=NB, h=N_HEADS64) for n in range(4)]
            for b in range(NB):
                x1, x2 = nsa[:, b, :, 0:ROPE_HALF], nsa[:, b, :, ROPE_HALF:2 * ROPE_HALF]
                dve.tensor_tensor(tmp[0][:, b], x1, rope[:, 0, b], ALU.mult)
                dve.tensor_tensor(tmp[1][:, b], x2, rope[:, 1, b], ALU.mult)
                dve.tensor_tensor(tmp[2][:, b], x2, rope[:, 0, b], ALU.mult)
                link(dve.tensor_tensor(tmp[3][:, b], x1, rope[:, 1, b], ALU.mult))
                dve.tensor_tensor(x1, tmp[0][:, b], tmp[1][:, b], ALU.subtract)
                ins = dve.tensor_tensor(x2, tmp[2][:, b], tmp[3][:, b], ALU.add)
            ins.then_inc(sig("roped"), 1)
            dve.wait_ge(sig("qk_squared"), since("qk_squared", 1))
            dve.tensor_tensor(kbT, kT, pair(6), ALU.mult).then_inc(sig("beta_used"), 1)
            dve.wait_ge(sig("qk_summed"), since("qk_summed", 1))
            sums = ps[:, 4:8, :].rearrange("p u (c t) -> p (u c) t", t=T)
            rs = own[:, 4:6, :].rearrange("p u (c t) -> p (u c) t", t=T)
            dve.tensor_scalar(rs, sums, EPS, None, ALU.add).then_inc(sig("sums_out"), 1)
            dve.wait_ge(sig("norms_ready"), since("norms_ready", 1))
            link(dve.reciprocal(rs, rs))
            dve.wait_ge(sig("beta_used"), since("beta_used", 1))
            link(dve.scalar_tensor_tensor(convT[:, 0:4, :], convT[:, 0:4, :], float(DH_GDN) ** -0.5, rs[:, 0:4, :], ALU.mult, ALU.mult))
            link(dve.tensor_tensor(convT[:, 4:8, :], convT[:, 4:8, :], rs[:, 4:8, :], ALU.mult))
            rk = own[:, 5, :].rearrange("p (h b t) -> p b h t", h=H_GDN, b=NB)
            dve.tensor_tensor(kbT, kbT, rk, ALU.mult).then_inc(sig("kb_ready"), 1)
            dve.wait_ge(sig("decays_ready"), since("decays_ready", 1))
            dve.wait_ge(sig("qk_summed"), since("qk_summed", 1))
            dve.tensor_tensor(qgT, qT, exp_gc, ALU.mult)
            flat = lambda u: u.rearrange("p b h n -> p (b h) n")
            link(dve.tensor_tensor(flat(decayT), flat(decayT), spread(sq(CUM), 1, NB * H_GDN), ALU.mult))
            link(dve.tensor_tensor(flat(decay_strict), flat(decayT), spread(sq(STRICT), 1, NB * H_GDN), ALU.mult))
            dve.wait_ge(sig("kk_ready"), since("kk_ready", 1))
            dve.tensor_tensor(aT, pair(4), decay_strict, ALU.mult).then_inc(sig("a_ready"), 1)
            dve.tensor_tensor(qk_decay, pair(6), decayT, ALU.mult).then_inc(sig("qk_ready"), 1)
            link(dve.tensor_tensor(beta_g, beta_g, beta, ALU.mult))
            dve.wait_ge(sig("kv_turned"), since("kv_turned", 1))
            for b in range(NB):
                dve.tensor_tensor(kbg[:, b], pair(4)[:, b], spread(beta_g[:, b], 2, P), ALU.mult)
                dve.tensor_tensor(kd[:, b], pair(4)[:, b], spread(e_last[:, b], 2, P), ALU.mult)
            dve.wait_ge(sig("kv_turned"), since("kv_turned", 2))
            for b in range(NB):
                ins = dve.tensor_tensor(vb[:, b], pair(6)[:, b], spread(beta[:, b], 2, P), ALU.mult)
            ins.then_inc(sig("kd_ready"), 1)
            dve.wait_ge(sig("a_ready"), since("a_ready", 1))
            dve.wait_ge(sig("inverse_started"), 2)
            for n in range(N_LEVEL):
                dve.tensor_tensor(flat(off), flat(aT), spread(sq(LEVEL0 + n), 1, NB * H_GDN), ALU.mult).then_inc(sig("off_ready"), 1)
                dve.wait_ge(sig("step_made"), n + 1)
                dve.tensor_tensor(inv, inv, pair(2), ALU.subtract)
                dve.tensor_tensor(invT, invT, pair(4), ALU.subtract).then_inc(sig("inverse_ready"), 1)
                dve.wait_ge(sig("inverse_ready"), n + 1)
            for c in range(N_CHUNK):
                b, r = c // 2, slice(CHUNK * (c % 2), CHUNK * (c % 2) + CHUNK)
                if c == 0:
                    dve.wait_ge(sig("uw_ready"), 1)
                    dve.tensor_copy(vnew[r, b], uu[r, b]).then_inc(sig("vnew_ready"), 1)
                else:
                    dve.wait_ge(sig("ws_made"), c)
                    dve.tensor_tensor(vnew[r, b], uu[r, b], ps[r, 4, :].rearrange("p (h n) -> p h n", h=H_GDN),
                                      ALU.subtract).then_inc(sig("vnew_ready"), 1)
                if c < N_CHUNK - 1:
                    dve.wait_ge(sig("kv_made"), c + 1)
                    if c >= 1:
                        dve.wait_ge(sig("o_made"), c)
                    for h in range(H_GDN):
                        new, add = state[:, (c + 1) % 2, h, :], ps[:, 5, h * P:(h + 1) * P]
                        if c == 0:
                            ins = dve.tensor_copy(new, add)
                        else:
                            last = exp_gc[:, b, h, r.stop - 1:r.stop]
                            ins = dve.scalar_tensor_tensor(new, state[:, c % 2, h, :], last, add, ALU.mult, ALU.add)
                    ins.then_inc(sig("state_ready"), 1)
                    dve.wait_ge(sig("state_ready"), c + 1)
            dve.wait_ge(sig("o_squared"), 1)
            link(dve.tensor_reduce(o_ss, o_sq, AX_X, ALU.add))
            dve.tensor_scalar(o_ss, o_ss, 1.0 / DH_GDN, EPS, ALU.mult, ALU.add).then_inc(sig("o_mean"), 1)
            dve.wait_ge(sig("o_root"), 1)
            link(dve.reciprocal(o_ss, o_ss))
            link(dve.tensor_tensor(o_gdn, o_gdn, spread(o_ss, 3, P), ALU.mult))
            link(dve.tensor_tensor(flat(o_gdn), flat(o_gdn), spread(rows[:, R_ONORM:R_ONORM + P], 1, NB * H_GDN), ALU.mult))
            dve.tensor_tensor(o_gdn, o_gdn, silu_z.rearrange("p b (h n) -> p b h n", h=H_GDN), ALU.mult).then_inc(sig("o_normed"), 1)

            dve.wait_ge(sig("pairs_made"), since("pairs_made", 1))
            made = ps[:, 3, :].rearrange("p (s g n a) -> p s g n a", s=2, g=NSA_G, a=CMP_A // 2)
            for s in range(2):
                for ah in range(2):
                    pos = cols[:, C_POS + s * CMP_A + 8 * ah:C_POS + s * CMP_A + 8 * ah + 8]
                    ins = dve.tensor_tensor(pairs[:, s, 8 * ah:8 * ah + 8, :, :].rearrange("p a g n -> p g n a"),
                                            made[:, s, :, ah:ah + N_CMP, :], spread(spread(pos, 1, N_CMP), 1, NSA_G), ALU.add)
            ins.then_inc(sig("pairs_ready"), 1)
            dve.wait_ge(sig("o_normed"), 1)
            dve.memset(own[:, 5, 0:64], 0.0).then_inc(sig("hid_zeroed"), 1)
            dve.wait_ge(sig("hid_ready"), since("hid_ready", 2))
            dve.tensor_copy(hid_rep, spread(hid[:, 1, :, :], 2, NSA_R)).then_inc(sig("hid_rep_ready"), 1)
            dve.wait_ge(sig("kv_cmp_made"), since("kv_cmp_made", 1))
            dve.tensor_copy(kcT, ps[:, 4, 64:80])
            dve.tensor_tensor(v_cmp, spread(ps[:, 4, 128:192], 1, NSA_H), spread(cols[:, C_BLK:C_BLK + NSA_H], 2, NSA_D), ALU.mult)\
               .then_inc(sig("kv_cmp_ready"), 1)
            mx, total = soft[:, 64:72], soft[:, 72:80]
            gates = lambda b, kind: ctl[:, b, 0:24].rearrange("p (h k) -> p h k", k=3)[:, :, kind]
            for b in range(NB):
                dve.wait_ge(sig("s_cmp_made"), b + 1)
                for g in range(NSA_G):
                    ins = dve.tensor_tensor(p_cmp[:, g * NSA_R:(g + 1) * NSA_R, :],
                                            ps[:, 5 + g, 0:NSA_R * CMP_STRIDE].rearrange("p (h n) -> p h n", n=CMP_STRIDE),
                                            spread(vis[:, 1, b, :], 1, NSA_R), ALU.add)
                link(ins)
                link(dve.tensor_reduce(mx, p_cmp, AX_X, ALU.max))
                dve.tensor_tensor(p_cmp, p_cmp, spread(mx, 2, CMP_STRIDE), ALU.subtract).then_inc(sig("s_cmp_ready"), 1)
                dve.wait_ge(sig("exp_cmp_ready"), b + 1)
                link(dve.tensor_reduce(total, p_cmp, AX_X, ALU.add))
                dve.tensor_tensor(p_cmp, p_cmp, spread(vis[:, 0, b, :], 1, NSA_H), ALU.mult).then_inc(sig("p_cmp_ready"), 1)
                link(dve.reciprocal(total, total))
                link(dve.tensor_tensor(total, total, gates(b, 0), ALU.mult))
                dve.wait_ge(sig("o_cmp_made"), b + 1)
                dve.tensor_tensor(o_nsa[:, b, :].rearrange("p (h d) -> p h d", d=NSA_D),
                                  ps[:, 4, :].rearrange("p (h d) -> p h d", d=NSA_D), spread(total, 2, NSA_D), ALU.mult)\
                   .then_inc(sig("o_cmp_out"), 1)

            def job_out(j):
                b, s = JOBS[j]
                total = soft[:, 32 + 8 * j:40 + 8 * j]
                dve.wait_ge(sig("o_job_made"), j + 1)
                link(dve.reciprocal(total, total))
                link(dve.tensor_tensor(total, total, gates(b, 1 + s), ALU.mult))
                part = o_part.rearrange("p (h d) -> p h d", d=NSA_D)
                dve.tensor_tensor(part, ps[:, 6, :].rearrange("p (h d) -> p h d", d=NSA_D), spread(total, 2, NSA_D), ALU.mult)\
                   .then_inc(sig("o_job_out"), 1)
                dve.wait_ge(sig("o_job_out"), j + 1)
                ins = dve.tensor_tensor(o_nsa[:, b, :], o_nsa[:, b, :], o_part, ALU.add)
                if s:
                    ins.then_inc(sig("o_nsa_ready"), 1)
                    dve.wait_ge(sig("o_nsa_ready"), b + 1)
                else:
                    link(ins)

            for j, (b, s) in enumerate(JOBS):
                nk = (b + 1) * P
                width = NSA_H * nk
                p = probs[j % 2][:, 0:width].rearrange("p (h n) -> p h n", n=nk)
                got = ps[:, 0:width // BANK, :].rearrange("p b (h n) -> p (b h) n", n=nk)
                dve.wait_ge(sig("scores_made"), j + 1)
                if b:
                    dve.tensor_copy(p[:, :, 0:P], got[:, :, 0:P])
                dve.tensor_tensor(p[:, :, nk - P:nk], got[:, :, nk - P:nk], spread(sq(CAUSAL), 1, NSA_H), ALU.add)\
                   .then_inc(sig("scores_out"), 1)
                dve.wait_ge(sig("scores_out"), j + 1)
                link(dve.tensor_reduce(soft[:, 8 * j:8 * j + 8], p, AX_X, ALU.max))
                dve.tensor_scalar(soft[:, 8 * j:8 * j + 8], soft[:, 8 * j:8 * j + 8], -float(NSA_D) ** -0.5, None, ALU.mult)\
                   .then_inc(sig("maxima_ready"), 1)
                if j:
                    job_out(j - 1)
            job_out(len(JOBS) - 1)
            halves = lambda n: ps[:, n:n + 2, :].rearrange("p h n -> p (h n)")
            dve.wait_ge(sig("branch_made"), 2)
            for b in range(NB):
                link(dve.tensor_tensor(merge[:, b, 0, :], merge[:, b, 0, :], halves(4 * b), ALU.mult))
                link(dve.tensor_tensor(merge[:, b, 1, :], merge[:, b, 1, :], halves(4 * b + 2), ALU.mult))
                dve.tensor_tensor(merge[:, b, 0, :], merge[:, b, 0, :], merge[:, b, 1, :], ALU.add).then_inc(sig("merged"), 1)
            dve.wait_ge(sig("w_out_made"), 2)
            for b in range(NB):
                link(dve.tensor_tensor(x[:, b, :], x[:, b, :], halves(4 + 2 * b), ALU.add))
            dve.sem_inc(sig("x2_added"), 1)
            for n in range(3):
                dve.wait_ge(sig("filt_layer"), since("filt_layer", n + 1))
                link(dve.tensor_scalar(arg, ps[0:64, 0, 0:T], cols[0:64, C_FB + n:C_FB + n + 1], cols[0:64, C_FREQ + n:C_FREQ + n + 1],
                                       ALU.add, ALU.mult))
                link(dve.tensor_scalar(turns_, arg, 1.0 / TWO_PI, ROUND_MAGIC, ALU.mult, ALU.add))
                link(dve.tensor_scalar(turns_, turns_, ROUND_MAGIC, None, ALU.subtract))
                for part in (TWO_PI_HI, TWO_PI_MID, TWO_PI_LO):
                    link(dve.scalar_tensor_tensor(arg, turns_, -part, arg, ALU.mult, ALU.add))
                dve.tensor_scalar(arg, arg, 3.1415925, -3.1415925, ALU.min, ALU.max).then_inc(sig("arg_ready"), 1)
                dve.wait_ge(sig("arg_ready"), since("arg_ready", n + 1))
            dve.wait_ge(sig("filt_out_made"), since("filt_out_made", 1))
            dve.tensor_tensor(kern.rearrange("p b d n -> p b d n"), ps[:, 0:4, :].rearrange("p (b d) n -> p b d n", d=2),
                              spread(decay2, 2, 2), ALU.mult).then_inc(sig("kern_ready"), 1)
            dve.wait_ge(sig("filter_turned"), since("filter_turned", 1))
            dve.reciprocal(filt_norm, ps[:, 4, 0:NHT]).then_inc(sig("filt_norm_ready"), 1)
            dve.wait_ge(sig("merged"), 2)
            row_scales(x, merge[:, 0, 1, :])
            dve.wait_ge(sig("merge_turned"), since("merge_turned", 4))
            for b in range(NB):
                dve.tensor_scalar(merge[:, b, 0, :], x[:, b, :], stat[:, b:b + 1], None, ALU.mult).then_inc(sig("x2_normed"), 1)
            turned_out(0, "x2_turned", "h2_ready", C_FFN)

            def ffn(s):
                for b in range(NB):
                    dve.wait_ge(sig("gate_ready"), 2 * s.n + b + 1)
                    ins = dve.tensor_tensor(gated[:, s.par, b, :], gated[:, s.par, b, :], ps[:, 2 * s.par + b, FC:2 * FC], ALU.mult)
                ins.then_inc(sig("gated_ready"), 1)

            ffn(Step(0))
            with dve.Fori(0, (N_FC - 1) // 2) as i:
                for parity in range(2):
                    ffn(Step(i=i, parity=parity))
            dve.wait_ge(sig("down_made"), N_FC)
            for b in range(NB):
                link(dve.tensor_tensor(x[:, b, :], x[:, b, :], halves(4 + 2 * b), ALU.add))
            row_scales(x, merge[:, 0, 1, :])
            for b in range(NB):
                link(dve.scalar_tensor_tensor(x[:, b, :], x[:, b, :], stat[:, b:b + 1], rows[:, R_FIN1:R_FIN1 + D], ALU.mult, ALU.mult))
            row_scales(x, merge[:, 0, 1, :])
            for b in range(NB):
                dve.tensor_scalar(merge[:, b, 0, :], x[:, b, :], stat[:, b:b + 1], None, ALU.mult).then_inc(sig("x3_normed"), 1)
            turned_out(0, "x3_turned", "h3_ready", C_N1)
            dve.wait_ge(sig("u2_out"), 6)
            for k in range(3):
                for ct in range(CT):
                    tap = cols[:, C_CONV2 + k * CT + ct:C_CONV2 + k * CT + ct + 1]
                    if k == 0:
                        ins = dve.tensor_scalar(conv2[:, ct, :], u2[:, ct, 0:T], tap, cols[:, C_CONVB2 + ct:C_CONVB2 + ct + 1],
                                                ALU.mult, ALU.add)
                    else:
                        ins = dve.scalar_tensor_tensor(conv2[:, ct, :], u2[:, ct, k:k + T], tap, conv2[:, ct, :], ALU.mult, ALU.add)
                link(ins)
            dve.tensor_tensor(zT, zT, conv2[:, 2 * NHT:3 * NHT, :], ALU.mult).then_inc(sig("z_ready"), 1)
            dve.wait_ge(sig("zF_ready"), since("zF_ready", 4))
            re, im = slice(0, 2), slice(2, 4)
            dve.tensor_tensor(cross, zF[:, im, :], kernF[:, im, :], ALU.mult)
            link(dve.tensor_tensor(prodF[:, re, :], zF[:, re, :], kernF[:, re, :], ALU.mult))
            link(dve.tensor_tensor(prodF[:, re, :], prodF[:, re, :], cross, ALU.subtract))
            dve.tensor_tensor(cross, zF[:, im, :], kernF[:, re, :], ALU.mult)
            link(dve.tensor_tensor(prodF[:, im, :], zF[:, re, :], kernF[:, im, :], ALU.mult))
            dve.tensor_tensor(prodF[:, im, :], prodF[:, im, :], cross, ALU.add).then_inc(sig("prod_ready"), 1)
            dve.wait_ge(sig("conv_made"), since("conv_made", 1))
            for ct in range(NHT):
                ins = dve.tensor_scalar(y_hy[:, ct, :], ps[:, 4 + ct // 2, (ct % 2) * T:(ct % 2 + 1) * T], filt_norm[:, ct:ct + 1],
                                        None, ALU.mult)
            link(ins)
            for ct in range(NHT):
                ins = dve.scalar_tensor_tensor(y_hy[:, ct, :], zT[:, ct, :], cols[:, C_FBIAS + ct:C_FBIAS + ct + 1], y_hy[:, ct, :],
                                               ALU.mult, ALU.add)
            link(ins)
            dve.tensor_tensor(y_hy, y_hy, conv2[:, 0:NHT, :], ALU.mult).then_inc(sig("y_hy_ready"), 1)
            dve.wait_ge(sig("y_summed"), since("y_summed", 1))
            dve.tensor_scalar(y_rs, ps[:, 0:4, :].rearrange("p f n -> p (f n)"), 1.0 / NSA_D, EPS, ALU.mult, ALU.add).then_inc(sig("y_mean"), 1)
            dve.wait_ge(sig("y_root"), since("y_root", 1))
            link(dve.reciprocal(y_rs, y_rs))
            for n, y in enumerate((y_hy, y_fo)):
                for ct in range(NHT):
                    gain = cols[:, C_MIXG + n * NHT + ct:C_MIXG + n * NHT + ct + 1]
                    ins = dve.scalar_tensor_tensor(y[:, ct, :], y[:, ct, :], gain, y_rs[:, (n * NHT + ct) * T:(n * NHT + ct + 1) * T],
                                                   ALU.mult, ALU.mult)
                ins.then_inc(sig("y_ready2"), 1)
            dve.wait_ge(sig("out2_made"), since("out2_made", 1))
            for b in range(NB):
                ins = dve.tensor_tensor(x[:, b, :], x[:, b, :], halves(4 + 2 * b), ALU.add)
            link(ins)
            row_scales(x, merge[:, 0, 1, :])
            for b in range(NB):
                dve.tensor_scalar(merge[:, b, 0, :], x[:, b, :], stat[:, b:b + 1], None, ALU.mult).then_inc(sig("x4_normed"), 1)
            turned_out(0, "x4_turned", "h4_ready", C_N2)
            dve.memset(zero, 0.0).then_inc(sig("zero_ready"), 1)

            def first_best(values, n, tmp, out):
                big = spread(rows[:, R_BIG:R_BIG + n], 1, NB)
                wide = lambda v: v.broadcast_to([P, NB, n])
                link(dve.tensor_reduce(best, values, AX_X, ALU.max))
                link(dve.tensor_tensor(tmp, values, wide(best), ALU.is_equal))
                link(dve.tensor_tensor(tmp, tmp, big, ALU.mult))
                link(dve.tensor_reduce(first, tmp, AX_X, ALU.min))
                link(dve.tensor_tensor(out, big, wide(first), ALU.is_equal))

            dve.wait_ge(sig("logits_made"), since("logits_made", 1))
            n = N_GRP + N_EXP
            link(dve.tensor_tensor(logits, ps[:, 4, 0:NB * n].rearrange("p (b e) -> p b e", b=NB),
                                   spread(rows[:, R_BIAS:R_BIAS + n], 1, NB), ALU.add))
            first_best(l_grp, N_GRP, eq4, one_grp)
            link(dve.tensor_tensor(ex[:, :, 0:N_GRP], l_grp, best.broadcast_to([P, NB, N_GRP]), ALU.subtract))
            in_group = lambda b: spread(one_grp[:, b, :], 2, EPG)
            by_group = lambda v, b: v[:, b, :].rearrange("p (g e) -> p g e", e=EPG)
            link(dve.tensor_scalar(eq4, one_grp, -1.0, -NEG, ALU.add, ALU.mult))
            for b in range(NB):
                link(dve.tensor_tensor(by_group(l_exp, b), by_group(l_exp, b), in_group(b), ALU.mult))
                link(dve.tensor_tensor(by_group(l_exp, b), by_group(l_exp, b), spread(eq4[:, b, :], 2, EPG), ALU.add))
            first_best(l_exp, N_EXP, eq, one1)
            link(dve.tensor_copy(second, best))
            link(dve.scalar_tensor_tensor(l_exp, one1, 2 * NEG, l_exp, ALU.mult, ALU.add))
            first_best(l_exp, N_EXP, eq, one2)
            dve.tensor_tensor(chosen, one1, one2, ALU.add).then_inc(sig("chosen_ready"), 1)
            dve.tensor_tensor(ex[:, :, N_GRP:N_GRP + 1], best, second, ALU.subtract).then_inc(sig("ex_ready"), 1)
            dve.wait_ge(sig("ex_out"), 1)
            link(dve.tensor_reduce(best, ex[:, :, 0:N_GRP], AX_X, ALU.add))
            link(dve.scalar_tensor_tensor(first, ex[:, :, N_GRP:N_GRP + 1], 1.0, best, ALU.add, ALU.mult))
            w1 = weights[:, 0:NB].rearrange("p (b e) -> p b e", e=1)
            w2 = weights[:, NB:2 * NB].rearrange("p (b e) -> p b e", e=1)
            link(dve.reciprocal(w1, first))
            link(dve.tensor_tensor(w2, w1, ex[:, :, N_GRP:N_GRP + 1], ALU.mult))
            dve.wait_ge(sig("ranks_made"), since("ranks_made", 1))
            link(dve.tensor_scalar(counts, ps[:, 3, 64:96], 1.0 / CAP, None, ALU.mult))
            link(dve.tensor_tensor(steps, spread(counts, 2, 7), spread(rows[:, R_IOTA + 1:R_IOTA + 8], 1, N_EXP), ALU.is_gt))
            link(dve.tensor_reduce(more, steps, AX_X, ALU.add))
            link(dve.tensor_copy(over_ends[0], more))
            for k in range(5):
                a, b, s = over_ends[k % 2], over_ends[(k + 1) % 2], 1 << k
                dve.tensor_copy(b[:, 0:s], a[:, 0:s])
                link(dve.tensor_tensor(b[:, s:], a[:, s:], a[:, 0:N_EXP - s], ALU.add))
            ends = over_ends[1]
            iota = rows[:, R_IOTA:R_IOTA + N_EXP]
            link(dve.tensor_tensor(base, ends, more, ALU.subtract))
            link(dve.tensor_tensor(base, base, iota, ALU.subtract))
            link(dve.tensor_scalar(base, base, float(CAP), float(CAP * (N_EXP - 1)), ALU.mult, ALU.add))
            rank = ps[:, 3, 0:64].rearrange("p (b e) -> p b e", b=NB)
            link(dve.tensor_scalar(shift, rank, float(CAP), None, ALU.is_ge))
            link(dve.tensor_tensor(shift, shift, spread(base, 1, NB), ALU.mult))
            link(dve.tensor_tensor(slot_of, rank, shift, ALU.add))
            link(dve.tensor_scalar(base, iota, float(CAP), None, ALU.mult))
            link(dve.tensor_tensor(slot_of, slot_of, spread(base, 1, NB), ALU.add))
            for n, one in enumerate((one1, one2)):
                link(dve.tensor_tensor(eq, one, slot_of, ALU.mult))
                link(dve.tensor_reduce(slots_of[:, n * NB:(n + 1) * NB], eq, AX_X, ALU.add))
            link(dve.tensor_tensor(table_cmp, spread(ends, 1, 16), spread(rows[:, R_IOTA:R_IOTA + 16], 2, N_EXP), ALU.is_le))
            link(dve.tensor_reduce(table[:, 0:16], table_cmp, AX_X, ALU.add))
            link(dve.tensor_scalar(table[:, 0:16], table[:, 0:16], float(N_EXP - 1), None, ALU.min))
            link(dve.tensor_copy(table[:, 16:17], ends[:, N_EXP - 1:N_EXP]))
            dve.tensor_copy(table_i, table).then_inc(sig("table_ready"), 1)

            def rows_out(par):
                return dve.tensor_tensor(hgT[par], ps[:, 0, 0:256].rearrange("p (k c) -> p k c", c=CAP),
                                         spread(cols[:, C_N2:C_N2 + KT], 2, CAP), ALU.mult)

            def activation_out():
                dve.tensor_copy(pickT.rearrange("p b t -> p (b t)"), ps[:, 3, 256:512])
                return dve.tensor_tensor(actT.rearrange("p f c -> p (f c)"), silu_g, ps[:, 3, P:2 * P], ALU.mult)

            def rows_and_up(par, n):
                dve.wait_ge(sig("gathered"), n + 1)
                rows_out(par).then_inc(sig("hg_ready"), 1)
                dve.wait_ge(sig("item_gu_made"), n + 1)
                dve.tensor_copy(part_gu[par][:, DE:2 * DE], ps[:, 2, :]).then_inc(sig("part_u_ready"), 1)

            def product_and_down(n, next_par=None):
                dve.wait_ge(sig("silu_g_ready"), n + 1)
                activation_out().then_inc(sig("act_ready"), 1)
                if next_par is not None:
                    item_picks(dve, pick_link, next_par).then_inc(sig("picked"), 1)
                dve.wait_ge(sig("item_down_made"), n + 1)
                dve.tensor_copy(part_d[:, BANK:], ps[:, 2, :]).then_inc(sig("part_d_vector"), 1)

            PICK_LINKS = 3 * NB

            class Links:

                def __init__(self):
                    self.n = 0

                def __call__(self, ins):
                    self.n += 1
                    ins.then_inc(sig("pick_chain"), 1)
                    dve.wait_ge(sig("pick_chain"), self.n)

            pick_link = Links()
            item_picks(dve, pick_link, 0).then_inc(sig("picked"), 1)
            dve.wait_ge(sig("picked"), 1)
            item_picks(dve, pick_link, 1).then_inc(sig("picked"), 1)
            rows_and_up(0, 0)
            rows_and_up(1, 1)
            product_and_down(0, 0)
            with dve.Fori(0, N_EXP // 2 - 1) as i:
                pick_link.n = i * (2 * PICK_LINKS) + 3 * PICK_LINKS
                for par in (1, 0):
                    n = 2 * i + 2 - par
                    rows_and_up(1 - par, n + 1)
                    dve.wait_ge(sig("picked"), n + 2)
                    product_and_down(n, par)
            product_and_down(N_EXP - 1)
            dve.wait_ge(sig("scattered"), N_EXP)
            for b in range(NB):
                ins = dve.tensor_tensor(x[:, b, :], x[:, b, :], halves(4 + 2 * b), ALU.add)
            link(ins)
            dve.wait_ge(sig("picked"), N_EXP + 1)
            link(dve.tensor_scalar(slots_of, slots_of, float(CAP), None, ALU.add))
            dve.sem_inc(sig("over_next"), 1)
            n_over = dve.value_load(table_i[0:1, 16:17], min_val=0, max_val=16)
            over_link = Links()
            with dve.If(n_over > 0):
                with dve.Fori(0, n_over) as i:
                    over_link.n = i * PICK_LINKS + (N_EXP + 1) * PICK_LINKS
                    item_picks(dve, over_link, 0).then_inc(sig("over_vector"), 1)
                    dve.wait_ge(sig("over_tensor"), 5 * i + 1)
                    rows_out(0).then_inc(sig("over_vector"), 1)
                    dve.wait_ge(sig("over_tensor"), 5 * i + 2)
                    dve.tensor_copy(part_gu[0], halves(1)).then_inc(sig("over_vector"), 1)
                    dve.wait_ge(sig("over_scalar"), i + 1)
                    activation_out().then_inc(sig("over_vector"), 1)
                    dve.wait_ge(sig("over_tensor"), 5 * i + 4)
                    dve.tensor_copy(part_d, halves(1)).then_inc(sig("over_vector"), 1)
                    dve.wait_ge(sig("over_tensor"), 5 * i + 5)
                    for b in range(NB):
                        ins = dve.tensor_tensor(x[:, b, :], x[:, b, :], halves(4 + 2 * b), ALU.add)
                    ins.then_inc(sig("over_next"), 1)
                    dve.wait_ge(sig("over_next"), i + 2)
            row_scales(x, merge[:, 0, 1, :])
            for b in range(NB):
                dve.scalar_tensor_tensor(merge[:, b, 0, :], x[:, b, :], stat[:, b:b + 1], rows[:, R_FIN2:R_FIN2 + D], ALU.mult, ALU.mult)\
                   .then_inc(sig("out_ready"), 1)


def _constants(np):
    i = np.arange(P)
    sq = np.zeros((N_SQ, P, P), np.float32)
    same = i[:, None] // CHUNK == i[None, :] // CHUNK
    sq[IDENT] = np.eye(P)
    sq[CUM] = same & (i[:, None] <= i[None, :])
    sq[SAME] = same
    sq[STRICT] = same & (i[:, None] < i[None, :])
    for n in range(N_LEVEL):
        b = 1 << n
        sq[LEVEL0 + n] = (i[:, None] // (2 * b) == i[None, :] // (2 * b)) & (i[:, None] // b % 2 == 0) & (i[None, :] // b % 2 == 1)
    sq[ONES] = 1
    d = np.arange(NSA_D)
    ang = 2 * np.pi * np.outer(d, d) / NSA_D
    for j in range(2):
        s = slice(j * NSA_D, (j + 1) * NSA_D)
        sq[DFT_C, s, s] = np.cos(ang)
        sq[DFT_S, s, s] = -np.sin(ang)
    sq[CAUSAL] = np.where(i[None, :] <= i[:, None], 0, NEG)
    sq[RANK] = i[:, None] < i[None, :]
    out = {"squares": sq.transpose(1, 0, 2)}
    t = np.arange(T, dtype=np.float64)
    w = 2 * np.pi * (t + 0.5) / (2 * T)
    wt = np.outer(t, w)
    out["dft_fwd"] = np.concatenate([np.cos(wt), -np.sin(wt)], 1).reshape(NB, P, 2 * T).transpose(1, 0, 2)
    back = np.concatenate([np.cos(wt), np.sin(wt)], 1)
    back[0] = 0
    out["dft_bwd"] = back.reshape(NB, P, 2 * T).transpose(1, 0, 2)
    inv = np.concatenate([np.cos(wt).T, -np.sin(wt).T], 0) / T
    out["dft_inv"] = inv.reshape(2 * NB, P, T).transpose(1, 0, 2)
    wt = 2 * np.pi * np.outer(t, t) / T
    both = np.concatenate([np.cos(wt), np.sin(wt)], 1) / np.sqrt(T * NSA_D)
    out["dft_time"] = both.reshape(NB, P, 2 * T).transpose(1, 0, 2)
    f32 = np.float32
    ts = np.linspace(0, 1, T, dtype=f32)[:, None]
    ww = (f32(2 * np.pi / T) * np.arange(T, dtype=f32))[:, None]
    f = np.linspace(1e-4, 15, 16, dtype=f32)[None]
    out["emb"] = np.concatenate([ts, np.cos(f * ww), -np.sin(f * ww)], 1).T
    lo, hi = np.log(1e-2) / 1.5, np.log(1e-2) / 0.3
    deltas = np.abs(np.linspace(lo, hi, DH2, dtype=f32))
    out["decay"] = np.exp(-ts * deltas).reshape(NB, P, DH2).transpose(1, 0, 2)
    freq = f32(500000.0) ** (-np.arange(ROPE_HALF, dtype=f32) / ROPE_HALF)
    a = np.arange(T, dtype=f32)[:, None] * freq
    rope = np.zeros((2, T, N_HEADS64, ROPE_HALF), f32)
    rope[0] = 1
    for h in list(range(NSA_H)) + [8, 9, 12, 13, 16, 17]:
        rope[0, :, h], rope[1, :, h] = np.cos(a), np.sin(a)
    out["rope"] = rope.reshape(2, NB, P, N_HEADS64, ROPE_HALF).transpose(2, 0, 1, 3, 4)
    vis = np.zeros((T, CMP_STRIDE), f32)
    vis[:, :N_CMP] = np.arange(N_CMP)[None] * CMP_STRIDE + CMP_BLOCK - 1 <= np.arange(T)[:, None]
    add = np.where(vis > 0, 0, NEG)
    add[:, N_CMP:] = 3 * NEG
    out["vis"] = np.stack([vis, add]).reshape(2, NB, P, CMP_STRIDE).transpose(2, 0, 1, 3)
    return {k: np.ascontiguousarray(v, np.float32) for k, v in out.items()}


def _layout(np, x):
    f = lambda n: np.asarray(x[n], np.float32)
    feat = lambda v: v.reshape(-1, P).T
    tiles = lambda w: w.reshape(w.shape[0] // P, P, w.shape[1]).transpose(1, 0, 2)
    w = f("w_in")[0]
    a = 4 * H_GDN * DH_GDN
    ctl = 2 * H_GDN
    kv = a + ctl + (NSA_H + 6 * NSA_G) * NSA_D
    cols = np.concatenate([w[:, :a], w[:, a + ctl:kv], w[:, kv:kv + 3 * NSA_H], w[:, a:a + ctl],
                           np.zeros((D, 224), np.float32), w[:, kv + 3 * NSA_H:]], 1)
    out = {"w_in": cols.reshape(KT, P, -1, BANK).transpose(2, 1, 0, 3)}
    w1 = [f(n)[0].reshape(CMP_A, 2 * NSA_D, P).transpose(1, 0, 2) for n in ("cmp_w1_k", "cmp_w1_v")]
    out["cmp_w1"] = np.stack(w1, 1)
    out["cmp_w2"] = np.stack([f("cmp_w2_k")[0], f("cmp_w2_v")[0]], 1)
    out["w_branch"] = np.stack([tiles(f("w_branch_gdn")[0]), tiles(f("w_branch_nsa")[0])])
    out["w_out"] = f("w_out")[0].reshape(KT, P, 2, BANK).transpose(2, 1, 0, 3)
    gu = f("w_gate_up")[0].reshape(KT, P, 2, N_FC, FC)
    out["w_gu"] = gu.transpose(3, 1, 0, 2, 4)
    out["w_dn"] = f("w_down")[0].reshape(N_FC, FC // P, P, D).transpose(0, 2, 1, 3)
    out["w_in2"] = f("w_in_2")[0].reshape(KT, P, -1, BANK).transpose(2, 1, 0, 3)
    out["w_out2"] = f("w_out_2")[0].reshape(KT, P, 2, BANK).transpose(2, 1, 0, 3)
    pad = lambda v: np.concatenate([v, np.zeros((P - v.shape[0],) + v.shape[1:], np.float32)])
    i = np.arange(P)
    head = (i[:, None] // CMP_STRIDE == np.arange(NSA_H)[None]).astype(np.float32)
    fold = (i[:, None] % CAP == np.arange(CAP)[None]).astype(np.float32)
    pos = [f(n)[0].reshape(CMP_A, P).T for n in ("cmp_pos_k", "cmp_pos_v")]
    one = np.ones((P, 2), np.float32)
    one[0, 1] = 0
    out["cols"] = np.concatenate(
        [feat(f(n)[0]) for n in ("mix_norm_gain", "ffn_norm_gain", "norm1_g_2", "norm2_g_2", "mix_g_2")]
        + [feat(f("gdn_conv_w")[0].reshape(-1)), feat(f("conv_w_2")[0].reshape(-1)), feat(f("conv_b_2")[0]),
           feat(f("f_bias_2")[0]), pad(np.stack([f("f_b_in_2")[0], f("f_b_mid_2")[0, 0], f("f_b_mid_2")[0, 1]], 1)),
           pad(f("f_freq_2")[0].T)] + pos + [one, head, fold], 1)
    row = np.concatenate([f("gdn_a_log")[0], f("gdn_dt_bias")[0], f("gdn_out_norm_gain")[0], f("final_norm_gain"),
                          f("final_g_2"), f("b_group_2")[0], f("b_router_2")[0].reshape(-1),
                          np.arange(64, dtype=np.float32), np.arange(N_EXP, dtype=np.float32) - 1000])
    out["rows"] = np.broadcast_to(row, (P, row.size))
    out["filt_in"] = f("f_w_in_2")[0]
    out["filt_mid"] = f("f_w_mid_2")[0].transpose(1, 0, 2)
    out["filt_out"] = f("f_w_out_2")[0]
    router = np.concatenate([f("w_group_2")[0], f("w_router_2")[0].transpose(1, 0, 2).reshape(D, N_EXP)], 1)
    out["w_route"] = tiles(router)
    gate, up = (f(n)[0].reshape(N_EXP, KT, P, DE).transpose(0, 2, 1, 3) for n in ("w_gate_2", "w_up_2"))
    down = f("w_down_2")[0].reshape(N_EXP, DE // P, P, D).transpose(0, 2, 1, 3)
    out["w_exp"] = np.stack([gate.reshape(N_EXP, P, -1), up.reshape(N_EXP, P, -1), down.reshape(N_EXP, P, -1)], 2)
    out["x"] = f("x")[0].reshape(NB, P, D).transpose(1, 0, 2)
    return {k: np.ascontiguousarray(v, np.float32) for k, v in out.items()}


def kernel(**inputs):
    import numpy as np
    import concourse.bacc as bacc
    from concourse.bass_utils import run_bass_kernel_spmd as run

    arrays = {**_constants(np), **_layout(np, inputs)}
    nc = bacc.Bacc("TRN2", target_bir_lowering=False, num_devices=1)
    dram = {k: nc.dram_tensor(k, a.shape, F32, kind="ExternalInput").ap() for k, a in arrays.items()}
    dram["out"] = nc.dram_tensor("out", (P, NB, D), F32, kind="ExternalOutput").ap()
    two_layer_program(nc, dram)
    r = run(nc, [arrays], core_ids=[0])
    return r.results[0]["out"].transpose(1, 0, 2).reshape(1, T, D)
```

```python
from contextlib import ExitStack

import concourse.bass as bass
from concourse import mybir

F32 = mybir.dt.float32
I32 = mybir.dt.int32
ALU = mybir.AluOpType
ACT = mybir.ActivationFunctionType
AX_X = mybir.AxisListType.X

P = 128
T = 256
NB = T // P
D = 1024
KT = D // P
H_GDN, DH_GDN = 4, 128
CHUNK = 64
N_CHUNK = T // CHUNK
QKV = 3 * H_GDN * DH_GDN
CT = QKV // P
TAPS = 4
NSA_H, NSA_G, NSA_D = 8, 2, 64
NSA_R = NSA_H // NSA_G
ROPE_HALF = NSA_D // 8
N_HEADS64 = NSA_H + 6 * NSA_G
CMP_BLOCK, CMP_STRIDE = 32, 16
N_CMP = (T - CMP_BLOCK) // CMP_STRIDE + 1
CMP_A = CMP_BLOCK // 2
FFN = 2816
FC = 256
N_FC = FFN // FC
DH2 = 512
NHT = DH2 // P
N_EXP, N_GRP, EPG = 32, 4, 8
DE = 512
CAP = 32
MAX_ITEMS = 2 * T // CAP + N_EXP
EPS = 1e-6
NEG = -1e30
SLOTS = 6
BANK = 512
TWO_PI = 6.283185307179586
ROUND_MAGIC = 12582912.0
TWO_PI_HI, TWO_PI_MID = 6.28125, 0.0019350051879882812
TWO_PI_LO = TWO_PI - TWO_PI_HI - TWO_PI_MID

(IDENT, CUM, SAME, STRICT, LEVEL0) = range(5)
N_LEVEL = 6
ONES = LEVEL0 + N_LEVEL
DFT_C, DFT_S, CAUSAL, RANK = range(ONES + 1, ONES + 5)
N_SQ = RANK + 1
C_MIX, C_FFN, C_N1, C_N2, C_MIXG = 0, 8, 16, 24, 32
C_CONV = 40
C_CONV2 = C_CONV + TAPS * CT
C_CONVB2 = C_CONV2 + 3 * CT
C_FBIAS = C_CONVB2 + CT
C_FB = C_FBIAS + NHT
C_FREQ = C_FB + 3
C_POS = C_FREQ + 3
C_ONE = C_POS + 2 * CMP_A
C_BLK = C_ONE + 2
C_FOLD = C_BLK + NSA_H
N_COLS = C_FOLD + CAP
R_ALOG, R_DT, R_ONORM = 0, 4, 8
R_FIN1 = R_ONORM + DH_GDN
R_FIN2 = R_FIN1 + D
R_BIAS = R_FIN2 + D
R_IOTA = R_BIAS + N_GRP + N_EXP
R_BIG = R_IOTA + 64
N_ROWS = R_BIG + N_EXP


SHARED = {
    "delta_vector": [("conv_ready", 1), ("y_ready", 1), ("g_spread", 2), ("gc_out", 2), ("roped", 1),
        ("beta_used", 1), ("sums_out", 1), ("kb_ready", 1), ("a_ready", 1), ("qk_ready", 1), ("kd_ready", 1)],
    "delta_scalar": [("softplus_ready", 1), ("qk_squared", 1), ("exp_gc_ready", 1), ("decays_ready", 1),
        ("norms_ready", 1)],
    "delta_tensor": [("gc_ready", 1), ("qk_summed", 1), ("kk_ready", 1), ("kv_turned", 2)],
    "rows_normed": [("x_normed", 2), ("x2_normed", 2), ("x3_normed", 2), ("x4_normed", 2)],
    "rows_turned": [("x_turned", 4), ("merge_turned", 4), ("x2_turned", 4), ("x3_turned", 4), ("x4_turned", 4)],
    "rows_ready": [("h_ready", 4), ("h2_ready", 4), ("h3_ready", 4), ("h4_ready", 4)],
    "attn_tensor": [("nq_turned", 2), ("nk_turned", 1), ("pairs_made", 1), ("hid_made", 2), ("kv_cmp_made", 1)],
    "attn_scalar": [("nq_ready", 2), ("nk_ready", 1), ("hid_ready", 2)],
    "attn_vector": [("pairs_ready", 1), ("hid_zeroed", 1), ("hid_rep_ready", 1), ("kv_cmp_ready", 1)],
    "filter_tensor": [("filt_layer", 3), ("filt_out_made", 1), ("kernF_made", 1), ("filter_turned", 1)],
    "filter_scalar": [("filt_sin", 3), ("kern_abs_ready", 1), ("kernF_ready", 1)],
    "filter_vector": [("arg_ready", 3), ("kern_ready", 1), ("filt_norm_ready", 1)],
    "mix_tensor": [("four_projected", 2), ("four1_made", 4), ("z_turned", 2), ("four2_made", 1), ("zF_made", 4),
        ("conv_made", 1), ("y_summed", 1), ("out2_made", 1)],
    "mix_scalar": [("four_ready", 2), ("four1_ready", 4), ("z_tok_ready", 2), ("y_fo_ready", 1), ("zF_ready", 4),
        ("y_squared", 2), ("y_root", 1)],
    "mix_vector": [("z_ready", 1), ("prod_ready", 1), ("y_hy_ready", 1), ("y_mean", 1), ("y_ready2", 2)],
    "route_tensor": [("logits_made", 1), ("ranks_made", 1)],
    "route_vector": [("zero_ready", 1), ("chosen_ready", 1), ("ex_ready", 1), ("table_ready", 1)],
}
PLACE = {stage: (name, sum(n for _, n in stages[:i])) for name, stages in SHARED.items() for i, (stage, _) in enumerate(stages)}


def since(stage, n):
    return PLACE.get(stage, (stage, 0))[1] + n


class Signals:

    def __init__(self, nc, ctx):
        self.nc, self.ctx, self.known = nc, ctx, {}

    def __call__(self, name):
        name = PLACE.get(name, (name, 0))[0]
        if name not in self.known:
            self.known[name] = self.ctx.enter_context(self.nc.semaphore(name))
        return self.known[name]


def spread(ap, axis, n):
    ap = ap.unsqueeze(axis)
    shape = list(ap.shape)
    shape[axis] = n
    return ap.broadcast_to(shape)


def two_layer_program(nc, dram, dump=None):
    with ExitStack() as ctx:
        sig = Signals(nc, ctx)

        def sb(name, *shape, dt=F32):
            return ctx.enter_context(nc.sbuf_tensor("sb_" + name, [P, *shape], dt))[:]

        ps = ctx.enter_context(nc.psum_tensor("ps", [P, 8, BANK], F32))[:]

        ring = sb("ring", SLOTS, 4096)
        squares = sb("squares", N_SQ, P)
        cols = sb("cols", N_COLS)
        rows = sb("rows", N_ROWS)
        x = sb("x", NB, D)
        hT = sb("hT", KT, T)
        stat = sb("stat", 16)
        own = sb("own", 6, 1024)
        raw = sb("raw", CT, T + TAPS - 1)
        silu_z = sb("silu_z", NB, 512)
        nsa = sb("nsa", NB, N_HEADS64, NSA_D)
        merge = sb("merge", NB, 2, D)
        ctl = sb("ctl", NB, 32)
        small = sb("small", 512)

        ring_units = ring[:, 4:6, :].rearrange("p s (u n) -> p (s u) n", n=1024)
        unit = [ring_units[:, u, :] for u in range(8)] + [own[:, u, :] for u in range(6)]
        raw_flat = raw.rearrange("p c t -> p (c t)")

        per_head = lambda u: u.rearrange("p (b h n) -> p b h n", b=NB, h=H_GDN)
        convT = ring_units[:, 0:3, :].rearrange("p u (c t) -> p (u c) t", t=T)
        qkT_sq = raw.rearrange("p c t -> p (c t)")[:, 0:2048].rearrange("p (c t) -> p c t", t=T)
        qT = ring_units[:, 0, :].rearrange("p (h b t) -> p b h t", h=H_GDN, b=NB)
        kT = ring_units[:, 1, :].rearrange("p (h b t) -> p b h t", h=H_GDN, b=NB)
        vT = ring_units[:, 2, :].rearrange("p (h b t) -> p b h t", h=H_GDN, b=NB)
        kbT, qgT = per_head(unit[3]), per_head(unit[4])
        g_lhs, beta_lhs = per_head(unit[5]), per_head(unit[6])
        decay_strict, qk_decay = per_head(unit[5]), per_head(unit[6])
        decayT, exp_gc = per_head(unit[7]), per_head(unit[8])
        aT, inv, invT, off, mid = (per_head(unit[u]) for u in (9, 10, 11, 12, 13))
        kbg, kd, vb = (per_head(raw_flat[:, u * 1024:(u + 1) * 1024]) for u in range(3))
        uu, wT, vnew = per_head(unit[12]), per_head(unit[13]), per_head(unit[9])
        state = unit[2].rearrange("p (s h n) -> p s h n", s=2, h=H_GDN)
        o_gdn, o_sq = per_head(unit[10]), per_head(unit[11])
        oaT = own[:, 2, :].rearrange("p (h t) -> p h t", t=T)
        piece = lambda n, w: small[:, n:n + w].rearrange("p (b h) -> p b h", b=NB)
        sp_y, sp_m, g_tok, gc, gl = (piece(8 * n, 8) for n in range(5))
        e_last, beta_g, o_ss = (piece(8 * n, 8) for n in range(5, 8))

        pair = lambda bank: ps[:, bank:bank + 2, :].rearrange("p b (h n) -> p b h n", h=H_GDN)
        sq = lambda n: squares[:, n, :]
        ident = sq(IDENT)

        rope = sb("rope", 2, NB, N_HEADS64, ROPE_HALF)
        vis = sb("vis", 2, NB, CMP_STRIDE)
        cmp_w2 = sb("cmp_w2", 2, NSA_D)
        soft = sb("soft", 96)
        nqT = unit[0].rearrange("p (r t) -> p r t", t=T)
        nkT = unit[1][:, 0:512].rearrange("p (s t) -> p s t", t=T)
        o_part = unit[1][:, 512:768].rearrange("p (g r d) -> p g r d", g=NSA_G, d=NSA_D)
        p_cmpT = unit[1][:, 768:1024].rearrange("p (b t) -> p b t", b=NB)
        pairs = unit[3][:, 0:960].rearrange("p (s a g n) -> p s a g n", s=2, a=CMP_A, g=NSA_G)
        probs = [unit[5], unit[3]]
        hid = unit[7][:, 0:64].rearrange("p (s g n) -> p s g n", s=2, g=NSA_G)
        hid_rep = unit[7][:, 64:192].rearrange("p (g r n) -> p g r n", g=NSA_G, r=NSA_R)
        kcT = unit[7][:, 192:208]
        v_cmp = unit[7][:, 256:768].rearrange("p (h d) -> p h d", d=NSA_D)
        p_cmp = unit[7][:, 768:1024].rearrange("p (b h n) -> p b h n", b=NB, n=CMP_STRIDE)
        hT_flat = hT.rearrange("p k t -> p (k t)")
        probsT = hT_flat[:, 0:1024].rearrange("p (h n) -> p h n", n=P)
        o_nsa = hT_flat[:, 1024:2048].rearrange("p (b n) -> p b n", b=NB)
        obT = own[:, 3, :].rearrange("p (h t) -> p h t", t=T)
        JOBS = [(b, kind, half) for b in range(NB) for kind in range(2) for half in range(2)]
        N_JOB = len(JOBS)
        FIRST_TURN = 10
        FILL_STEPS = FIRST_TURN + 2 * N_JOB
        OUTPUTS_TURNED = 2 * (N_LEVEL + N_CHUNK) + 3
        job_heads = lambda flat, half: flat.rearrange("p (g r d) -> p g r d", g=NSA_G, r=NSA_R)[:, :, 2 * half:2 * half + 2, :]

        gated = nsa.rearrange("p b h d -> p (b h d)")[:, 0:1024].rearrange("p (i b n) -> p i b n", i=2, b=NB)
        gatedT = ctx.enter_context(nc.sbuf_tensor("sb_gatedT", [P, 2, NB, FC // P, P], F32))[:]

        class Step:

            def __init__(self, n=None, i=None, parity=None):
                self.n = n if i is None else 2 * i + parity + 1
                self.par = n % 2 if i is None else (parity + 1) % 2
                self.turns = n // 2 + 1 if i is None else i + 1 + (1 if self.par == 0 else 0)

        dft = [own[:, u, :].rearrange("p (b n) -> p b n", b=NB) for u in (0, 1, 3)]
        dft_fwd, dft_bwd, dft_time = dft
        dft_inv = own[:, 2, :].rearrange("p (f t) -> p f t", t=T)
        decay2 = own[:, 4, :].rearrange("p (b n) -> p b n", b=NB)
        filt_out = own[0:64, 5, :]
        kernF = own[:, 4:6, :].rearrange("p u (f n) -> p (u f) n", n=DH2)
        nsa_flat = nsa.rearrange("p b h d -> p (b h d)")
        emb, filt_in, filt_mid = nsa_flat[0:33, 1024:1280], nsa_flat[0:33, 1280:1344], nsa_flat[0:64, 1344:1472]
        w_route = sb("w_route", KT, N_GRP + N_EXP)
        kern = ring_units[:, 0:2, :].rearrange("p u (d n) -> p u d n", d=2)
        kern_abs = ring_units[:, 2:4, :].rearrange("p u (d n) -> p u d n", d=2)
        arg, turns_, act_a = (ring_units[0:64, 4, n * T:(n + 1) * T] for n in range(3))
        filt_norm = small[:, 72:76]
        u2 = raw_flat[:, 0:CT * (T + 2)].rearrange("p (c t) -> p c t", t=T + 2)
        merge_flat = merge.rearrange("p b i n -> p (b i n)")
        m_unit = [merge_flat[:, n * 1024:(n + 1) * 1024] for n in range(4)]
        conv2 = merge_flat[:, 0:CT * T].rearrange("p (c t) -> p c t", t=T)
        zT = m_unit[1].rearrange("p (c t) -> p c t", t=T)
        z_tok = m_unit[3].rearrange("p (b n) -> p b n", b=NB)
        u_four = silu_z
        four1 = nsa_flat[:, 0:2048].rearrange("p (c n) -> p c n", n=2 * T)
        zF = raw_flat[:, 0:2048].rearrange("p (f n) -> p f n", n=DH2)
        prodF = hT.rearrange("p k t -> p (k t)").rearrange("p (f n) -> p f n", n=DH2)
        cross = gatedT.rearrange("p i b f n -> p (i b f n)").rearrange("p (f n) -> p f n", n=DH2)
        y_hy = own[:, 1, :].rearrange("p (c t) -> p c t", t=T)
        y_fo = raw_flat[:, 2048:3072].rearrange("p (c t) -> p c t", t=T)
        y_sq = [m_unit[2], m_unit[3]]
        y_rs = merge_flat[:, 2048:4096]

        route = lambda n, w: raw_flat[:, n:n + w].rearrange("p (b e) -> p b e", b=NB)
        logits = route(0, 72)
        l_grp, l_exp = logits[:, :, 0:N_GRP], logits[:, :, N_GRP:]
        eq4, one_grp, eq, one1, one2, chosen = route(72, 8), route(80, 8), route(88, 64), route(152, 64), route(216, 64), route(280, 64)
        best = route(344, 2)
        ex = route(352, 10)
        shift, slot_of = route(368, 64), route(432, 64)
        vec = lambda n, w: raw_flat[:, n:n + w]
        over_ends = [vec(500, N_EXP), vec(532, N_EXP)]
        more, counts, base = vec(564, N_EXP), vec(596, N_EXP), vec(628, N_EXP)
        steps = vec(660, 7 * N_EXP).rearrange("p (e m) -> p e m", m=7)
        table_cmp = vec(900, 16 * N_EXP).rearrange("p (i e) -> p i e", e=N_EXP)
        table = vec(1420, 17)
        first, second = vec(1440, NB).rearrange("p (b e) -> p b e", e=1), vec(1442, NB).rearrange("p (b e) -> p b e", e=1)
        slots_of = vec(1444, 2 * NB)
        weights = vec(1448, 2 * NB)
        table_i = sb("table_i", 17, dt=I32)
        xn = merge[:, :, 0, :]
        rows_part, gu_part = (own[:, 0, n * 256:(n + 1) * 256] for n in range(2))
        down_part = own[:, 2, :]
        hgT = own[:, 1, 0:256].rearrange("p (k c) -> p k c", c=CAP)
        pick = [own[:, 3, 512 + 64 * n:576 + 64 * n].rearrange("p (b c) -> p b c", b=NB) for n in range(2)]
        pick_tmp = [own[:, 3, 640 + 32 * n:672 + 32 * n] for n in range(3 * NB)]
        zero = own[:, 3, 832:960]
        pick4 = [own[:, 4, 256 * n:256 * (n + 1)].rearrange("p (b j c) -> p b j c", b=NB, j=4) for n in range(2)]
        pickT = own[:, 4, 512:768].rearrange("p (b t) -> p b t", b=NB)
        silu_g = own[:, 4, 768:896]
        actT = own[:, 4, 896:1024].rearrange("p (f c) -> p f c", c=CAP)
        by_tile = lambda turned: turned.rearrange("p (c j s) -> p c j s", c=2, j=4)
        ITEM_SLOTS = ((3, 4, 5), (0, 1, 2))

        def item_steps(pe):

            def group(j):
                return slice(CAP * j, CAP * (j + 1))

            def gather(par):
                for b in range(NB):
                    for j in range(4):
                        m = pe.matmul(ps[group(j), 0, 0:256], pick[par][:, b, :], xn[:, b, j * 256:(j + 1) * 256],
                                      start=(b == 0), stop=(b == NB - 1))
                return m

            def turn(bank, part):
                for c in range(2):
                    m = pe.transpose(ps[:, bank, c * P:(c + 1) * P], part[:, c * P:(c + 1) * P], ident)
                return m

            def turn_rows(par):
                return turn(1, rows_part)

            def gate_up(par, slots):
                w = [ring[:, slots[n], :].rearrange("p (k n) -> p k n", n=DE) for n in range(2)]
                for k in range(KT):
                    for j in range(4):
                        m = pe.matmul(ps[group(j), 2, 0:256], hgT[:, k, :], w[j // 2][:, k, (j % 2) * 256:(j % 2 + 1) * 256],
                                      start=(k == 0), stop=(k == KT - 1))
                return m

            def turn_gate_up(par):
                turn(3, gu_part)
                for b in range(NB):
                    m = pe.transpose(ps[:, 3, 256 + b * P:256 + (b + 1) * P], pick4[par][:, b].rearrange("p j c -> p (j c)"), ident)
                return m

            def down(slot):
                w = ring[:, slot, :].rearrange("p (f n) -> p f n", n=D)
                for half in range(2):
                    for j in range(4):
                        m = pe.matmul(ps[group(j), 1 + half, :], actT[:, j, :], w[:, j, half * BANK:(half + 1) * BANK],
                                      start=True, stop=True)
                return m

            def scatter(start, stop):
                for b in range(NB):
                    for half in range(2):
                        m = pe.matmul(ps[:, 4 + 2 * b + half, :], pickT[:, b, :], down_part[:, half * BANK:(half + 1) * BANK],
                                      start=start, stop=stop, skip_group_check=True)
                return m
            return gather, turn_rows, gate_up, turn_gate_up, down, scatter

        def item_picks(dve, link, par):
            iota = rows[:, R_IOTA:R_IOTA + CAP]
            for b in range(NB):
                hit, hit_w, other_w = pick_tmp[3 * b:3 * b + 3]
                dve.tensor_scalar(hit, iota, slots_of[:, b:b + 1], None, ALU.is_equal)
                link(dve.tensor_scalar(hit_w, iota, slots_of[:, b:b + 1], weights[:, b:b + 1], ALU.is_equal, ALU.mult))
                at = NB + b
                dve.scalar_tensor_tensor(pick[par][:, b, :], iota, slots_of[:, at:at + 1], hit, ALU.is_equal, ALU.add)
                link(dve.tensor_scalar(other_w, iota, slots_of[:, at:at + 1], weights[:, at:at + 1], ALU.is_equal, ALU.mult))
                link(dve.tensor_tensor(hit_w, hit_w, other_w, ALU.add))
                dve.tensor_copy(pick4[par][:, b], spread(hit_w, 1, 4))
            return dve.tensor_scalar(slots_of, slots_of, -float(CAP), None, ALU.add)

        block = ctx.enter_context(nc.Block())
        IN2_SLOTS, OUT2_SLOTS = (3, 4, 5, 1), (0, 2)

        def chain(eng, name):
            count = [0]

            def link(ins):
                count[0] += 1
                ins.then_inc(sig(name), 1)
                eng.wait_ge(sig(name), count[0])
            return link

        stream = [("w_in", n) for n in range(11)] + [("cmp", 0), ("branch", 0), ("branch", 1), ("w_out", 0), ("w_out", 1)]
        where = {what: (n % 4, n // 4 + 1) for n, what in enumerate(stream)}

        def arrived(eng, what):
            slot, use = where[what]
            eng.wait_ge(sig(f"slot{slot}_loaded"), 16 * use)
            return ring[:, slot, :]

        def wait_used(eng, what):
            kind, i = what
            name, n = {"w_in": ("qkv_projected", 2 * i + 2) if i < 3 else ("projected", 2 * (i - 3) + 2), "cmp": ("hid_made", 2),
                       "branch": ("branch_made", i + 1), "w_out": ("w_out_made", i + 1)}[kind]
            eng.wait_ge(sig(name), since(name, n))

        @block.sync
        def _(sp):
            sp.dma_start(x, dram["x"]).then_inc(sig("x_loaded"), 16)
            sp.dma_start(squares, dram["squares"]).then_inc(sig("const_loaded"), 16)
            sp.dma_start(cols, dram["cols"]).then_inc(sig("const_loaded"), 16)
            for n, what in enumerate(stream):
                slot, use = where[what]
                if n >= 4:
                    wait_used(sp, stream[n - 4])
                dst = ring[:, slot, :]
                kind, i = what
                if kind == "w_in" and i == 6:
                    dst = dst.rearrange("p (k n) -> p k n", n=BANK)[:, :, 0:288]
                    src = dram["w_in"][i][:, :, 0:288]
                elif kind == "w_in":
                    src = dram["w_in"][i].rearrange("p k n -> p (k n)")
                elif kind == "cmp":
                    src = dram["cmp_w1"].rearrange("p v a n -> p (v a n)")
                elif kind == "branch":
                    src = dram["w_branch"][i].rearrange("p k n -> p (k n)")
                else:
                    src = dram["w_out"][i].rearrange("p k n -> p (k n)")
                sp.dma_start(dst, src).then_inc(sig(f"slot{slot}_loaded"), 16)
                if n == 1:
                    sp.dma_start(rows, dram["rows"]).then_inc(sig("rows_loaded"), 16)
                    sp.dma_start(rope, dram["rope"]).then_inc(sig("nsa_const_loaded"), 16)
                    sp.dma_start(vis, dram["vis"]).then_inc(sig("nsa_const_loaded"), 16)
                    sp.dma_start(cmp_w2, dram["cmp_w2"]).then_inc(sig("nsa_const_loaded"), 16)
            wait_used(sp, ("branch", 0))

            def load_gate_up(s):
                sp.dma_start(ring[:, s.par, :], dram["w_gu"][s.n].rearrange("p k h n -> p (k h n)"))\
                  .then_inc(sig(f"gu{s.par}_loaded"), 16)

            def load_down(s):
                sp.dma_start(ring[:, 2, s.par * 2048:(s.par + 1) * 2048], dram["w_dn"][s.n].rearrange("p f n -> p (f n)"))\
                  .then_inc(sig(f"dn{s.par}_loaded"), 16)

            load_gate_up(Step(0))
            wait_used(sp, ("branch", 1))
            for name, dst in (("dft_fwd", own[:, 0, :]), ("dft_bwd", own[:, 1, :]), ("dft_inv", own[:, 2, :]),
                              ("dft_time", own[:, 3, :]), ("decay", own[:, 4, :])):
                sp.dma_start(dst, dram[name].rearrange("p a n -> p (a n)")).then_inc(sig("mix_const_loaded"), 16)
            sp.dma_start(filt_out, dram["filt_out"]).then_inc(sig("mix_const_loaded"), 16)
            sp.dma_start(emb, dram["emb"]).then_inc(sig("mix_const_loaded"), 16)
            sp.dma_start(filt_in, dram["filt_in"]).then_inc(sig("mix_const_loaded"), 16)
            sp.dma_start(filt_mid, dram["filt_mid"].rearrange("p a n -> p (a n)")).then_inc(sig("mix_const_loaded"), 16)
            sp.dma_start(w_route, dram["w_route"]).then_inc(sig("mix_const_loaded"), 16)
            load_gate_up(Step(1))
            wait_used(sp, ("w_out", 0))
            load_down(Step(0))
            load_down(Step(1))
            with sp.Fori(0, (N_FC - 3) // 2) as i:
                for parity in range(2):
                    s = Step(i=i, parity=parity)
                    nxt = Step(i=i, parity=parity)
                    nxt.n, nxt.par = 2 * i + parity + 2, parity
                    sp.wait_ge(sig("gu_made"), 2 * (2 * i + parity) + 2)
                    load_gate_up(nxt)
                    sp.wait_ge(sig("down_made"), 2 * i + parity + 1)
                    load_down(nxt)
            s = Step(N_FC - 1)
            sp.wait_ge(sig("gu_made"), 2 * (N_FC - 2))
            load_gate_up(s)
            sp.wait_ge(sig("down_made"), N_FC - 2)
            load_down(s)
            wait_used(sp, ("w_out", 1))
            sp.wait_ge(sig("filter_turned"), since("filter_turned", 1))
            for c, slot in enumerate(IN2_SLOTS):
                if c == 3:
                    sp.wait_ge(sig("gu_made"), 2 * (N_FC - 1))
                sp.dma_start(ring[:, slot, :], dram["w_in2"][c].rearrange("p k n -> p (k n)")).then_inc(sig(f"slot{slot}_loaded"), 16)
            for half, slot in enumerate(OUT2_SLOTS):
                sp.wait_ge(sig("gu_made" if half == 0 else "down_made"), 2 * N_FC if half == 0 else N_FC)
                sp.dma_start(ring[:, slot, :], dram["w_out2"][half].rearrange("p k n -> p (k n)")).then_inc(sig(f"slot{slot}_loaded"), 16)
            def load_item(par, expert, done=None):
                for n, slot in enumerate(ITEM_SLOTS[par]):
                    if done is not None and n == 0:
                        sp.wait_ge(sig("item_gu_made"), done)
                    if done is not None and n == 2:
                        sp.wait_ge(sig("item_down_made"), done)
                    src = dram["w_exp"][expert].rearrange("p i n -> p (i n)")[:, n * 4096:(n + 1) * 4096] if isinstance(expert, int) \
                        else dram["w_exp"][bass.ds(expert, 1)].rearrange("e p i n -> p (e i n)")[:, n * 4096:(n + 1) * 4096]
                    sp.dma_start(ring[:, slot, :], src).then_inc(sig(f"item{par}_{n}_loaded"), 16)

            sp.wait_ge(sig("u2_projected"), 6)
            load_item(0, 0)
            sp.wait_ge(sig("out2_made"), since("out2_made", 1))
            load_item(1, 1)
            with sp.Fori(0, N_EXP // 2 - 1) as i:
                for par in range(2):
                    load_item(par, 2 * i + par + 2, 2 * i + par + 1)
            sp.wait_ge(sig("table_ready"), since("table_ready", 1))
            sp.wait_ge(sig("item_down_made"), N_EXP)
            n_over = sp.value_load(table_i[0:1, 16:17], min_val=0, max_val=16)
            with sp.If(n_over > 0):
                with sp.Fori(0, n_over) as i:
                    sp.wait_ge(sig("over_next"), i + 1)
                    expert = sp.value_load(table_i[0:1, bass.ds(i, 1)], min_val=0, max_val=N_EXP - 1)
                    for n, slot in enumerate(ITEM_SLOTS[0]):
                        sp.dma_start(ring[:, slot, :], dram["w_exp"][bass.ds(expert, 1)].rearrange("e p i n -> p (e i n)")[:, n * 4096:(n + 1) * 4096])\
                          .then_inc(sig("over_loaded"), 16)
            sp.wait_ge(sig("out_ready"), NB)
            sp.dma_start(dram["out"], merge[:, :, 0, :]).then_inc(sig("out_stored"), 16)
            sp.wait_ge(sig("out_stored"), 16)

        @block.gpsimd
        def _(pool):
            pool.memset(raw[:, :, 0:TAPS - 1], 0.0).then_inc(sig("raw_padded"), 1)
            pool.wait_ge(sig("const_loaded"), 32)
            for t in (inv, invT):
                pool.tensor_copy(t.rearrange("p b h n -> p (b h) n"), spread(ident, 1, NB * H_GDN)).then_inc(sig("inverse_started"), 1)
            pool.wait_ge(sig("o_normed"), 1)
            pool.memset(u2[:, :, 0:1], 0.0)
            pool.memset(u2[:, :, T + 1:T + 2], 0.0).then_inc(sig("u2_padded"), 1)

        @block.tensor
        def _(pe):
            def transposes(bank, sources, signal):
                for n, s in enumerate(sources):
                    m = pe.transpose(ps[:, bank, n * P:(n + 1) * P], s, ident)
                m.then_inc(sig(signal), 1)

            def turn_rows(tok, ready, signal, first_free=None):
                for b in range(NB):
                    pe.wait_ge(sig(ready), since(ready, b + 1))
                    for half in range(2):
                        transposes(2 * b + half, [tok[:, b, (4 * half + n) * P:(4 * half + n + 1) * P] for n in range(4)], signal)

            def project(c):
                w = arrived(pe, ("w_in", c)).rearrange("p (k n) -> p k n", n=BANK)
                width = 288 if c == 6 else BANK
                for b in range(NB):
                    n = 2 * (c - 3) + b
                    if n >= 4:
                        pe.wait_ge(sig("projected_out"), n - 3)
                    for k in range(KT):
                        m = pe.matmul(ps[:, n % 4, 0:width], hT[:, k, b * P:(b + 1) * P], w[:, k, 0:width],
                                      start=(k == 0), stop=(k == KT - 1))
                    m.then_inc(sig("projected"), 1)

            pe.wait_ge(sig("const_loaded"), 32)
            turn_rows(merge[:, :, 0, :], "x_normed", "x_turned")
            pe.wait_ge(sig("h_ready"), since("h_ready", 4))
            for c in range(3):
                w = arrived(pe, ("w_in", c)).rearrange("p (k n) -> p k n", n=BANK)
                for pr in range(2 * c, 2 * c + 2):
                    if pr >= 4:
                        pe.wait_ge(sig("qkv_out"), pr - 3)
                    for ct in (2 * pr, 2 * pr + 1):
                        for k in range(KT):
                            m = pe.matmul(ps[:, 4 + pr % 4, (ct % 2) * T:(ct % 2 + 1) * T],
                                          w[:, k, (ct % 4) * P:(ct % 4 + 1) * P], hT[:, k, :],
                                          start=(k == 0), stop=(k == KT - 1))
                    m.then_inc(sig("qkv_projected"), 1)
            for c in range(3, 7):
                project(c)

            pe.wait_ge(sig("qkv_out"), 6)
            pe.wait_ge(sig("g_spread"), since("g_spread", 2))
            for b in range(NB):
                for h in range(H_GDN):
                    pe.matmul(pair(4)[:, b, h, :], g_lhs[:, b, h, :], sq(CUM), start=True, stop=True)
                    pe.matmul(pair(6)[:, b, h, :], beta_lhs[:, b, h, :], ident, start=True, stop=True)
            pe.wait_ge(sig("projected_out"), 8)
            gt = g_tok.rearrange("p b h -> p (b h)")
            pe.matmul(ps[:, 0, 0:8], sq(CUM), gt, start=True, stop=True)
            pe.matmul(ps[:, 0, 8:16], sq(SAME), gt, start=True, stop=True).then_inc(sig("gc_ready"), 1)
            pe.wait_ge(sig("gc_out"), since("gc_out", 2))
            pe.wait_ge(sig("beta_used"), since("beta_used", 1))
            pe.wait_ge(sig("qk_squared"), since("qk_squared", 1))
            for n in range(4):
                m = pe.matmul(ps[:, 4 + n, :], sq(ONES), qkT_sq[:, 2 * n:2 * n + 2, :].rearrange("p c t -> p (c t)"),
                              start=True, stop=True)
            m.then_inc(sig("qk_summed"), 1)
            project(7)
            pe.wait_ge(sig("kb_ready"), since("kb_ready", 1))
            for b in range(NB):
                for h in range(H_GDN):
                    pe.matmul(pair(4)[:, b, h, :], kT[:, b, h, :], kbT[:, b, h, :], start=True, stop=True)
                    m = pe.matmul(pair(6)[:, b, h, :], kT[:, b, h, :], qT[:, b, h, :], start=True, stop=True)
            m.then_inc(sig("kk_ready"), 1)
            project(8)
            for n, (src, done) in enumerate(((kT, "a_ready"), (vT, "qk_ready"))):
                pe.wait_ge(sig(done), since(done, 1))
                for b in range(NB):
                    for h in range(H_GDN):
                        m = pe.transpose(pair(4 + 2 * n)[:, b, h, :], src[:, b, h, :], ident)
                m.then_inc(sig("kv_turned"), 1)
            project(9)
            project(10)
            pe.wait_ge(sig("projected_out"), 16)
            pe.wait_ge(sig("kd_ready"), since("kd_ready", 1))
            pe.wait_ge(sig("inverse_started"), 2)

            def attention_step(t):
                if t == 0:
                    pe.wait_ge(sig("roped"), since("roped", 1))
                    for b in range(NB):
                        transposes(4 + b, [nsa[:, b, 2 * r:2 * r + 2, :].rearrange("p h d -> p (h d)") for r in range(NSA_R)], "nq_turned")
                    transposes(6, [nsa[:, b, h:h + 2, :].rearrange("p h d -> p (h d)") for h in (12, 16) for b in range(NB)], "nk_turned")
                    for s in range(2):
                        for g in range(NSA_G):
                            for b in range(NB):
                                for l2 in range(2):
                                    at = (2 * s + g) * P + b * CHUNK
                                    m = pe.matmul(ps[l2 * NSA_D:(l2 + 1) * NSA_D, 7, at:at + CHUNK], nsa[:, b, 8 + 2 * s + g, :],
                                                  ident[:, l2::2], start=True, stop=True)
                    m.then_inc(sig("pairs_made"), 1)
                elif t in (1, 2):
                    s, n = t - 1, NSA_G * N_CMP
                    w1 = arrived(pe, ("cmp", 0)).rearrange("p (s a n) -> p s a n", s=2, a=CMP_A)
                    pe.wait_ge(sig("pairs_ready"), since("pairs_ready", 1))
                    pe.wait_ge(sig("nq_ready"), since("nq_ready", 2))
                    for a in range(CMP_A):
                        m = pe.matmul(ps[:, 4 + s, 0:n], w1[:, s, a, :], pairs[:, s, a, :, :].rearrange("p g n -> p (g n)"),
                                      start=(a == 0), stop=(a == CMP_A - 1))
                    m.then_inc(sig("hid_made"), 1)
                elif t == 3:
                    pe.wait_ge(sig("nsa_const_loaded"), 48)
                    pe.wait_ge(sig("hid_ready"), since("hid_ready", 2))
                    for g in range(NSA_G):
                        pe.matmul(ps[g * NSA_D:(g + 1) * NSA_D, 4, 64:80], cmp_w2[:, 0, :], hid[:, 0, g, :], start=True, stop=True)
                    pe.wait_ge(sig("hid_rep_ready"), since("hid_rep_ready", 1))
                    pe.matmul(ps[:, 4, 128:192], hid_rep.rearrange("p g r n -> p (g r n)"), cmp_w2[:, 1, :], start=True, stop=True)\
                      .then_inc(sig("kv_cmp_made"), 1)
                elif t == 4:
                    pe.wait_ge(sig("kv_cmp_ready"), since("kv_cmp_ready", 1))
                    pe.wait_ge(sig("nk_ready"), since("nk_ready", 1))
                    for b in range(NB):
                        for h in range(NSA_H):
                            r, g = h // NSA_G, h % NSA_G
                            gp = slice(g * NSA_D, (g + 1) * NSA_D)
                            at = (b * NSA_R + r) * CMP_STRIDE
                            m = pe.matmul(ps[:, 5 + g, at:at + CMP_STRIDE], nqT[gp, r, b * P:(b + 1) * P], kcT[gp, :],
                                          start=True, stop=True)
                    m.then_inc(sig("s_cmp_made"), 1)
                elif t == 6:
                    pe.wait_ge(sig("p_cmp_ready"), 1)
                    transposes(7, [p_cmp[:, b].rearrange("p h n -> p (h n)") for b in range(NB)], "p_cmp_turned")
                elif t == 7:
                    pe.wait_ge(sig("p_cmpT_ready"), 1)
                    for b in range(NB):
                        m = pe.matmul(ps[:, 4 + b, :], p_cmpT[:, b, :], v_cmp.rearrange("p h d -> p (h d)"), start=True, stop=True)
                    m.then_inc(sig("o_cmp_made"), 1)
                elif t in (8, 9):
                    job_scores(t - 8)
                elif t >= FIRST_TURN and (t - FIRST_TURN) % 2 == 0:
                    job_turn((t - FIRST_TURN) // 2)
                elif t > FIRST_TURN:
                    q = (t - FIRST_TURN) // 2
                    job_output(q)
                    if q + 2 < N_JOB:
                        job_scores(q + 2)

            def job_scores(q):
                b, kind, half = JOBS[q]
                nk = (b + 1) * P
                if q:
                    pe.wait_ge(sig("scores_out"), q)
                else:
                    pe.wait_ge(sig("o_cmp_out"), 1)
                for rr in range(2):
                    for g in range(NSA_G):
                        gp = slice(g * NSA_D, (g + 1) * NSA_D)
                        m = pe.matmul(ps[:, 4 + g, rr * nk:(rr + 1) * nk], nqT[gp, 2 * half + rr, b * P:(b + 1) * P],
                                      nkT[gp, kind, 0:nk], start=True, stop=True)
                m.then_inc(sig("scores_made"), 1)

            def job_turn(q):
                b = JOBS[q][0]
                pe.wait_ge(sig("probs_ready"), q + 1)
                if q:
                    pe.wait_ge(sig("o_job_out"), q)
                for n in range(4 * (b + 1)):
                    m = pe.transpose(ps[:, 6 + n // 4, (n % 4) * P:(n % 4 + 1) * P], probs[q % 2][:, n * P:(n + 1) * P], ident)
                m.then_inc(sig("probs_turned"), 1)

            def job_output(q):
                b, kind, half = JOBS[q]
                pe.wait_ge(sig("probsT_ready"), q + 1)
                for h in range(4):
                    for kb in range(b + 1):
                        m = pe.matmul(ps[:, 7, h * NSA_D:(h + 1) * NSA_D], probsT[:, h * (b + 1) + kb, :],
                                      nsa[:, kb, 14 + 4 * kind + h // 2, :], start=(kb == 0), stop=(kb == b))
                m.then_inc(sig("o_job_made"), 1)

            for n in range(N_LEVEL):
                pe.wait_ge(sig("off_ready"), n + 1)
                if n:
                    pe.wait_ge(sig("inverse_ready"), n)
                for b in range(NB):
                    for h in range(H_GDN):
                        m = pe.matmul(pair(0)[:, b, h, :], off[:, b, h, :], inv[:, b, h, :], start=True, stop=True)
                m.then_inc(sig("mid_made"), 1)
                attention_step(2 * n)
                pe.wait_ge(sig("mid_ready"), n + 1)
                for b in range(NB):
                    for h in range(H_GDN):
                        pe.matmul(pair(2)[:, b, h, :], invT[:, b, h, :], mid[:, b, h, :], start=True, stop=True)
                        m = pe.matmul(pair(0)[:, b, h, :], mid[:, b, h, :], invT[:, b, h, :], start=True, stop=True)
                m.then_inc(sig("step_made"), 1)
                attention_step(2 * n + 1)
            pe.wait_ge(sig("inverse_ready"), N_LEVEL)
            for b in range(NB):
                for h in range(H_GDN):
                    pe.matmul(pair(0)[:, b, h, :], invT[:, b, h, :], vb[:, b, h, :], start=True, stop=True)
                    m = pe.matmul(pair(2)[:, b, h, :], kbg[:, b, h, :], invT[:, b, h, :], start=True, stop=True)
            m.then_inc(sig("uw_made"), 1)
            attention_step(2 * N_LEVEL)
            pe.wait_ge(sig("uw_ready"), 2)
            for c in range(N_CHUNK):
                b, r = c // 2, slice(CHUNK * (c % 2), CHUNK * (c % 2) + CHUNK)
                heads = range(H_GDN)
                if c:
                    pe.wait_ge(sig("state_ready"), c)
                    for h in heads:
                        m = pe.matmul(ps[r, 0, h * P:(h + 1) * P], wT[:, b, h, r], state[:, c % 2, h, :], start=True, stop=True)
                    m.then_inc(sig("ws_made"), 1)
                    attention_step(2 * N_LEVEL + 2 * c)
                pe.wait_ge(sig("vnew_ready"), c + 1)
                if c < N_CHUNK - 1:
                    for h in heads:
                        m = pe.matmul(ps[:, 1, h * P:(h + 1) * P], kd[r, b, h, :], vnew[r, b, h, :], start=True, stop=True)
                    m.then_inc(sig("kv_made"), 1)
                for h in heads:
                    if c:
                        pe.matmul(pair(2)[r, b, h, :], qgT[:, b, h, r], state[:, c % 2, h, :], start=True, stop=False)
                    m = pe.matmul(pair(2)[r, b, h, :], qk_decay[r, b, h, r], vnew[r, b, h, :], start=(c == 0), stop=True)
                m.then_inc(sig("o_made"), 1)
                attention_step(2 * N_LEVEL + 2 * c + 1)
            for t in range(2 * N_LEVEL + 2 * N_CHUNK, OUTPUTS_TURNED):
                attention_step(t)
            pe.wait_ge(sig("o_normed"), 1)
            for b in range(NB):
                for h in range(H_GDN):
                    m = pe.transpose(pair(0)[:, b, h, :], o_gdn[:, b, h, :], ident)
            m.then_inc(sig("o_turned"), 1)
            for t in range(OUTPUTS_TURNED, FILL_STEPS):
                attention_step(t)
            pe.wait_ge(sig("oa_ready"), 1)
            pe.wait_ge(sig("o_nsa_ready"), 1)
            for b in range(NB):
                transposes(2 + b, [o_nsa[:, b, n * P:(n + 1) * P] for n in range(4)], "ob_turned")

            pe.wait_ge(sig("ob_ready"), NB)
            for br, src in enumerate((oaT, obT)):
                w = arrived(pe, ("branch", br)).rearrange("p (k n) -> p k n", n=D)
                for b in range(NB):
                    for half in range(2):
                        for k in range(4):
                            m = pe.matmul(ps[:, 4 * b + 2 * br + half, :], src[:, k, b * P:(b + 1) * P],
                                          w[:, k, half * BANK:(half + 1) * BANK], start=(k == 0), stop=(k == 3))
                m.then_inc(sig("branch_made"), 1)
            for b in range(NB):
                pe.wait_ge(sig("merged"), NB)
                for half in range(2):
                    transposes(2 * b + half, [merge[:, b, 0, (4 * half + n) * P:(4 * half + n + 1) * P] for n in range(4)], "merge_turned")
            pe.wait_ge(sig("mergedT_ready"), 4)
            for half in range(2):
                w = arrived(pe, ("w_out", half)).rearrange("p (k n) -> p k n", n=BANK)
                for b in range(NB):
                    for k in range(KT):
                        m = pe.matmul(ps[:, 4 + 2 * b + half, :], hT[:, k, b * P:(b + 1) * P], w[:, k, :],
                                      start=(k == 0), stop=(k == KT - 1))
                m.then_inc(sig("w_out_made"), 1)

            pe.wait_ge(sig("mix_const_loaded"), 160)
            pe.matmul(ps[0:64, 0, 0:T], filt_in, emb, start=True, stop=True).then_inc(sig("filt_layer"), 1)
            for n in range(2):
                pe.wait_ge(sig("filt_sin"), since("filt_sin", n + 1))
                pe.matmul(ps[0:64, 0, 0:T], filt_mid[:, n * 64:(n + 1) * 64], act_a, start=True, stop=True).then_inc(sig("filt_layer"), 1)
            pe.wait_ge(sig("filt_sin"), since("filt_sin", 3))
            for b in range(NB):
                for d in range(2):
                    m = pe.matmul(ps[:, 2 * b + d, :], act_a[:, b * P:(b + 1) * P], filt_out[:, d * DH2:(d + 1) * DH2], start=True, stop=True)
            m.then_inc(sig("filt_out_made"), 1)
            pe.wait_ge(sig("kern_ready"), since("kern_ready", 1))
            for f in range(4):
                for n, (mat, b, d) in enumerate(((dft_fwd, 0, 0), (dft_fwd, 1, 0), (dft_bwd, 0, 1), (dft_bwd, 1, 1))):
                    m = pe.matmul(ps[:, f, :], mat[:, b, f * P:(f + 1) * P], kern[:, b, d, :], start=(n == 0), stop=(n == 3))
            m.then_inc(sig("kernF_made"), 1)
            pe.wait_ge(sig("kern_abs_ready"), since("kern_abs_ready", 1))
            pe.wait_ge(sig("x2_added"), 1)
            for ct in range(NHT):
                for n in range(4):
                    b, d = n // 2, n % 2
                    one = C_ONE + (1 if (b, d) == (0, 1) else 0)
                    m = pe.matmul(ps[:, 4, ct:ct + 1], kern_abs[:, b, d, ct * P:(ct + 1) * P], cols[:, one:one + 1],
                                  start=(n == 0), stop=(n == 3))
            m.then_inc(sig("filter_turned"), 1)
            pe.wait_ge(sig("kernF_ready"), since("kernF_ready", 1))
            pe.wait_ge(sig("filt_norm_ready"), since("filt_norm_ready", 1))
            for b in range(NB):
                pe.wait_ge(sig("x2_normed"), since("x2_normed", b + 1))
                for half in range(2):
                    transposes(2 * b + half, [merge[:, b, 0, (4 * half + n) * P:(4 * half + n + 1) * P] for n in range(4)], "x2_turned")
            pe.wait_ge(sig("h2_ready"), since("h2_ready", 4))

            def gate_up(s, first=False):
                pe.wait_ge(sig(f"gu{s.par}_loaded"), 16 * s.turns)
                w = ring[:, s.par, :].rearrange("p (k n) -> p k n", n=BANK)
                if not first:
                    pe.wait_ge(sig("gatedT_ready"), s.n - 1)
                for b in range(NB):
                    for k in range(KT):
                        m = pe.matmul(ps[:, 2 * s.par + b, :], hT[:, k, b * P:(b + 1) * P], w[:, k, :],
                                      start=(k == 0), stop=(k == KT - 1))
                    m.then_inc(sig("gu_made"), 1)

            def down(s, start=False, stop=False):
                pe.wait_ge(sig("gated_ready"), s.n + 1)
                for b in range(NB):
                    for f in range(FC // P):
                        m = pe.transpose(ps[:, 2 * s.par + b, f * P:(f + 1) * P], gated[:, s.par, b, f * P:(f + 1) * P], ident)
                m.then_inc(sig("gated_turned"), 1)
                pe.wait_ge(sig(f"dn{s.par}_loaded"), 16 * s.turns)
                pe.wait_ge(sig("gatedT_ready"), s.n + 1)
                w = ring[:, 2, s.par * 2048:(s.par + 1) * 2048].rearrange("p (f n) -> p f n", n=D)
                for b in range(NB):
                    for half in range(2):
                        for f in range(FC // P):
                            m = pe.matmul(ps[:, 4 + 2 * b + half, :], gatedT[:, s.par, b, f, :], w[:, f, half * BANK:(half + 1) * BANK],
                                          start=start and f == 0, stop=stop and f == FC // P - 1, skip_group_check=True)
                m.then_inc(sig("down_made"), 1)

            gate_up(Step(0), first=True)
            gate_up(Step(1), first=True)
            down(Step(0), start=True)
            with pe.Fori(0, (N_FC - 3) // 2) as i:
                for parity in range(2):
                    s, nxt = Step(i=i, parity=parity), Step(i=i, parity=parity)
                    nxt.n, nxt.par, nxt.turns = 2 * i + parity + 2, parity, i + 2
                    gate_up(nxt)
                    down(s)
            gate_up(Step(N_FC - 1))
            down(Step(N_FC - 2))
            down(Step(N_FC - 1), stop=True)

            def mix_weights(slot):
                pe.wait_ge(sig(f"slot{slot}_loaded"), 16 * (len(stream) // 4 + 1 if slot < 4 else 1))

            for b in range(NB):
                pe.wait_ge(sig("x3_normed"), since("x3_normed", b + 1))
                for half in range(2):
                    transposes(2 * b + half, [merge[:, b, 0, (4 * half + n) * P:(4 * half + n + 1) * P] for n in range(4)], "x3_turned")
            pe.wait_ge(sig("h3_ready"), since("h3_ready", 4))
            for c in range(3):
                mix_weights(IN2_SLOTS[c])
                w = ring[:, IN2_SLOTS[c], :].rearrange("p (k n) -> p k n", n=BANK)
                for pr in range(2 * c, 2 * c + 2):
                    if pr >= 4:
                        pe.wait_ge(sig("u2_out"), pr - 3)
                    for ct in (2 * pr, 2 * pr + 1):
                        for k in range(KT):
                            m = pe.matmul(ps[:, 4 + pr % 4, (ct % 2) * T:(ct % 2 + 1) * T],
                                          w[:, k, (ct % 4) * P:(ct % 4 + 1) * P], hT[:, k, :],
                                          start=(k == 0), stop=(k == KT - 1))
                    m.then_inc(sig("u2_projected"), 1)
            mix_weights(IN2_SLOTS[3])
            w = ring[:, IN2_SLOTS[3], :].rearrange("p (k n) -> p k n", n=BANK)
            for b in range(NB):
                for k in range(KT):
                    m = pe.matmul(ps[:, b, :], hT[:, k, b * P:(b + 1) * P], w[:, k, :], start=(k == 0), stop=(k == KT - 1))
                m.then_inc(sig("four_projected"), 1)
            pe.wait_ge(sig("four_ready"), since("four_ready", NB))
            for ct in range(NHT):
                for b in range(NB):
                    m = pe.matmul(ps[:, ct, :], u_four[:, b, ct * P:(ct + 1) * P], dft_time[:, b, :], start=(b == 0), stop=(b == NB - 1))
                m.then_inc(sig("four1_made"), 1)
            pe.wait_ge(sig("z_ready"), since("z_ready", 1))
            for b in range(NB):
                transposes(4 + b, [zT[:, ct, b * P:(b + 1) * P] for ct in range(NHT)], "z_turned")
            pe.wait_ge(sig("four1_ready"), since("four1_ready", NHT))
            for ct in range(NHT):
                at = ps[:, 6 + ct // 2, (ct % 2) * T:(ct % 2 + 1) * T]
                pe.matmul(at, sq(DFT_C), four1[:, ct, 0:T], start=True, stop=False)
                m = pe.matmul(at, sq(DFT_S), four1[:, ct, T:2 * T], start=False, stop=True)
            m.then_inc(sig("four2_made"), 1)
            pe.wait_ge(sig("z_tok_ready"), since("z_tok_ready", NB))
            for f in range(4):
                for b in range(NB):
                    m = pe.matmul(ps[:, f, :], dft_fwd[:, b, f * P:(f + 1) * P], z_tok[:, b, :], start=(b == 0), stop=(b == NB - 1))
                m.then_inc(sig("zF_made"), 1)
            pe.wait_ge(sig("prod_ready"), since("prod_ready", 1))
            for ct in range(NHT):
                for f in range(4):
                    m = pe.matmul(ps[:, 4 + ct // 2, (ct % 2) * T:(ct % 2 + 1) * T], prodF[:, f, ct * P:(ct + 1) * P],
                                  dft_inv[:, f, :], start=(f == 0), stop=(f == 3))
            m.then_inc(sig("conv_made"), 1)
            for n in range(2):
                pe.wait_ge(sig("y_squared"), since("y_squared", n + 1))
                for half in range(2):
                    m = pe.matmul(ps[:, 2 * n + half, :], sq(SAME), y_sq[n][:, half * BANK:(half + 1) * BANK], start=True, stop=True)
            m.then_inc(sig("y_summed"), 1)
            pe.wait_ge(sig("y_ready2"), since("y_ready2", 2))
            for half in range(2):
                mix_weights(OUT2_SLOTS[half])
                w = ring[:, OUT2_SLOTS[half], :].rearrange("p (k n) -> p k n", n=BANK)
                for b in range(NB):
                    for k in range(KT):
                        src = y_hy if k < NHT else y_fo
                        m = pe.matmul(ps[:, 4 + 2 * b + half, :], src[:, k % NHT, b * P:(b + 1) * P], w[:, k, :],
                                      start=(k == 0), stop=(k == KT - 1))
            m.then_inc(sig("out2_made"), 1)

            for b in range(NB):
                pe.wait_ge(sig("x4_normed"), since("x4_normed", b + 1))
                for half in range(2):
                    transposes(2 * b + half, [merge[:, b, 0, (4 * half + n) * P:(4 * half + n + 1) * P] for n in range(4)], "x4_turned")
            pe.wait_ge(sig("h4_ready"), since("h4_ready", 4))
            n = N_GRP + N_EXP
            for b in range(NB):
                for k in range(KT):
                    m = pe.matmul(ps[:, 4, b * n:(b + 1) * n], hT[:, k, b * P:(b + 1) * P], w_route[:, k, :], start=(k == 0), stop=(k == KT - 1))
            m.then_inc(sig("logits_made"), 1)
            pe.wait_ge(sig("chosen_ready"), since("chosen_ready", 1))
            pe.matmul(ps[:, 3, 0:32], sq(RANK), chosen[:, 0, :], start=True, stop=True)
            pe.matmul(ps[:, 3, 32:64], sq(ONES), chosen[:, 0, :], start=True, stop=False)
            pe.matmul(ps[:, 3, 32:64], sq(RANK), chosen[:, 1, :], start=False, stop=True)
            pe.matmul(ps[:, 3, 64:96], sq(ONES), chosen[:, 0, :], start=True, stop=False)
            pe.matmul(ps[:, 3, 64:96], sq(ONES), chosen[:, 1, :], start=False, stop=True).then_inc(sig("ranks_made"), 1)
            gather, turn_item_rows, item_gate_up, turn_gate_up, item_down, scatter = item_steps(pe)
            pe.wait_ge(sig("zero_ready"), since("zero_ready", 1))
            for bank in range(4, 8):
                pe.matmul(ps[:, bank, :], zero, squares[:, 0:4, :].rearrange("p a n -> p (a n)"), start=True, stop=False, skip_group_check=True)

            pe.wait_ge(sig("picked"), 1)
            gather(0).then_inc(sig("gathered"), 1)
            pe.wait_ge(sig("rows_part_ready"), 1)
            turn_item_rows(0).then_inc(sig("item_rows_turned"), 1)

            def item(par, n, turn, last=False):
                pe.wait_ge(sig("hg_ready"), n + 1)
                for k in range(2):
                    pe.wait_ge(sig(f"item{par}_{k}_loaded"), 16 * turn)
                item_gate_up(par, ITEM_SLOTS[par]).then_inc(sig("item_gu_made"), 1)
                if not last:
                    pe.wait_ge(sig("picked"), n + 2)
                    gather(1 - par).then_inc(sig("gathered"), 1)
                pe.wait_ge(sig("gu_part_ready"), n + 1)
                turn_gate_up(par).then_inc(sig("gate_up_turned"), 1)
                if not last:
                    pe.wait_ge(sig("rows_part_ready"), n + 2)
                    turn_item_rows(1 - par).then_inc(sig("item_rows_turned"), 1)
                pe.wait_ge(sig("act_ready"), n + 1)
                if not last:
                    pe.wait_ge(sig("hg_ready"), n + 2)
                pe.wait_ge(sig(f"item{par}_2_loaded"), 16 * turn)
                item_down(ITEM_SLOTS[par][2]).then_inc(sig("item_down_made"), 1)
                pe.wait_ge(sig("pickT_ready"), n + 1)
                pe.wait_ge(sig("down_scalar"), n + 1)
                pe.wait_ge(sig("down_vector"), n + 1)
                scatter(False, last).then_inc(sig("scattered"), 1)

            with pe.Fori(0, N_EXP // 2 - 1) as i:
                for par in range(2):
                    item(par, 2 * i + par, i + 1)
            item(0, N_EXP - 2, N_EXP // 2)
            item(1, N_EXP - 1, N_EXP // 2, last=True)
            pe.wait_ge(sig("table_ready"), since("table_ready", 1))
            n_over = pe.value_load(table_i[0:1, 16:17], min_val=0, max_val=16)
            with pe.If(n_over > 0):
                with pe.Fori(0, n_over) as i:
                    pe.wait_ge(sig("over_vector"), 6 * i + 1)
                    gather(0).then_inc(sig("over_tensor"), 1)
                    pe.wait_ge(sig("over_vector"), 6 * i + 2)
                    turn_item_rows(0).then_inc(sig("over_tensor"), 1)
                    pe.wait_ge(sig("over_vector"), 6 * i + 3)
                    pe.wait_ge(sig("over_loaded"), 48 * i + 48)
                    item_gate_up(0, ITEM_SLOTS[0]).then_inc(sig("over_tensor"), 1)
                    pe.wait_ge(sig("over_vector"), 6 * i + 4)
                    turn_gate_up(0).then_inc(sig("over_tensor"), 1)
                    pe.wait_ge(sig("over_vector"), 6 * i + 5)
                    item_down(ITEM_SLOTS[0][2]).then_inc(sig("over_tensor"), 1)
                    pe.wait_ge(sig("over_vector"), 6 * i + 6)
                    scatter(True, True).then_inc(sig("over_tensor"), 1)

        @block.scalar
        def _(act):
            link = chain(act, "act_chain")

            def root(values, ready, n, done):
                act.wait_ge(sig(ready), since(ready, n))
                act.activation(values, values, ACT.Sqrt).then_inc(sig(done), 1)

            root(stat[:, 0:NB], "row_mean", 1, "row_root")
            act.wait_ge(sig("raw_padded"), 1)
            for pr in range(6):
                act.wait_ge(sig("qkv_projected"), pr + 1)
                act.activation(raw[:, 2 * pr:2 * pr + 2, TAPS - 1:], ps[:, 4 + pr % 4, :].rearrange("p (c t) -> p c t", t=T),
                               ACT.Copy).then_inc(sig("qkv_out"), 1)

            def columns_out(n, out, func):
                act.wait_ge(sig("projected"), n + 1)
                return act.activation(out, ps[:, n % 4, 0:out.free_size()], func)

            for b in range(NB):
                columns_out(b, silu_z[:, b, :], ACT.Silu).then_inc(sig("projected_out"), 1)
            for b in range(NB):
                act.wait_ge(sig("projected"), 3 + b)
                act.activation(nsa[:, b, 0:NSA_H, :].rearrange("p (r g) d -> p g r d", g=NSA_G),
                               ps[:, 2 + b, :].rearrange("p (g r d) -> p g r d", g=NSA_G, d=NSA_D), ACT.Copy)\
                   .then_inc(sig("projected_out"), 1)
            flat = nsa.rearrange("p b h d -> p b (h d)")
            for b in range(NB):
                columns_out(4 + b, flat[:, b, 512:1024], ACT.Copy).then_inc(sig("projected_out"), 1)
            for b in range(NB):
                act.wait_ge(sig("projected"), 7 + b)
                act.activation(flat[:, b, 1024:1280], ps[:, 2 + b, 0:256], ACT.Copy)
                act.activation(ctl[:, b, 0:28], ps[:, 2 + b, 256:284], ACT.Sigmoid)
                act.activation(ctl[:, b, 28:32], ps[:, 2 + b, 284:288], ACT.Copy).then_inc(sig("projected_out"), 1)
            act.wait_ge(sig("y_ready"), since("y_ready", 1))
            link(act.activation(sp_m, sp_y, ACT.Abs))
            link(act.activation(sp_m, sp_m, ACT.Exp, scale=-1.0))
            link(act.activation(sp_m, sp_m, ACT.Ln, bias=1.0))
            act.activation(small[:, 64:68], rows[:, R_ALOG:R_ALOG + 4], ACT.Exp).then_inc(sig("softplus_ready"), 1)
            act.wait_ge(sig("conv_ready"), since("conv_ready", 1))
            link(act.activation(convT.rearrange("p c t -> p (c t)"), convT.rearrange("p c t -> p (c t)"), ACT.Silu))
            act.activation(qkT_sq.rearrange("p c t -> p (c t)"), convT[:, 0:8, :].rearrange("p c t -> p (c t)"),
                           ACT.Square).then_inc(sig("qk_squared"), 1)
            act.wait_ge(sig("gc_ready"), since("gc_ready", 1))
            act.activation(exp_gc.rearrange("p b h n -> p b (h n)"), ps[:, 4:6, :], ACT.Exp).then_inc(sig("exp_gc_ready"), 1)
            act.wait_ge(sig("gc_out"), since("gc_out", 2))
            link(act.activation(decayT.rearrange("p b h n -> p (b h n)"), decayT.rearrange("p b h n -> p (b h n)"), ACT.Exp))
            act.activation(e_last, e_last, ACT.Exp)
            act.activation(beta_g, gc, ACT.Exp).then_inc(sig("decays_ready"), 1)
            act.wait_ge(sig("sums_out"), since("sums_out", 1))
            norms = own[:, 4:6, :]
            act.activation(norms, norms, ACT.Sqrt).then_inc(sig("norms_ready"), 1)
            for n in range(8, 16):
                branch, half, b = (n - 8) // 4, (n - 8) // 2 % 2, n % 2
                columns_out(n, merge[:, b, branch, half * BANK:(half + 1) * BANK], ACT.Sigmoid).then_inc(sig("projected_out"), 1)

            def attention_step(t):
                if t == 0:
                    for b in range(NB):
                        act.wait_ge(sig("nq_turned"), since("nq_turned", b + 1))
                        act.activation(nqT[:, :, b * P:(b + 1) * P], ps[:, 4 + b, :].rearrange("p (r t) -> p r t", t=P), ACT.Copy)\
                           .then_inc(sig("nq_ready"), 1)
                    act.wait_ge(sig("nk_turned"), since("nk_turned", 1))
                    act.activation(nkT.rearrange("p s t -> p (s t)"), ps[:, 6, :], ACT.Copy).then_inc(sig("nk_ready"), 1)
                elif t in (1, 2):
                    s = t - 1
                    act.wait_ge(sig("hid_zeroed"), since("hid_zeroed", 1))
                    act.wait_ge(sig("hid_made"), since("hid_made", s + 1))
                    act.activation(hid[:, s, :, 0:N_CMP], ps[:, 4 + s, 0:NSA_G * N_CMP].rearrange("p (g n) -> p g n", n=N_CMP),
                                   ACT.Silu).then_inc(sig("hid_ready"), 1)
                elif t == 5:
                    act.wait_ge(sig("s_cmp_ready"), 1)
                    act.activation(p_cmp, p_cmp, ACT.Exp, scale=float(NSA_D) ** -0.5).then_inc(sig("exp_cmp_ready"), 1)
                elif t == 6:
                    act.wait_ge(sig("p_cmp_turned"), 1)
                    act.activation(p_cmpT.rearrange("p b t -> p (b t)"), ps[:, 7, 0:256], ACT.Copy).then_inc(sig("p_cmpT_ready"), 1)
                elif t == 9:
                    job_exp(0)
                elif t >= FIRST_TURN and (t - FIRST_TURN) % 2 == 0:
                    q = (t - FIRST_TURN) // 2
                    n = 4 * (JOBS[q][0] + 1)
                    act.wait_ge(sig("probs_turned"), q + 1)
                    act.activation(probsT[:, 0:n, :].rearrange("p h n -> p (h n)"), ps[:, 6:6 + n // 4, :].rearrange("p b n -> p (b n)"),
                                   ACT.Copy).then_inc(sig("probsT_ready"), 1)
                    if q + 1 < N_JOB:
                        job_exp(q + 1)

            def job_exp(q):
                nk = (JOBS[q][0] + 1) * P
                act.wait_ge(sig("maxima_ready"), q + 1)
                for h in range(4):
                    p = probs[q % 2][:, h * nk:(h + 1) * nk]
                    ins = act.activation(p, p, ACT.Exp, bias=soft[:, 4 * q + h:4 * q + h + 1], scale=float(NSA_D) ** -0.5,
                                         accum_out=soft[:, 32 + 4 * q + h:33 + 4 * q + h])
                ins.then_inc(sig("probs_ready"), 1)

            for n in range(N_LEVEL):
                act.wait_ge(sig("mid_made"), n + 1)
                if n:
                    act.wait_ge(sig("inverse_ready"), n)
                act.activation(mid, pair(0), ACT.Copy).then_inc(sig("mid_ready"), 1)
                attention_step(2 * n)
                attention_step(2 * n + 1)
            act.wait_ge(sig("uw_made"), 1)
            act.wait_ge(sig("inverse_ready"), N_LEVEL)
            act.activation(uu, pair(0), ACT.Copy).then_inc(sig("uw_ready"), 1)
            act.activation(wT, pair(2), ACT.Copy).then_inc(sig("uw_ready"), 1)
            for t in range(2 * N_LEVEL, 2 * (N_LEVEL + N_CHUNK)):
                attention_step(t)
            act.wait_ge(sig("o_made"), N_CHUNK)
            link(act.activation(o_gdn, pair(2), ACT.Copy))
            act.activation(o_sq, o_gdn, ACT.Square).then_inc(sig("o_squared"), 1)
            attention_step(2 * (N_LEVEL + N_CHUNK))
            root(o_ss, "o_mean", 1, "o_root")
            for t in range(2 * (N_LEVEL + N_CHUNK) + 1, OUTPUTS_TURNED):
                attention_step(t)
            act.wait_ge(sig("o_turned"), 1)
            act.activation(oaT.rearrange("p h (b t) -> p b h t", b=NB), pair(0), ACT.Copy).then_inc(sig("oa_ready"), 1)
            for t in range(OUTPUTS_TURNED, FILL_STEPS):
                attention_step(t)
            for b in range(NB):
                act.wait_ge(sig("ob_turned"), b + 1)
                act.activation(obT[:, :, b * P:(b + 1) * P], ps[:, 2 + b, :].rearrange("p (h t) -> p h t", t=P), ACT.Copy)\
                   .then_inc(sig("ob_ready"), 1)

            def plain_out(signal_in, signal_out):
                for n in range(4):
                    b, half = n // 2, n % 2
                    act.wait_ge(sig(signal_in), since(signal_in, n + 1))
                    act.activation(hT[:, 4 * half:4 * half + 4, b * P:(b + 1) * P],
                                   ps[:, n, :].rearrange("p (k t) -> p k t", t=P), ACT.Copy).then_inc(sig(signal_out), 1)

            plain_out("merge_turned", "mergedT_ready")
            for n in range(3):
                act.wait_ge(sig("arg_ready"), since("arg_ready", n + 1))
                act.activation(act_a, arg, ACT.Sin).then_inc(sig("filt_sin"), 1)
            act.wait_ge(sig("kern_ready"), since("kern_ready", 1))
            act.activation(kern_abs.rearrange("p b d n -> p (b d n)"), kern.rearrange("p b d n -> p (b d n)"), ACT.Abs).then_inc(sig("kern_abs_ready"), 1)
            act.wait_ge(sig("kernF_made"), since("kernF_made", 1))
            act.activation(kernF.rearrange("p f n -> p (f n)"), ps[:, 0:4, :].rearrange("p f n -> p (f n)"), ACT.Copy).then_inc(sig("kernF_ready"), 1)
            root(stat[:, 0:NB], "row_mean", 2, "row_root")

            def ffn(s):
                for b in range(NB):
                    act.wait_ge(sig("gu_made"), 2 * s.n + b + 1)
                    act.activation(gated[:, s.par, b, :], ps[:, 2 * s.par + b, 0:FC], ACT.Silu).then_inc(sig("gate_ready"), 1)
                act.wait_ge(sig("gated_turned"), s.n + 1)
                act.activation(gatedT[:, s.par].rearrange("p b f n -> p b (f n)"), ps[:, 2 * s.par:2 * s.par + 2, 0:FC], ACT.Copy)\
                   .then_inc(sig("gatedT_ready"), 1)

            ffn(Step(0))
            with act.Fori(0, (N_FC - 1) // 2) as i:
                for parity in range(2):
                    ffn(Step(i=i, parity=parity))
            root(stat[:, 0:NB], "row_mean", 3, "row_root")
            root(stat[:, 0:NB], "row_mean", 4, "row_root")
            act.wait_ge(sig("u2_padded"), 1)
            for pr in range(6):
                act.wait_ge(sig("u2_projected"), pr + 1)
                act.activation(u2[:, 2 * pr:2 * pr + 2, 1:T + 1], ps[:, 4 + pr % 4, :].rearrange("p (c t) -> p c t", t=T),
                               ACT.Copy).then_inc(sig("u2_out"), 1)
            for b in range(NB):
                act.wait_ge(sig("four_projected"), since("four_projected", b + 1))
                act.activation(u_four[:, b, :], ps[:, b, :], ACT.Copy).then_inc(sig("four_ready"), 1)
            for ct in range(NHT):
                act.wait_ge(sig("four1_made"), since("four1_made", ct + 1))
                act.activation(four1[:, ct, :], ps[:, ct, :], ACT.Copy).then_inc(sig("four1_ready"), 1)
            for b in range(NB):
                act.wait_ge(sig("z_turned"), since("z_turned", b + 1))
                act.activation(z_tok[:, b, :], ps[:, 4 + b, :], ACT.Copy).then_inc(sig("z_tok_ready"), 1)
            act.wait_ge(sig("four2_made"), since("four2_made", 1))
            act.activation(y_fo, ps[:, 6:8, :].rearrange("p b (c t) -> p (b c) t", t=T), ACT.Copy).then_inc(sig("y_fo_ready"), 1)
            for f in range(4):
                act.wait_ge(sig("zF_made"), since("zF_made", f + 1))
                act.activation(zF[:, f, :], ps[:, f, :], ACT.Copy).then_inc(sig("zF_ready"), 1)
            act.wait_ge(sig("y_fo_ready"), since("y_fo_ready", 1))
            act.activation(y_sq[1], y_fo.rearrange("p c t -> p (c t)"), ACT.Square)
            act.wait_ge(sig("y_hy_ready"), since("y_hy_ready", 1))
            act.activation(y_sq[0], y_hy.rearrange("p c t -> p (c t)"), ACT.Square).then_inc(sig("y_squared"), 2)
            act.wait_ge(sig("y_mean"), since("y_mean", 1))
            act.activation(y_rs, y_rs, ACT.Sqrt).then_inc(sig("y_root"), 1)
            root(stat[:, 0:NB], "row_mean", 5, "row_root")
            act.wait_ge(sig("ex_ready"), since("ex_ready", 1))
            act.activation(ex, ex, ACT.Exp).then_inc(sig("ex_out"), 1)

            def silu_gate():
                return act.activation(silu_g.rearrange("p (c h s) -> p c h s", c=2, h=2), by_tile(ps[:, 3, 0:256])[:, :, 0:2, :], ACT.Silu)

            def rows_part_out(n):
                act.wait_ge(sig("gathered"), n + 1)
                act.activation(rows_part, ps[:, 0, 0:256], ACT.Copy).then_inc(sig("rows_part_ready"), 1)

            def item_out(n, last=False):
                act.wait_ge(sig("item_gu_made"), n + 1)
                act.activation(gu_part, ps[:, 2, 0:256], ACT.Copy).then_inc(sig("gu_part_ready"), 1)
                if not last:
                    rows_part_out(n + 1)
                act.wait_ge(sig("gate_up_turned"), n + 1)
                silu_gate().then_inc(sig("silu_g_ready"), 1)
                act.wait_ge(sig("item_down_made"), n + 1)
                act.activation(down_part[:, 0:BANK], ps[:, 1, :], ACT.Copy).then_inc(sig("down_scalar"), 1)

            rows_part_out(0)
            with act.Fori(0, N_EXP - 1) as n:
                item_out(n)
            item_out(N_EXP - 1, last=True)
            act.wait_ge(sig("table_ready"), since("table_ready", 1))
            n_over = act.value_load(table_i[0:1, 16:17], min_val=0, max_val=16)
            with act.If(n_over > 0):
                with act.Fori(0, n_over) as i:
                    act.wait_ge(sig("over_tensor"), 6 * i + 4)
                    silu_gate().then_inc(sig("over_scalar"), 1)
            root(stat[:, 0:NB], "row_mean", 6, "row_root")

        @block.vector
        def _(dve):
            link = chain(dve, "dve_chain")

            rows_scaled = [0]

            def row_scales(src, junk, ready=None):
                for b in range(NB):
                    if ready:
                        dve.wait_ge(sig(ready[0]), ready[1] + b)
                    link(dve.tensor_tensor_reduce(junk, src[:, b, :], src[:, b, :], 1.0, 0.0, ALU.mult, ALU.add, stat[:, b:b + 1]))
                dve.tensor_scalar(stat[:, 0:NB], stat[:, 0:NB], 1.0 / D, EPS, ALU.mult, ALU.add).then_inc(sig("row_mean"), 1)
                rows_scaled[0] += 1
                dve.wait_ge(sig("row_root"), rows_scaled[0])
                link(dve.reciprocal(stat[:, 0:NB], stat[:, 0:NB]))

            def turned_out(first, signal_in, signal_out, gains):
                for n in range(4):
                    b, half = n // 2, n % 2
                    dve.wait_ge(sig(signal_in), since(signal_in, n + 1))
                    dve.tensor_tensor(hT[:, 4 * half:4 * half + 4, b * P:(b + 1) * P],
                                      ps[:, n, :].rearrange("p (k t) -> p k t", t=P),
                                      spread(cols[:, gains + 4 * half:gains + 4 * half + 4], 2, P), ALU.mult)\
                       .then_inc(sig(signal_out), 1)

            dve.wait_ge(sig("x_loaded"), 16)
            row_scales(x, merge[:, 0, 1, :])
            for b in range(NB):
                dve.tensor_scalar(merge[:, b, 0, :], x[:, b, :], stat[:, b:b + 1], None, ALU.mult).then_inc(sig("x_normed"), 1)
            dve.wait_ge(sig("const_loaded"), 32)
            turned_out(0, "x_turned", "h_ready", C_MIX)

            dve.wait_ge(sig("qkv_out"), 6)
            for k in range(TAPS):
                for ct in range(CT):
                    tap = cols[:, C_CONV + k * CT + ct:C_CONV + k * CT + ct + 1]
                    src = raw[:, ct, k:k + T]
                    if k == 0:
                        ins = dve.tensor_scalar(convT[:, ct, :], src, tap, None, ALU.mult)
                    else:
                        ins = dve.scalar_tensor_tensor(convT[:, ct, :], src, tap, convT[:, ct, :], ALU.mult, ALU.add)
                if k < TAPS - 1:
                    link(ins)
            ins.then_inc(sig("conv_ready"), 1)
            dve.wait_ge(sig("projected_out"), 8)
            dve.wait_ge(sig("rows_loaded"), 16)
            dve.tensor_tensor(sp_y, ctl[:, :, 28:32], spread(rows[:, R_DT:R_DT + 4], 1, NB), ALU.add).then_inc(sig("y_ready"), 1)
            dve.wait_ge(sig("y_ready"), since("y_ready", 1))
            dve.wait_ge(sig("softplus_ready"), since("softplus_ready", 1))
            link(dve.scalar_tensor_tensor(sp_y, sp_y, 0.0, sp_m, ALU.max, ALU.add))
            link(dve.scalar_tensor_tensor(g_tok, sp_y, -1.0, spread(small[:, 64:68], 1, NB), ALU.mult, ALU.mult))
            dve.tensor_copy(g_lhs, spread(g_tok, 3, P)).then_inc(sig("g_spread"), 1)
            beta = ctl[:, :, 24:28]
            dve.tensor_copy(beta_lhs, spread(beta, 3, P)).then_inc(sig("g_spread"), 1)
            dve.wait_ge(sig("gc_ready"), since("gc_ready", 1))
            link(dve.tensor_copy(small[:, 24:40], ps[:, 0, 0:16]))
            dve.tensor_tensor(e_last, gl, gc, ALU.subtract).then_inc(sig("gc_out"), 1)
            dve.wait_ge(sig("exp_gc_ready"), since("exp_gc_ready", 1))
            for b in range(NB):
                for h in range(H_GDN):
                    ins = dve.tensor_scalar(decayT[:, b, h, :], pair(4)[:, b, h, :], gc[:, b, h:h + 1], 0.0,
                                            ALU.subtract, ALU.min)
            ins.then_inc(sig("gc_out"), 1)
            dve.wait_ge(sig("nsa_const_loaded"), 48)
            dve.wait_ge(sig("projected_out"), 8)
            tmp = [own[:, 4:6, :].rearrange("p u n -> p (u n)")[:, 320 * n:320 * n + 320]
                   .rearrange("p (b h d) -> p b h d", b=NB, h=N_HEADS64) for n in range(4)]
            for b in range(NB):
                x1, x2 = nsa[:, b, :, 0:ROPE_HALF], nsa[:, b, :, ROPE_HALF:2 * ROPE_HALF]
                dve.tensor_tensor(tmp[0][:, b], x1, rope[:, 0, b], ALU.mult)
                dve.tensor_tensor(tmp[1][:, b], x2, rope[:, 1, b], ALU.mult)
                dve.tensor_tensor(tmp[2][:, b], x2, rope[:, 0, b], ALU.mult)
                link(dve.tensor_tensor(tmp[3][:, b], x1, rope[:, 1, b], ALU.mult))
                dve.tensor_tensor(x1, tmp[0][:, b], tmp[1][:, b], ALU.subtract)
                ins = dve.tensor_tensor(x2, tmp[2][:, b], tmp[3][:, b], ALU.add)
            ins.then_inc(sig("roped"), 1)
            dve.wait_ge(sig("qk_squared"), since("qk_squared", 1))
            dve.tensor_tensor(kbT, kT, pair(6), ALU.mult).then_inc(sig("beta_used"), 1)
            dve.wait_ge(sig("qk_summed"), since("qk_summed", 1))
            sums = ps[:, 4:8, :].rearrange("p u (c t) -> p (u c) t", t=T)
            rs = own[:, 4:6, :].rearrange("p u (c t) -> p (u c) t", t=T)
            dve.tensor_scalar(rs, sums, EPS, None, ALU.add).then_inc(sig("sums_out"), 1)
            dve.wait_ge(sig("norms_ready"), since("norms_ready", 1))
            link(dve.reciprocal(rs, rs))
            dve.wait_ge(sig("beta_used"), since("beta_used", 1))
            link(dve.scalar_tensor_tensor(convT[:, 0:4, :], convT[:, 0:4, :], float(DH_GDN) ** -0.5, rs[:, 0:4, :], ALU.mult, ALU.mult))
            link(dve.tensor_tensor(convT[:, 4:8, :], convT[:, 4:8, :], rs[:, 4:8, :], ALU.mult))
            rk = own[:, 5, :].rearrange("p (h b t) -> p b h t", h=H_GDN, b=NB)
            dve.tensor_tensor(kbT, kbT, rk, ALU.mult).then_inc(sig("kb_ready"), 1)
            dve.wait_ge(sig("decays_ready"), since("decays_ready", 1))
            dve.wait_ge(sig("qk_summed"), since("qk_summed", 1))
            dve.tensor_tensor(qgT, qT, exp_gc, ALU.mult)
            flat = lambda u: u.rearrange("p b h n -> p (b h) n")
            link(dve.tensor_tensor(flat(decayT), flat(decayT), spread(sq(CUM), 1, NB * H_GDN), ALU.mult))
            link(dve.tensor_tensor(flat(decay_strict), flat(decayT), spread(sq(STRICT), 1, NB * H_GDN), ALU.mult))
            dve.wait_ge(sig("kk_ready"), since("kk_ready", 1))
            dve.tensor_tensor(aT, pair(4), decay_strict, ALU.mult).then_inc(sig("a_ready"), 1)
            dve.tensor_tensor(qk_decay, pair(6), decayT, ALU.mult).then_inc(sig("qk_ready"), 1)
            link(dve.tensor_tensor(beta_g, beta_g, beta, ALU.mult))
            dve.wait_ge(sig("kv_turned"), since("kv_turned", 1))
            for b in range(NB):
                dve.tensor_tensor(kbg[:, b], pair(4)[:, b], spread(beta_g[:, b], 2, P), ALU.mult)
                dve.tensor_tensor(kd[:, b], pair(4)[:, b], spread(e_last[:, b], 2, P), ALU.mult)
            dve.wait_ge(sig("kv_turned"), since("kv_turned", 2))
            for b in range(NB):
                ins = dve.tensor_tensor(vb[:, b], pair(6)[:, b], spread(beta[:, b], 2, P), ALU.mult)
            ins.then_inc(sig("kd_ready"), 1)
            dve.wait_ge(sig("a_ready"), since("a_ready", 1))
            dve.wait_ge(sig("inverse_started"), 2)

            gates = lambda b, kind: ctl[:, b, 0:24].rearrange("p (h k) -> p h k", k=3)[:, :, kind]
            mx, total = (soft[:, n:n + 16].rearrange("p (b h) -> p b h", b=NB) for n in (64, 80))

            def attention_step(t):
                if t == 0:
                    dve.wait_ge(sig("pairs_made"), since("pairs_made", 1))
                    made = ps[:, 7, :].rearrange("p (s g n a) -> p s g n a", s=2, g=NSA_G, a=CMP_A // 2)
                    for s in range(2):
                        for ah in range(2):
                            pos = cols[:, C_POS + s * CMP_A + 8 * ah:C_POS + s * CMP_A + 8 * ah + 8]
                            ins = dve.tensor_tensor(pairs[:, s, 8 * ah:8 * ah + 8, :, :].rearrange("p a g n -> p g n a"),
                                                    made[:, s, :, ah:ah + N_CMP, :], spread(spread(pos, 1, N_CMP), 1, NSA_G), ALU.add)
                    ins.then_inc(sig("pairs_ready"), 1)
                    dve.memset(unit[7][:, 0:64], 0.0).then_inc(sig("hid_zeroed"), 1)
                elif t == 2:
                    dve.wait_ge(sig("hid_ready"), since("hid_ready", 2))
                    dve.tensor_copy(hid_rep, spread(hid[:, 1, :, :], 2, NSA_R)).then_inc(sig("hid_rep_ready"), 1)
                elif t == 3:
                    dve.wait_ge(sig("kv_cmp_made"), since("kv_cmp_made", 1))
                    dve.tensor_copy(kcT, ps[:, 4, 64:80])
                    dve.tensor_tensor(v_cmp, spread(ps[:, 4, 128:192], 1, NSA_H), spread(cols[:, C_BLK:C_BLK + NSA_H], 2, NSA_D), ALU.mult)\
                       .then_inc(sig("kv_cmp_ready"), 1)
                elif t == 4:
                    dve.wait_ge(sig("s_cmp_made"), 1)
                    for g in range(NSA_G):
                        ins = dve.tensor_tensor(p_cmp[:, :, g * NSA_R:(g + 1) * NSA_R, :],
                                                ps[:, 5 + g, 0:NB * NSA_R * CMP_STRIDE].rearrange("p (b h n) -> p b h n", b=NB, n=CMP_STRIDE),
                                                spread(vis[:, 1], 2, NSA_R), ALU.add)
                    link(ins)
                    link(dve.tensor_reduce(mx, p_cmp, AX_X, ALU.max))
                    dve.tensor_tensor(p_cmp, p_cmp, spread(mx, 3, CMP_STRIDE), ALU.subtract).then_inc(sig("s_cmp_ready"), 1)
                elif t == 5:
                    dve.wait_ge(sig("exp_cmp_ready"), 1)
                    link(dve.tensor_reduce(total, p_cmp, AX_X, ALU.add))
                    dve.tensor_tensor(p_cmp, p_cmp, spread(vis[:, 0], 2, NSA_H), ALU.mult).then_inc(sig("p_cmp_ready"), 1)
                    link(dve.reciprocal(total, total))
                    for b in range(NB):
                        ins = dve.tensor_tensor(total[:, b], total[:, b], gates(b, 0), ALU.mult)
                    link(ins)
                elif t == 7:
                    dve.wait_ge(sig("o_cmp_made"), 1)
                    dve.tensor_tensor(o_nsa.rearrange("p b (h d) -> p b h d", d=NSA_D),
                                      ps[:, 4:6, :].rearrange("p b (h d) -> p b h d", d=NSA_D), spread(total, 3, NSA_D), ALU.mult)\
                       .then_inc(sig("o_cmp_out"), 1)
                elif t in (8, 9):
                    job_maxima(t - 8)
                elif t > FIRST_TURN and (t - FIRST_TURN) % 2:
                    q = (t - FIRST_TURN) // 2
                    job_out(q)
                    if q + 2 < N_JOB:
                        job_maxima(q + 2)

            def job_maxima(q):
                b = JOBS[q][0]
                nk = (b + 1) * P
                p = probs[q % 2][:, 0:4 * nk].rearrange("p (g r n) -> p g r n", g=NSA_G, n=nk)
                got = ps[:, 4:6, 0:2 * nk].rearrange("p g (r n) -> p g r n", n=nk)
                mine = soft[:, 4 * q:4 * q + 4]
                dve.wait_ge(sig("scores_made"), q + 1)
                if b:
                    dve.tensor_copy(p[:, :, :, 0:P], got[:, :, :, 0:P])
                dve.tensor_tensor(p[:, :, :, nk - P:nk], got[:, :, :, nk - P:nk], spread(spread(sq(CAUSAL), 1, 2), 1, NSA_G), ALU.add)\
                   .then_inc(sig("scores_out"), 1)
                dve.wait_ge(sig("scores_out"), q + 1)
                link(dve.tensor_reduce(mine, probs[q % 2][:, 0:4 * nk].rearrange("p (h n) -> p h n", n=nk), AX_X, ALU.max))
                dve.tensor_scalar(mine, mine, -float(NSA_D) ** -0.5, None, ALU.mult).then_inc(sig("maxima_ready"), 1)

            def job_out(q):
                b, kind, half = JOBS[q]
                sums = soft[:, 32 + 4 * q:36 + 4 * q]
                by_group = sums.rearrange("p (g r) -> p g r", g=NSA_G)
                gate = gates(b, 1 + kind).rearrange("p (g r) -> p g r", g=NSA_G)[:, :, 2 * half:2 * half + 2]
                dve.wait_ge(sig("probs_ready"), q + 1)
                link(dve.reciprocal(sums, sums))
                link(dve.tensor_tensor(by_group, by_group, gate, ALU.mult))
                dve.wait_ge(sig("o_job_made"), q + 1)
                dve.tensor_tensor(o_part, ps[:, 7, 0:256].rearrange("p (g r d) -> p g r d", g=NSA_G, d=NSA_D), spread(by_group, 3, NSA_D), ALU.mult)\
                   .then_inc(sig("o_job_out"), 1)
                dve.wait_ge(sig("o_job_out"), q + 1)
                into = job_heads(o_nsa[:, b, :], half)
                ins = dve.tensor_tensor(into, into, o_part, ALU.add)
                if q == N_JOB - 1:
                    ins.then_inc(sig("o_nsa_ready"), 1)
                else:
                    link(ins)

            def level_off(n):
                dve.tensor_tensor(flat(off), flat(aT), spread(sq(LEVEL0 + n), 1, NB * H_GDN), ALU.mult).then_inc(sig("off_ready"), 1)

            level_off(0)
            for n in range(N_LEVEL):
                attention_step(2 * n)
                dve.wait_ge(sig("step_made"), n + 1)
                dve.tensor_tensor(inv, inv, pair(2), ALU.subtract)
                dve.tensor_tensor(invT, invT, pair(0), ALU.subtract).then_inc(sig("inverse_ready"), 1)
                dve.wait_ge(sig("inverse_ready"), n + 1)
                if n < N_LEVEL - 1:
                    level_off(n + 1)
                attention_step(2 * n + 1)
            for c in range(N_CHUNK):
                b, r = c // 2, slice(CHUNK * (c % 2), CHUNK * (c % 2) + CHUNK)
                if c == 0:
                    dve.wait_ge(sig("uw_ready"), 1)
                    dve.tensor_copy(vnew[r, b], uu[r, b]).then_inc(sig("vnew_ready"), 1)
                else:
                    dve.wait_ge(sig("ws_made"), c)
                    dve.tensor_tensor(vnew[r, b], uu[r, b], ps[r, 0, :].rearrange("p (h n) -> p h n", h=H_GDN),
                                      ALU.subtract).then_inc(sig("vnew_ready"), 1)
                attention_step(2 * N_LEVEL + 2 * c)
                if c < N_CHUNK - 1:
                    dve.wait_ge(sig("kv_made"), c + 1)
                    if c >= 1:
                        dve.wait_ge(sig("o_made"), c)
                    for h in range(H_GDN):
                        new, add = state[:, (c + 1) % 2, h, :], ps[:, 1, h * P:(h + 1) * P]
                        if c == 0:
                            ins = dve.tensor_copy(new, add)
                        else:
                            last = exp_gc[:, b, h, r.stop - 1:r.stop]
                            ins = dve.scalar_tensor_tensor(new, state[:, c % 2, h, :], last, add, ALU.mult, ALU.add)
                    ins.then_inc(sig("state_ready"), 1)
                    dve.wait_ge(sig("state_ready"), c + 1)
                attention_step(2 * N_LEVEL + 2 * c + 1)
            attention_step(2 * (N_LEVEL + N_CHUNK))
            dve.wait_ge(sig("o_squared"), 1)
            link(dve.tensor_reduce(o_ss, o_sq, AX_X, ALU.add))
            dve.tensor_scalar(o_ss, o_ss, 1.0 / DH_GDN, EPS, ALU.mult, ALU.add).then_inc(sig("o_mean"), 1)
            attention_step(2 * (N_LEVEL + N_CHUNK) + 1)
            dve.wait_ge(sig("o_root"), 1)
            link(dve.reciprocal(o_ss, o_ss))
            link(dve.tensor_tensor(o_gdn, o_gdn, spread(o_ss, 3, P), ALU.mult))
            link(dve.tensor_tensor(flat(o_gdn), flat(o_gdn), spread(rows[:, R_ONORM:R_ONORM + P], 1, NB * H_GDN), ALU.mult))
            dve.tensor_tensor(o_gdn, o_gdn, silu_z.rearrange("p b (h n) -> p b h n", h=H_GDN), ALU.mult).then_inc(sig("o_normed"), 1)
            for t in range(2 * (N_LEVEL + N_CHUNK) + 2, FILL_STEPS):
                attention_step(t)
            halves = lambda n: ps[:, n:n + 2, :].rearrange("p h n -> p (h n)")
            dve.wait_ge(sig("branch_made"), 2)
            for b in range(NB):
                link(dve.tensor_tensor(merge[:, b, 0, :], merge[:, b, 0, :], halves(4 * b), ALU.mult))
                link(dve.tensor_tensor(merge[:, b, 1, :], merge[:, b, 1, :], halves(4 * b + 2), ALU.mult))
                dve.tensor_tensor(merge[:, b, 0, :], merge[:, b, 0, :], merge[:, b, 1, :], ALU.add).then_inc(sig("merged"), 1)
            dve.wait_ge(sig("w_out_made"), 2)
            for b in range(NB):
                link(dve.tensor_tensor(x[:, b, :], x[:, b, :], halves(4 + 2 * b), ALU.add))
            dve.sem_inc(sig("x2_added"), 1)
            for n in range(3):
                dve.wait_ge(sig("filt_layer"), since("filt_layer", n + 1))
                link(dve.tensor_scalar(arg, ps[0:64, 0, 0:T], cols[0:64, C_FB + n:C_FB + n + 1], cols[0:64, C_FREQ + n:C_FREQ + n + 1],
                                       ALU.add, ALU.mult))
                link(dve.tensor_scalar(turns_, arg, 1.0 / TWO_PI, ROUND_MAGIC, ALU.mult, ALU.add))
                link(dve.tensor_scalar(turns_, turns_, ROUND_MAGIC, None, ALU.subtract))
                for part in (TWO_PI_HI, TWO_PI_MID, TWO_PI_LO):
                    link(dve.scalar_tensor_tensor(arg, turns_, -part, arg, ALU.mult, ALU.add))
                dve.tensor_scalar(arg, arg, 3.1415925, -3.1415925, ALU.min, ALU.max).then_inc(sig("arg_ready"), 1)
                dve.wait_ge(sig("arg_ready"), since("arg_ready", n + 1))
            dve.wait_ge(sig("filt_out_made"), since("filt_out_made", 1))
            dve.tensor_tensor(kern.rearrange("p b d n -> p b d n"), ps[:, 0:4, :].rearrange("p (b d) n -> p b d n", d=2),
                              spread(decay2, 2, 2), ALU.mult).then_inc(sig("kern_ready"), 1)
            dve.wait_ge(sig("filter_turned"), since("filter_turned", 1))
            dve.reciprocal(filt_norm, ps[:, 4, 0:NHT]).then_inc(sig("filt_norm_ready"), 1)
            dve.wait_ge(sig("merged"), 2)
            row_scales(x, merge[:, 0, 1, :])
            dve.wait_ge(sig("merge_turned"), since("merge_turned", 4))
            for b in range(NB):
                dve.tensor_scalar(merge[:, b, 0, :], x[:, b, :], stat[:, b:b + 1], None, ALU.mult).then_inc(sig("x2_normed"), 1)
            turned_out(0, "x2_turned", "h2_ready", C_FFN)

            def ffn(s):
                for b in range(NB):
                    dve.wait_ge(sig("gate_ready"), 2 * s.n + b + 1)
                    ins = dve.tensor_tensor(gated[:, s.par, b, :], gated[:, s.par, b, :], ps[:, 2 * s.par + b, FC:2 * FC], ALU.mult)
                ins.then_inc(sig("gated_ready"), 1)

            ffn(Step(0))
            with dve.Fori(0, (N_FC - 1) // 2) as i:
                for parity in range(2):
                    ffn(Step(i=i, parity=parity))
            dve.wait_ge(sig("down_made"), N_FC)
            for b in range(NB):
                link(dve.tensor_tensor(x[:, b, :], x[:, b, :], halves(4 + 2 * b), ALU.add))
            row_scales(x, merge[:, 0, 1, :])
            for b in range(NB):
                link(dve.scalar_tensor_tensor(x[:, b, :], x[:, b, :], stat[:, b:b + 1], rows[:, R_FIN1:R_FIN1 + D], ALU.mult, ALU.mult))
            row_scales(x, merge[:, 0, 1, :])
            for b in range(NB):
                dve.tensor_scalar(merge[:, b, 0, :], x[:, b, :], stat[:, b:b + 1], None, ALU.mult).then_inc(sig("x3_normed"), 1)
            turned_out(0, "x3_turned", "h3_ready", C_N1)
            dve.wait_ge(sig("u2_out"), 6)
            for k in range(3):
                for ct in range(CT):
                    tap = cols[:, C_CONV2 + k * CT + ct:C_CONV2 + k * CT + ct + 1]
                    if k == 0:
                        ins = dve.tensor_scalar(conv2[:, ct, :], u2[:, ct, 0:T], tap, cols[:, C_CONVB2 + ct:C_CONVB2 + ct + 1],
                                                ALU.mult, ALU.add)
                    else:
                        ins = dve.scalar_tensor_tensor(conv2[:, ct, :], u2[:, ct, k:k + T], tap, conv2[:, ct, :], ALU.mult, ALU.add)
                link(ins)
            dve.tensor_tensor(zT, zT, conv2[:, 2 * NHT:3 * NHT, :], ALU.mult).then_inc(sig("z_ready"), 1)
            dve.wait_ge(sig("zF_ready"), since("zF_ready", 4))
            re, im = slice(0, 2), slice(2, 4)
            dve.tensor_tensor(cross, zF[:, im, :], kernF[:, im, :], ALU.mult)
            link(dve.tensor_tensor(prodF[:, re, :], zF[:, re, :], kernF[:, re, :], ALU.mult))
            link(dve.tensor_tensor(prodF[:, re, :], prodF[:, re, :], cross, ALU.subtract))
            dve.tensor_tensor(cross, zF[:, im, :], kernF[:, re, :], ALU.mult)
            link(dve.tensor_tensor(prodF[:, im, :], zF[:, re, :], kernF[:, im, :], ALU.mult))
            dve.tensor_tensor(prodF[:, im, :], prodF[:, im, :], cross, ALU.add).then_inc(sig("prod_ready"), 1)
            dve.wait_ge(sig("conv_made"), since("conv_made", 1))
            for ct in range(NHT):
                ins = dve.tensor_scalar(y_hy[:, ct, :], ps[:, 4 + ct // 2, (ct % 2) * T:(ct % 2 + 1) * T], filt_norm[:, ct:ct + 1],
                                        None, ALU.mult)
            link(ins)
            for ct in range(NHT):
                ins = dve.scalar_tensor_tensor(y_hy[:, ct, :], zT[:, ct, :], cols[:, C_FBIAS + ct:C_FBIAS + ct + 1], y_hy[:, ct, :],
                                               ALU.mult, ALU.add)
            link(ins)
            dve.tensor_tensor(y_hy, y_hy, conv2[:, 0:NHT, :], ALU.mult).then_inc(sig("y_hy_ready"), 1)
            dve.wait_ge(sig("y_summed"), since("y_summed", 1))
            dve.tensor_scalar(y_rs, ps[:, 0:4, :].rearrange("p f n -> p (f n)"), 1.0 / NSA_D, EPS, ALU.mult, ALU.add).then_inc(sig("y_mean"), 1)
            dve.wait_ge(sig("y_root"), since("y_root", 1))
            link(dve.reciprocal(y_rs, y_rs))
            for n, y in enumerate((y_hy, y_fo)):
                for ct in range(NHT):
                    gain = cols[:, C_MIXG + n * NHT + ct:C_MIXG + n * NHT + ct + 1]
                    ins = dve.scalar_tensor_tensor(y[:, ct, :], y[:, ct, :], gain, y_rs[:, (n * NHT + ct) * T:(n * NHT + ct + 1) * T],
                                                   ALU.mult, ALU.mult)
                ins.then_inc(sig("y_ready2"), 1)
            dve.wait_ge(sig("out2_made"), since("out2_made", 1))
            for b in range(NB):
                ins = dve.tensor_tensor(x[:, b, :], x[:, b, :], halves(4 + 2 * b), ALU.add)
            link(ins)
            row_scales(x, merge[:, 0, 1, :])
            for b in range(NB):
                dve.tensor_scalar(merge[:, b, 0, :], x[:, b, :], stat[:, b:b + 1], None, ALU.mult).then_inc(sig("x4_normed"), 1)
            turned_out(0, "x4_turned", "h4_ready", C_N2)
            dve.memset(zero, 0.0).then_inc(sig("zero_ready"), 1)

            def first_best(values, n, tmp, out):
                big = spread(rows[:, R_BIG:R_BIG + n], 1, NB)
                wide = lambda v: v.broadcast_to([P, NB, n])
                link(dve.tensor_reduce(best, values, AX_X, ALU.max))
                link(dve.tensor_tensor(tmp, values, wide(best), ALU.is_equal))
                link(dve.tensor_tensor(tmp, tmp, big, ALU.mult))
                link(dve.tensor_reduce(first, tmp, AX_X, ALU.min))
                link(dve.tensor_tensor(out, big, wide(first), ALU.is_equal))

            dve.wait_ge(sig("logits_made"), since("logits_made", 1))
            n = N_GRP + N_EXP
            link(dve.tensor_tensor(logits, ps[:, 4, 0:NB * n].rearrange("p (b e) -> p b e", b=NB),
                                   spread(rows[:, R_BIAS:R_BIAS + n], 1, NB), ALU.add))
            first_best(l_grp, N_GRP, eq4, one_grp)
            link(dve.tensor_tensor(ex[:, :, 0:N_GRP], l_grp, best.broadcast_to([P, NB, N_GRP]), ALU.subtract))
            in_group = lambda b: spread(one_grp[:, b, :], 2, EPG)
            by_group = lambda v, b: v[:, b, :].rearrange("p (g e) -> p g e", e=EPG)
            link(dve.tensor_scalar(eq4, one_grp, -1.0, -NEG, ALU.add, ALU.mult))
            for b in range(NB):
                link(dve.tensor_tensor(by_group(l_exp, b), by_group(l_exp, b), in_group(b), ALU.mult))
                link(dve.tensor_tensor(by_group(l_exp, b), by_group(l_exp, b), spread(eq4[:, b, :], 2, EPG), ALU.add))
            first_best(l_exp, N_EXP, eq, one1)
            link(dve.tensor_copy(second, best))
            link(dve.scalar_tensor_tensor(l_exp, one1, 2 * NEG, l_exp, ALU.mult, ALU.add))
            first_best(l_exp, N_EXP, eq, one2)
            dve.tensor_tensor(chosen, one1, one2, ALU.add).then_inc(sig("chosen_ready"), 1)
            dve.tensor_tensor(ex[:, :, N_GRP:N_GRP + 1], best, second, ALU.subtract).then_inc(sig("ex_ready"), 1)
            dve.wait_ge(sig("ex_out"), 1)
            link(dve.tensor_reduce(best, ex[:, :, 0:N_GRP], AX_X, ALU.add))
            link(dve.scalar_tensor_tensor(first, ex[:, :, N_GRP:N_GRP + 1], 1.0, best, ALU.add, ALU.mult))
            w1 = weights[:, 0:NB].rearrange("p (b e) -> p b e", e=1)
            w2 = weights[:, NB:2 * NB].rearrange("p (b e) -> p b e", e=1)
            link(dve.reciprocal(w1, first))
            link(dve.tensor_tensor(w2, w1, ex[:, :, N_GRP:N_GRP + 1], ALU.mult))
            dve.wait_ge(sig("ranks_made"), since("ranks_made", 1))
            link(dve.tensor_scalar(counts, ps[:, 3, 64:96], 1.0 / CAP, None, ALU.mult))
            link(dve.tensor_tensor(steps, spread(counts, 2, 7), spread(rows[:, R_IOTA + 1:R_IOTA + 8], 1, N_EXP), ALU.is_gt))
            link(dve.tensor_reduce(more, steps, AX_X, ALU.add))
            link(dve.tensor_copy(over_ends[0], more))
            for k in range(5):
                a, b, s = over_ends[k % 2], over_ends[(k + 1) % 2], 1 << k
                dve.tensor_copy(b[:, 0:s], a[:, 0:s])
                link(dve.tensor_tensor(b[:, s:], a[:, s:], a[:, 0:N_EXP - s], ALU.add))
            ends = over_ends[1]
            iota = rows[:, R_IOTA:R_IOTA + N_EXP]
            link(dve.tensor_tensor(base, ends, more, ALU.subtract))
            link(dve.tensor_tensor(base, base, iota, ALU.subtract))
            link(dve.tensor_scalar(base, base, float(CAP), float(CAP * (N_EXP - 1)), ALU.mult, ALU.add))
            rank = ps[:, 3, 0:64].rearrange("p (b e) -> p b e", b=NB)
            link(dve.tensor_scalar(shift, rank, float(CAP), None, ALU.is_ge))
            link(dve.tensor_tensor(shift, shift, spread(base, 1, NB), ALU.mult))
            link(dve.tensor_tensor(slot_of, rank, shift, ALU.add))
            link(dve.tensor_scalar(base, iota, float(CAP), None, ALU.mult))
            link(dve.tensor_tensor(slot_of, slot_of, spread(base, 1, NB), ALU.add))
            for n, one in enumerate((one1, one2)):
                link(dve.tensor_tensor(eq, one, slot_of, ALU.mult))
                link(dve.tensor_reduce(slots_of[:, n * NB:(n + 1) * NB], eq, AX_X, ALU.add))
            link(dve.tensor_tensor(table_cmp, spread(ends, 1, 16), spread(rows[:, R_IOTA:R_IOTA + 16], 2, N_EXP), ALU.is_le))
            link(dve.tensor_reduce(table[:, 0:16], table_cmp, AX_X, ALU.add))
            link(dve.tensor_scalar(table[:, 0:16], table[:, 0:16], float(N_EXP - 1), None, ALU.min))
            link(dve.tensor_copy(table[:, 16:17], ends[:, N_EXP - 1:N_EXP]))
            dve.tensor_copy(table_i, table).then_inc(sig("table_ready"), 1)

            def rows_out():
                return dve.tensor_tensor(hgT.rearrange("p (j c) s -> p c j s", j=4), by_tile(ps[:, 1, 0:256]),
                                         spread(cols[:, C_N2:C_N2 + KT].rearrange("p (j c) -> p c j", j=4), 3, CAP), ALU.mult)

            def activation_out():
                return dve.tensor_tensor(actT.rearrange("p (h c) s -> p c h s", h=2),
                                         silu_g.rearrange("p (c h s) -> p c h s", c=2, h=2), by_tile(ps[:, 3, 0:256])[:, :, 2:4, :], ALU.mult)

            def weights_out():
                return dve.tensor_copy(pickT.rearrange("p b t -> p (b t)"), ps[:, 3, 256:512])

            def item_rows_out(n):
                dve.wait_ge(sig("item_rows_turned"), n + 1)
                rows_out().then_inc(sig("hg_ready"), 1)

            def item_vector(par, n, picks=True, last=False):
                dve.wait_ge(sig("silu_g_ready"), n + 1)
                activation_out().then_inc(sig("act_ready"), 1)
                weights_out().then_inc(sig("pickT_ready"), 1)
                if not last:
                    item_rows_out(n + 1)
                dve.wait_ge(sig("item_down_made"), n + 1)
                dve.tensor_copy(down_part[:, BANK:], ps[:, 2, :]).then_inc(sig("down_vector"), 1)
                if picks:
                    dve.wait_ge(sig("picked"), n + 2)
                    item_picks(dve, pick_link, par).then_inc(sig("picked"), 1)

            PICK_LINKS = 3 * NB

            class Links:

                def __init__(self):
                    self.n = 0

                def __call__(self, ins):
                    self.n += 1
                    ins.then_inc(sig("pick_chain"), 1)
                    dve.wait_ge(sig("pick_chain"), self.n)

            pick_link = Links()
            item_picks(dve, pick_link, 0).then_inc(sig("picked"), 1)
            dve.wait_ge(sig("picked"), 1)
            item_picks(dve, pick_link, 1).then_inc(sig("picked"), 1)
            item_rows_out(0)
            with dve.Fori(0, N_EXP // 2 - 1) as i:
                pick_link.n = i * (2 * PICK_LINKS) + 2 * PICK_LINKS
                for par in range(2):
                    item_vector(par, 2 * i + par)
            item_vector(0, N_EXP - 2, picks=False)
            item_vector(1, N_EXP - 1, picks=False, last=True)
            dve.wait_ge(sig("scattered"), N_EXP)
            for b in range(NB):
                ins = dve.tensor_tensor(x[:, b, :], x[:, b, :], halves(4 + 2 * b), ALU.add)
            link(ins)
            dve.wait_ge(sig("picked"), N_EXP)
            dve.sem_inc(sig("over_next"), 1)
            n_over = dve.value_load(table_i[0:1, 16:17], min_val=0, max_val=16)
            over_link = Links()
            with dve.If(n_over > 0):
                with dve.Fori(0, n_over) as i:
                    over_link.n = i * PICK_LINKS + N_EXP * PICK_LINKS
                    item_picks(dve, over_link, 0).then_inc(sig("over_vector"), 1)
                    dve.wait_ge(sig("over_tensor"), 6 * i + 1)
                    dve.tensor_copy(rows_part, ps[:, 0, 0:256]).then_inc(sig("over_vector"), 1)
                    dve.wait_ge(sig("over_tensor"), 6 * i + 2)
                    rows_out().then_inc(sig("over_vector"), 1)
                    dve.wait_ge(sig("over_tensor"), 6 * i + 3)
                    dve.tensor_copy(gu_part, ps[:, 2, 0:256]).then_inc(sig("over_vector"), 1)
                    dve.wait_ge(sig("over_scalar"), i + 1)
                    weights_out()
                    activation_out().then_inc(sig("over_vector"), 1)
                    dve.wait_ge(sig("over_tensor"), 6 * i + 5)
                    dve.tensor_copy(down_part, halves(1)).then_inc(sig("over_vector"), 1)
                    dve.wait_ge(sig("over_tensor"), 6 * i + 6)
                    for b in range(NB):
                        ins = dve.tensor_tensor(x[:, b, :], x[:, b, :], halves(4 + 2 * b), ALU.add)
                    ins.then_inc(sig("over_next"), 1)
                    dve.wait_ge(sig("over_next"), i + 2)
            row_scales(x, merge[:, 0, 1, :])
            for b in range(NB):
                dve.scalar_tensor_tensor(merge[:, b, 0, :], x[:, b, :], stat[:, b:b + 1], rows[:, R_FIN2:R_FIN2 + D], ALU.mult, ALU.mult)\
                   .then_inc(sig("out_ready"), 1)


def _constants(np):
    i = np.arange(P)
    sq = np.zeros((N_SQ, P, P), np.float32)
    same = i[:, None] // CHUNK == i[None, :] // CHUNK
    sq[IDENT] = np.eye(P)
    sq[CUM] = same & (i[:, None] <= i[None, :])
    sq[SAME] = same
    sq[STRICT] = same & (i[:, None] < i[None, :])
    for n in range(N_LEVEL):
        b = 1 << n
        sq[LEVEL0 + n] = (i[:, None] // (2 * b) == i[None, :] // (2 * b)) & (i[:, None] // b % 2 == 0) & (i[None, :] // b % 2 == 1)
    sq[ONES] = 1
    d = np.arange(NSA_D)
    ang = 2 * np.pi * np.outer(d, d) / NSA_D
    for j in range(2):
        s = slice(j * NSA_D, (j + 1) * NSA_D)
        sq[DFT_C, s, s] = np.cos(ang)
        sq[DFT_S, s, s] = -np.sin(ang)
    sq[CAUSAL] = np.where(i[None, :] <= i[:, None], 0, NEG)
    sq[RANK] = i[:, None] < i[None, :]
    out = {"squares": sq.transpose(1, 0, 2)}
    t = np.arange(T, dtype=np.float64)
    w = 2 * np.pi * (t + 0.5) / (2 * T)
    wt = np.outer(t, w)
    out["dft_fwd"] = np.concatenate([np.cos(wt), -np.sin(wt)], 1).reshape(NB, P, 2 * T).transpose(1, 0, 2)
    back = np.concatenate([np.cos(wt), np.sin(wt)], 1)
    back[0] = 0
    out["dft_bwd"] = back.reshape(NB, P, 2 * T).transpose(1, 0, 2)
    inv = np.concatenate([np.cos(wt).T, -np.sin(wt).T], 0) / T
    out["dft_inv"] = inv.reshape(2 * NB, P, T).transpose(1, 0, 2)
    wt = 2 * np.pi * np.outer(t, t) / T
    both = np.concatenate([np.cos(wt), np.sin(wt)], 1) / np.sqrt(T * NSA_D)
    out["dft_time"] = both.reshape(NB, P, 2 * T).transpose(1, 0, 2)
    f32 = np.float32
    ts = np.linspace(0, 1, T, dtype=f32)[:, None]
    ww = (f32(2 * np.pi / T) * np.arange(T, dtype=f32))[:, None]
    f = np.linspace(1e-4, 15, 16, dtype=f32)[None]
    out["emb"] = np.concatenate([ts, np.cos(f * ww), -np.sin(f * ww)], 1).T
    lo, hi = np.log(1e-2) / 1.5, np.log(1e-2) / 0.3
    deltas = np.abs(np.linspace(lo, hi, DH2, dtype=f32))
    out["decay"] = np.exp(-ts * deltas).reshape(NB, P, DH2).transpose(1, 0, 2)
    freq = f32(500000.0) ** (-np.arange(ROPE_HALF, dtype=f32) / ROPE_HALF)
    a = np.arange(T, dtype=f32)[:, None] * freq
    rope = np.zeros((2, T, N_HEADS64, ROPE_HALF), f32)
    rope[0] = 1
    for h in list(range(NSA_H)) + [8, 9, 12, 13, 16, 17]:
        rope[0, :, h], rope[1, :, h] = np.cos(a), np.sin(a)
    out["rope"] = rope.reshape(2, NB, P, N_HEADS64, ROPE_HALF).transpose(2, 0, 1, 3, 4)
    vis = np.zeros((T, CMP_STRIDE), f32)
    vis[:, :N_CMP] = np.arange(N_CMP)[None] * CMP_STRIDE + CMP_BLOCK - 1 <= np.arange(T)[:, None]
    add = np.where(vis > 0, 0, NEG)
    add[:, N_CMP:] = 3 * NEG
    out["vis"] = np.stack([vis, add]).reshape(2, NB, P, CMP_STRIDE).transpose(2, 0, 1, 3)
    return {k: np.ascontiguousarray(v, np.float32) for k, v in out.items()}


def _layout(np, x):
    f = lambda n: np.asarray(x[n], np.float32)
    feat = lambda v: v.reshape(-1, P).T
    tiles = lambda w: w.reshape(w.shape[0] // P, P, w.shape[1]).transpose(1, 0, 2)
    w = f("w_in")[0]
    a = 4 * H_GDN * DH_GDN
    ctl = 2 * H_GDN
    kv = a + ctl + (NSA_H + 6 * NSA_G) * NSA_D
    cols = np.concatenate([w[:, :a], w[:, a + ctl:kv], w[:, kv:kv + 3 * NSA_H], w[:, a:a + ctl],
                           np.zeros((D, 224), np.float32), w[:, kv + 3 * NSA_H:]], 1)
    out = {"w_in": cols.reshape(KT, P, -1, BANK).transpose(2, 1, 0, 3)}
    w1 = [f(n)[0].reshape(CMP_A, 2 * NSA_D, P).transpose(1, 0, 2) for n in ("cmp_w1_k", "cmp_w1_v")]
    out["cmp_w1"] = np.stack(w1, 1)
    out["cmp_w2"] = np.stack([f("cmp_w2_k")[0], f("cmp_w2_v")[0]], 1)
    out["w_branch"] = np.stack([tiles(f("w_branch_gdn")[0]), tiles(f("w_branch_nsa")[0])])
    out["w_out"] = f("w_out")[0].reshape(KT, P, 2, BANK).transpose(2, 1, 0, 3)
    gu = f("w_gate_up")[0].reshape(KT, P, 2, N_FC, FC)
    out["w_gu"] = gu.transpose(3, 1, 0, 2, 4)
    out["w_dn"] = f("w_down")[0].reshape(N_FC, FC // P, P, D).transpose(0, 2, 1, 3)
    out["w_in2"] = f("w_in_2")[0].reshape(KT, P, -1, BANK).transpose(2, 1, 0, 3)
    out["w_out2"] = f("w_out_2")[0].reshape(KT, P, 2, BANK).transpose(2, 1, 0, 3)
    pad = lambda v: np.concatenate([v, np.zeros((P - v.shape[0],) + v.shape[1:], np.float32)])
    i = np.arange(P)
    head = (i[:, None] // CMP_STRIDE == np.arange(NSA_H)[None]).astype(np.float32)
    fold = (i[:, None] % CAP == np.arange(CAP)[None]).astype(np.float32)
    pos = [f(n)[0].reshape(CMP_A, P).T for n in ("cmp_pos_k", "cmp_pos_v")]
    one = np.ones((P, 2), np.float32)
    one[0, 1] = 0
    out["cols"] = np.concatenate(
        [feat(f(n)[0]) for n in ("mix_norm_gain", "ffn_norm_gain", "norm1_g_2", "norm2_g_2", "mix_g_2")]
        + [feat(f("gdn_conv_w")[0].reshape(-1)), feat(f("conv_w_2")[0].reshape(-1)), feat(f("conv_b_2")[0]),
           feat(f("f_bias_2")[0]), pad(np.stack([f("f_b_in_2")[0], f("f_b_mid_2")[0, 0], f("f_b_mid_2")[0, 1]], 1)),
           pad(f("f_freq_2")[0].T)] + pos + [one, head, fold], 1)
    row = np.concatenate([f("gdn_a_log")[0], f("gdn_dt_bias")[0], f("gdn_out_norm_gain")[0], f("final_norm_gain"),
                          f("final_g_2"), f("b_group_2")[0], f("b_router_2")[0].reshape(-1),
                          np.arange(64, dtype=np.float32), np.arange(N_EXP, dtype=np.float32) - 1000])
    out["rows"] = np.broadcast_to(row, (P, row.size))
    out["filt_in"] = f("f_w_in_2")[0]
    out["filt_mid"] = f("f_w_mid_2")[0].transpose(1, 0, 2)
    out["filt_out"] = f("f_w_out_2")[0]
    router = np.concatenate([f("w_group_2")[0], f("w_router_2")[0].transpose(1, 0, 2).reshape(D, N_EXP)], 1)
    out["w_route"] = tiles(router)
    gate, up = (f(n)[0].reshape(N_EXP, KT, P, DE).transpose(0, 2, 1, 3) for n in ("w_gate_2", "w_up_2"))
    down = f("w_down_2")[0].reshape(N_EXP, DE // P, P, D).transpose(0, 2, 1, 3)
    out["w_exp"] = np.stack([gate.reshape(N_EXP, P, -1), up.reshape(N_EXP, P, -1), down.reshape(N_EXP, P, -1)], 2)
    out["x"] = f("x")[0].reshape(NB, P, D).transpose(1, 0, 2)
    return {k: np.ascontiguousarray(v, np.float32) for k, v in out.items()}


def kernel(**inputs):
    import numpy as np
    import concourse.bacc as bacc
    from concourse.bass_utils import run_bass_kernel_spmd as run

    arrays = {**_constants(np), **_layout(np, inputs)}
    nc = bacc.Bacc("TRN2", target_bir_lowering=False, num_devices=1)
    dram = {k: nc.dram_tensor(k, a.shape, F32, kind="ExternalInput").ap() for k, a in arrays.items()}
    dram["out"] = nc.dram_tensor("out", (P, NB, D), F32, kind="ExternalOutput").ap()
    two_layer_program(nc, dram)
    r = run(nc, [arrays], core_ids=[0])
    return r.results[0]["out"].transpose(1, 0, 2).reshape(1, T, D)
```

```python
from contextlib import ExitStack

import concourse.bass as bass
from concourse import mybir

F32 = mybir.dt.float32
I32 = mybir.dt.int32
ALU = mybir.AluOpType
ACT = mybir.ActivationFunctionType
AX_X = mybir.AxisListType.X

P = 128
T = 256
NB = T // P
D = 1024
KT = D // P
H_GDN, DH_GDN = 4, 128
CHUNK = 64
N_CHUNK = T // CHUNK
QKV = 3 * H_GDN * DH_GDN
CT = QKV // P
TAPS = 4
NSA_H, NSA_G, NSA_D = 8, 2, 64
NSA_R = NSA_H // NSA_G
ROPE_HALF = NSA_D // 8
N_HEADS64 = NSA_H + 6 * NSA_G
CMP_BLOCK, CMP_STRIDE = 32, 16
N_CMP = (T - CMP_BLOCK) // CMP_STRIDE + 1
CMP_A = CMP_BLOCK // 2
FFN = 2816
FC = 256
N_FC = FFN // FC
DH2 = 512
NHT = DH2 // P
N_EXP, N_GRP, EPG = 32, 4, 8
DE = 512
CAP = 32
FAR = 65536.0
EPS = 1e-6
NEG = -1e30
SLOTS = 6
BANK = 512
TWO_PI = 6.283185307179586
ROUND_MAGIC = 12582912.0
TWO_PI_HI, TWO_PI_MID = 6.28125, 0.0019350051879882812
TWO_PI_LO = TWO_PI - TWO_PI_HI - TWO_PI_MID

(IDENT, CUM, SAME, STRICT, LEVEL0) = range(5)
N_LEVEL = 6
ONES = LEVEL0 + N_LEVEL
DFT_C, DFT_S, CAUSAL, RANK = range(ONES + 1, ONES + 5)
N_SQ = RANK + 1
C_MIX, C_FFN, C_N1, C_N2, C_MIXG = 0, 8, 16, 24, 32
C_CONV = 40
C_CONV2 = C_CONV + TAPS * CT
C_CONVB2 = C_CONV2 + 3 * CT
C_FBIAS = C_CONVB2 + CT
C_FB = C_FBIAS + NHT
C_FREQ = C_FB + 3
C_POS = C_FREQ + 3
C_ONE = C_POS + 2 * CMP_A
C_BLK = C_ONE + 2
C_SUM = C_BLK + NSA_H
N_COLS = C_SUM + 2 * NSA_G * N_CMP
R_ALOG, R_DT, R_ONORM = 0, 4, 8
R_FIN1 = R_ONORM + DH_GDN
R_FIN2 = R_FIN1 + D
R_BIAS = R_FIN2 + D
R_IOTA = R_BIAS + N_GRP + N_EXP
R_BIG = R_IOTA + 64
N_ROWS = R_BIG + N_EXP


SHARED = {
    "delta_vector": [("conv_ready", 1), ("y_ready", 1), ("g_spread", 2), ("gc_out", 2), ("roped", 1),
        ("beta_used", 1), ("sums_out", 1), ("kb_ready", 1), ("a_ready", 1), ("qk_ready", 1), ("kd_ready", 1)],
    "delta_scalar": [("softplus_ready", 1), ("qk_squared", 1), ("exp_gc_ready", 1), ("decays_ready", 1),
        ("norms_ready", 1)],
    "delta_tensor": [("gc_ready", 1), ("qk_summed", 1), ("kk_ready", 1), ("kv_turned", 2)],
    "rows_normed": [("x_normed", 2), ("x2_normed", 2), ("x3_normed", 2)],
    "rows_turned": [("x_turned", 4), ("merge_turned", 4), ("x2_turned", 4), ("x3_turned", 4), ("x4_turned", 4)],
    "rows_ready": [("h_ready", 4), ("h2_ready", 4), ("h3_ready", 4), ("h4_ready", 4)],
    "attn_tensor": [("nq_turned", 2), ("nk_turned", 1), ("pairs_made", 1), ("hid_made", 2), ("kv_cmp_made", 1)],
    "attn_scalar": [("nq_ready", 2), ("nk_ready", 1), ("hid_ready", 2)],
    "attn_vector": [("pairs_ready", 1), ("hid_zeroed", 1), ("hid_rep_ready", 1), ("kv_cmp_ready", 1)],
    "filter_tensor": [("filt_layer", 3), ("filt_out_made", 1), ("filter_turned", 1), ("kernF_made", 1)],
    "filter_scalar": [("filt_sin", 3), ("kern_abs_ready", 1), ("kernF_ready", 1)],
    "filter_vector": [("arg_ready", 3), ("kern_ready", 1), ("filt_norm_ready", 1)],
    "mix_tensor": [("four_projected", 2), ("four1_made", 4), ("four2_made", 1), ("fo_summed", 1), ("z_turned", 2),
        ("zF_made", 4), ("conv_made", 1), ("hy_summed", 1), ("out2_made", 2)],
    "mix_scalar": [("four_ready", 2), ("four1_ready", 4), ("y_fo_ready", 1), ("fo_squared", 1), ("fo_root", 1),
        ("z_tok_ready", 2), ("zF_ready", 4), ("hy_squared", 1), ("hy_root", 2)],
    "mix_vector": [("z_ready", 1), ("fo_mean", 1), ("fo_normed", 1), ("prod_ready", 1), ("y_hy_ready", 1), ("hy_mean", 2),
        ("hy_normed", 2)],
    "route_tensor": [("logits_made", 1), ("ranks_made", 1)],
    "route_vector": [("zero_ready", 1), ("chosen_ready", 1), ("ex_ready", 1), ("table_ready", 1)],
}
PLACE = {stage: (name, sum(n for _, n in stages[:i])) for name, stages in SHARED.items() for i, (stage, _) in enumerate(stages)}


def since(stage, n):
    return PLACE.get(stage, (stage, 0))[1] + n


class Signals:

    def __init__(self, nc, ctx):
        self.nc, self.ctx, self.known = nc, ctx, {}

    def __call__(self, name):
        name = PLACE.get(name, (name, 0))[0]
        if name not in self.known:
            self.known[name] = self.ctx.enter_context(self.nc.semaphore(name))
        return self.known[name]


def spread(ap, axis, n):
    ap = ap.unsqueeze(axis)
    shape = list(ap.shape)
    shape[axis] = n
    return ap.broadcast_to(shape)


def two_layer_program(nc, dram, dump=None):
    with ExitStack() as ctx:
        sig = Signals(nc, ctx)

        def sb(name, *shape, dt=F32):
            return ctx.enter_context(nc.sbuf_tensor("sb_" + name, [P, *shape], dt))[:]

        ps = ctx.enter_context(nc.psum_tensor("ps", [P, 8, BANK], F32))[:]

        ring = sb("ring", SLOTS, 4096)
        squares = sb("squares", N_SQ, P)
        cols = sb("cols", N_COLS)
        rows = sb("rows", N_ROWS)
        x = sb("x", NB, D)
        hT = sb("hT", KT, T)
        stat = sb("stat", 16)
        own = sb("own", 6, 1024)
        raw = sb("raw", CT, T + TAPS - 1)
        silu_z = sb("silu_z", NB, 512)
        nsa = sb("nsa", NB, N_HEADS64, NSA_D)
        merge = sb("merge", NB, 2, D)
        ctl = sb("ctl", NB, 32)
        small = sb("small", 512)

        ring_units = ring[:, 4:6, :].rearrange("p s (u n) -> p (s u) n", n=1024)
        unit = [ring_units[:, u, :] for u in range(8)] + [own[:, u, :] for u in range(6)]
        raw_flat = raw.rearrange("p c t -> p (c t)")

        per_head = lambda u: u.rearrange("p (b h n) -> p b h n", b=NB, h=H_GDN)
        convT = ring_units[:, 0:3, :].rearrange("p u (c t) -> p (u c) t", t=T)
        qkT_sq = raw.rearrange("p c t -> p (c t)")[:, 0:2048].rearrange("p (c t) -> p c t", t=T)
        qT = ring_units[:, 0, :].rearrange("p (h b t) -> p b h t", h=H_GDN, b=NB)
        kT = ring_units[:, 1, :].rearrange("p (h b t) -> p b h t", h=H_GDN, b=NB)
        vT = ring_units[:, 2, :].rearrange("p (h b t) -> p b h t", h=H_GDN, b=NB)
        kbT, qgT = per_head(unit[3]), per_head(unit[4])
        g_lhs, beta_lhs = per_head(unit[5]), per_head(unit[6])
        decay_strict, qk_decay = per_head(unit[5]), per_head(unit[6])
        decayT, exp_gc = per_head(unit[7]), per_head(unit[8])
        aT, inv, invT, off, mid = (per_head(unit[u]) for u in (9, 10, 11, 12, 13))
        kbg, kd, vb = (per_head(raw_flat[:, u * 1024:(u + 1) * 1024]) for u in range(3))
        uu, wT, vnew = per_head(unit[12]), per_head(unit[13]), per_head(unit[9])
        state = unit[2].rearrange("p (s h n) -> p s h n", s=2, h=H_GDN)
        o_gdn, o_sq = per_head(unit[10]), per_head(unit[11])
        oaT = own[:, 2, :].rearrange("p (h t) -> p h t", t=T)
        piece = lambda n, w: small[:, n:n + w].rearrange("p (b h) -> p b h", b=NB)
        sp_y, sp_m, g_tok, gc, gl = (piece(8 * n, 8) for n in range(5))
        e_last, beta_g, o_ss = (piece(8 * n, 8) for n in range(5, 8))

        pair = lambda bank: ps[:, bank:bank + 2, :].rearrange("p b (h n) -> p b h n", h=H_GDN)
        sq = lambda n: squares[:, n, :]
        ident = sq(IDENT)

        rope = sb("rope", 2, NB, N_HEADS64, ROPE_HALF)
        vis = sb("vis", 2, NB, CMP_STRIDE)
        cmp_w2 = sb("cmp_w2", 2, NSA_D)
        soft = sb("soft", 96)
        nqT = unit[0].rearrange("p (r t) -> p r t", t=T)
        nkT = unit[1][:, 0:512].rearrange("p (s t) -> p s t", t=T)
        o_part = unit[1][:, 512:768].rearrange("p (g r d) -> p g r d", g=NSA_G, d=NSA_D)
        p_cmpT = unit[1][:, 768:1024].rearrange("p (b t) -> p b t", b=NB)
        pairs_all = unit[3].rearrange("p (s a n) -> p s a n", s=2, a=CMP_A)
        pairs = pairs_all[:, :, :, 0:NSA_G * N_CMP].rearrange("p s a (g n) -> p s a g n", g=NSA_G)
        hid_part = unit[7][:, 768:896]
        probs = [unit[5], unit[3]]
        hid = unit[7][:, 0:64].rearrange("p (s g n) -> p s g n", s=2, g=NSA_G)
        hid_rep = unit[7][:, 64:192].rearrange("p (g r n) -> p g r n", g=NSA_G, r=NSA_R)
        kcT = unit[7][:, 192:224].rearrange("p (g n) -> p g n", g=NSA_G)
        v_cmp = unit[7][:, 256:768].rearrange("p (h d) -> p h d", d=NSA_D)
        p_cmp = unit[7][:, 768:1024].rearrange("p (b h n) -> p b h n", b=NB, n=CMP_STRIDE)
        hT_flat = hT.rearrange("p k t -> p (k t)")
        probsT = hT_flat[:, 0:1024].rearrange("p (h n) -> p h n", n=P)
        o_nsa = hT_flat[:, 1024:2048].rearrange("p (b n) -> p b n", b=NB)
        obT = own[:, 3, :].rearrange("p (h t) -> p h t", t=T)
        JOBS = [(b, kind, half) for b in range(NB) for kind in range(2) for half in range(2)]
        N_JOB = len(JOBS)
        FIRST_TURN = 10
        FILL_STEPS = FIRST_TURN + 2 * N_JOB
        OUTPUTS_TURNED = 2 * (N_LEVEL + N_CHUNK) + 4
        job_heads = lambda flat, half: flat.rearrange("p (g r d) -> p g r d", g=NSA_G, r=NSA_R)[:, :, 2 * half:2 * half + 2, :]

        gated = nsa.rearrange("p b h d -> p (b h d)")[:, 0:1024].rearrange("p (i b n) -> p i b n", i=2, b=NB)
        gatedT = ctx.enter_context(nc.sbuf_tensor("sb_gatedT", [P, 2, NB, FC // P, P], F32))[:]

        class Step:

            def __init__(self, n=None, i=None, parity=None):
                self.n = n if i is None else 2 * i + parity + 1
                self.par = n % 2 if i is None else (parity + 1) % 2
                self.turns = n // 2 + 1 if i is None else i + 1 + (1 if self.par == 0 else 0)

        dft = [own[:, u, :].rearrange("p (b n) -> p b n", b=NB) for u in (0, 1, 3)]
        dft_fwd, dft_bwd, dft_time = dft
        dft_inv = own[:, 2, :].rearrange("p (f t) -> p f t", t=T)
        decay2 = own[:, 4, :].rearrange("p (b n) -> p b n", b=NB)
        filt_out = own[0:64, 5, :]
        kernF = own[:, 4:6, :].rearrange("p u (f n) -> p (u f) n", n=DH2)
        nsa_flat = nsa.rearrange("p b h d -> p (b h d)")
        gatedT_flat = gatedT.rearrange("p i b f n -> p (i b f n)")
        emb, filt_in, filt_mid = gatedT_flat[0:33, 768:1024], small[0:33, 128:192], small[0:64, 192:320]
        w_route = sb("w_route", KT, N_GRP + N_EXP)
        kern = own[:, 4:6, :].rearrange("p d (b n) -> p d b n", b=NB)
        kern_abs = ring_units[:, 2:4, :].rearrange("p d (b n) -> p d b n", b=NB)
        arg, turns_, act_a = (gatedT_flat[0:64, n * T:(n + 1) * T] for n in range(3))
        filt_norm = small[:, 72:76]
        u2 = raw_flat[:, 0:CT * (T + 2)].rearrange("p (c t) -> p c t", t=T + 2)
        merge_flat = merge.rearrange("p b i n -> p (b i n)")
        m_unit = [merge_flat[:, n * 1024:(n + 1) * 1024] for n in range(4)]
        conv2 = merge_flat[:, 0:CT * T].rearrange("p (c t) -> p c t", t=T)
        zT = m_unit[1].rearrange("p (c t) -> p c t", t=T)
        z_tok = m_unit[3].rearrange("p (b n) -> p b n", b=NB)
        u_four = silu_z
        four1 = nsa_flat[:, 0:2048].rearrange("p (c n) -> p c n", n=2 * T)
        zF = nsa_flat[:, 0:2048].rearrange("p (f n) -> p f n", n=DH2)
        prodF = hT.rearrange("p k t -> p (k t)").rearrange("p (f n) -> p f n", n=DH2)
        cross = gatedT.rearrange("p i b f n -> p (i b f n)").rearrange("p (f n) -> p f n", n=DH2)
        y_hy = own[:, 1, :].rearrange("p (c t) -> p c t", t=T)
        y_fo = silu_z.rearrange("p b n -> p (b n)").rearrange("p (c t) -> p c t", t=T)
        y_sq_hy, y_sq_fo = m_unit[2], m_unit[3]
        root_hy, root_fo = m_unit[3], gatedT_flat

        route = lambda n, w: raw_flat[:, n:n + w].rearrange("p (b e) -> p b e", b=NB)
        logits = route(0, 72)
        l_grp, l_exp = logits[:, :, 0:N_GRP], logits[:, :, N_GRP:]
        eq4, one_grp, eq, one1, one2, chosen = route(72, 8), route(80, 8), route(88, 64), route(152, 64), route(216, 64), route(280, 64)
        best = route(344, 2)
        ex = route(352, 10)
        shift, slot_of = route(368, 64), route(432, 64)
        vec = lambda n, w: raw_flat[:, n:n + w]
        over_ends = [vec(500, N_EXP), vec(532, N_EXP)]
        more, counts, base = vec(564, N_EXP), vec(596, N_EXP), vec(628, N_EXP)
        steps = vec(660, 7 * N_EXP).rearrange("p (e m) -> p e m", m=7)
        table_cmp = vec(900, 16 * N_EXP).rearrange("p (i e) -> p i e", e=N_EXP)
        table = vec(1420, 17)
        first, second = vec(1440, NB).rearrange("p (b e) -> p b e", e=1), vec(1442, NB).rearrange("p (b e) -> p b e", e=1)
        slots_of = vec(1444, 2 * NB)
        weights = vec(1448, 2 * NB)
        slots_beyond = vec(1452, 2 * NB)
        rank_count = vec(1456, 96)
        table_i = sb("table_i", 17, dt=I32)
        xn = merge[:, :, 0, :]
        rows_part, gu_part = (own[:, 0, n * 256:(n + 1) * 256] for n in range(2))
        down_part = own[:, 2, :]
        hgT = own[:, 1, 0:256].rearrange("p (k c) -> p k c", c=CAP)
        pick = [own[:, 3, 512 + 64 * n:576 + 64 * n].rearrange("p (b c) -> p b c", b=NB) for n in range(2)]
        pick_tmp = [own[:, 3, 640 + 32 * n:672 + 32 * n] for n in range(3 * NB)]
        zero = own[:, 3, 832:960]
        pick4 = [own[:, 4, 256 * n:256 * (n + 1)].rearrange("p (b j c) -> p b j c", b=NB, j=4) for n in range(2)]
        pickT = [own[:, 5, 256 * n:256 * (n + 1)].rearrange("p (b t) -> p b t", b=NB) for n in range(2)]
        silu_g = own[:, 4, 768:896]
        actT = own[:, 4, 896:1024].rearrange("p (f c) -> p f c", c=CAP)
        by_tile = lambda turned: turned.rearrange("p (c j s) -> p c j s", c=2, j=4)
        ITEM_SLOTS = ((4, 5, 3), (1, 0, 2))
        FIRST_SLOTS = (3, 4, 5)
        SPARE_ITEM = 2
        SPARE = ([nsa_flat[:, k * DE:(k + 1) * DE] for k in range(5)] + [raw_flat[:, 1556 + k * DE:1556 + (k + 1) * DE] for k in range(3)],
                 [m_unit[1][:, 0:DE], m_unit[1][:, DE:], m_unit[3][:, 0:DE], m_unit[3][:, DE:], gatedT_flat[:, 0:DE], gatedT_flat[:, DE:],
                  silu_z[:, 0, :], silu_z[:, 1, :]])

        def gate_up_tiles(slots):
            return [[ring[:, slot, k * DE:(k + 1) * DE] for k in range(KT)] for slot in slots[0:2]]

        def item_steps(pe):

            def group(j):
                return slice(CAP * j, CAP * (j + 1))

            def gather(par):
                for b in range(NB):
                    for j in range(4):
                        m = pe.matmul(ps[group(j), 0, 0:256], pick[par][:, b, :], xn[:, b, j * 256:(j + 1) * 256],
                                      start=(b == 0), stop=(b == NB - 1))
                return m

            def turn(bank, part):
                for c in range(2):
                    m = pe.transpose(ps[:, bank, c * P:(c + 1) * P], part[:, c * P:(c + 1) * P], ident)
                return m

            def turn_rows():
                return turn(1, rows_part)

            def gate_up(w):
                for k in range(KT):
                    for j in range(4):
                        m = pe.matmul(ps[group(j), 2, 0:256], hgT[:, k, :], w[j // 2][k][:, (j % 2) * 256:(j % 2 + 1) * 256],
                                      start=(k == 0), stop=(k == KT - 1))
                return m

            def turn_gate_up(par):
                turn(3, gu_part)
                for b in range(NB):
                    m = pe.transpose(ps[:, 3, 256 + b * P:256 + (b + 1) * P], pick4[par][:, b].rearrange("p j c -> p (j c)"), ident)
                return m

            def down(slot):
                w = ring[:, slot, :].rearrange("p (f n) -> p f n", n=D)
                for half in range(2):
                    for j in range(4):
                        m = pe.matmul(ps[group(j), half, :], actT[:, j, :], w[:, j, half * BANK:(half + 1) * BANK],
                                      start=True, stop=True)
                return m

            def scatter(par, start, stop, signal=None):
                for b in range(NB):
                    for half in range(2):
                        m = pe.matmul(ps[:, 4 + 2 * b + half, :], pickT[par][:, b, :], down_part[:, half * BANK:(half + 1) * BANK],
                                      start=start, stop=stop, skip_group_check=True)
                    if signal:
                        m.then_inc(sig(signal), 1)
                return m
            return gather, turn_rows, gate_up, turn_gate_up, down, scatter

        def item_picks(dve, link, par):
            iota = rows[:, R_IOTA:R_IOTA + CAP]
            for b in range(NB):
                hit, hit_w, other_w = pick_tmp[3 * b:3 * b + 3]
                dve.tensor_scalar(hit, iota, slots_of[:, b:b + 1], None, ALU.is_equal)
                link(dve.tensor_scalar(hit_w, iota, slots_of[:, b:b + 1], weights[:, b:b + 1], ALU.is_equal, ALU.mult))
                at = NB + b
                dve.scalar_tensor_tensor(pick[par][:, b, :], iota, slots_of[:, at:at + 1], hit, ALU.is_equal, ALU.add)
                link(dve.tensor_scalar(other_w, iota, slots_of[:, at:at + 1], weights[:, at:at + 1], ALU.is_equal, ALU.mult))
                link(dve.tensor_tensor(hit_w, hit_w, other_w, ALU.add))
                dve.tensor_copy(pick4[par][:, b], spread(hit_w, 1, 4))
            return dve.tensor_scalar(slots_of, slots_of, -float(CAP), None, ALU.add)

        block = ctx.enter_context(nc.Block())
        IN2_SLOTS, OUT2_SLOTS = (3, 4, 5, 1), (0, 2)
        HYENA_PAIRS = (2, 3, 4, 5, 0, 1)

        def chain(eng, name):
            count = [0]

            def link(ins):
                count[0] += 1
                ins.then_inc(sig(name), 1)
                eng.wait_ge(sig(name), count[0])
            return link

        stream = [("w_in", n) for n in range(11)] + [("cmp", 0), ("branch", 0), ("branch", 1), ("w_out", 0), ("w_out", 1)]
        where = {what: (n % 4, n // 4 + 1) for n, what in enumerate(stream)}

        def arrived(eng, what):
            slot, use = where[what]
            eng.wait_ge(sig(f"slot{slot}_loaded"), 16 * use)
            return ring[:, slot, :]

        def wait_used(eng, what):
            kind, i = what
            name, n = {"w_in": ("qkv_projected", 2 * i + 2) if i < 3 else ("projected", 2 * (i - 3) + 2), "cmp": ("hid_made", 1),
                       "branch": ("branch_made", 2 * i + 2), "w_out": ("w_out_made", i + 3)}[kind]
            eng.wait_ge(sig(name), since(name, n))

        @block.sync
        def _(sp):
            for b in range(NB):
                sp.dma_start(x[:, b, :], dram["x"][:, b, :]).then_inc(sig(f"x{b}_loaded"), 16)
            sp.dma_start(squares, dram["squares"]).then_inc(sig("const_loaded"), 16)
            sp.dma_start(cols, dram["cols"]).then_inc(sig("const_loaded"), 16)
            for n, what in enumerate(stream):
                slot, use = where[what]
                if n >= 4:
                    wait_used(sp, stream[n - 4])
                dst = ring[:, slot, :]
                kind, i = what
                if kind == "w_in" and i == 6:
                    dst = dst.rearrange("p (k n) -> p k n", n=BANK)[:, :, 0:288]
                    src = dram["w_in"][i][:, :, 0:288]
                elif kind == "w_in":
                    src = dram["w_in"][i].rearrange("p k n -> p (k n)")
                elif kind == "cmp":
                    src = dram["cmp_w1"].rearrange("p v a n -> p (v a n)")
                elif kind == "branch":
                    src = dram["w_branch"][i].rearrange("p k n -> p (k n)")
                else:
                    src = dram["w_out"][i].rearrange("p k n -> p (k n)")
                sp.dma_start(dst, src).then_inc(sig(f"slot{slot}_loaded"), 16)
                if n == 1:
                    sp.dma_start(rows, dram["rows"]).then_inc(sig("rows_loaded"), 16)
                    sp.dma_start(rope, dram["rope"]).then_inc(sig("nsa_const_loaded"), 16)
                    sp.dma_start(vis, dram["vis"]).then_inc(sig("nsa_const_loaded"), 16)
                    sp.dma_start(cmp_w2, dram["cmp_w2"]).then_inc(sig("nsa_const_loaded"), 16)
                    sp.dma_start(emb, dram["emb"]).then_inc(sig("filter_small_loaded"), 16)
                    sp.dma_start(filt_in, dram["filt_in"]).then_inc(sig("filter_small_loaded"), 16)
                    sp.dma_start(filt_mid, dram["filt_mid"].rearrange("p a n -> p (a n)")).then_inc(sig("filter_small_loaded"), 16)
                    sp.dma_start(w_route, dram["w_route"]).then_inc(sig("mix_const_loaded"), 16)
            sp.wait_ge(sig("o_made"), N_CHUNK)
            for name, dst in (("dft_fwd", own[:, 0, :]), ("dft_bwd", own[:, 1, :]), ("decay", own[:, 4, :])):
                sp.dma_start(dst, dram[name].rearrange("p a n -> p (a n)")).then_inc(sig("filter_loaded"), 16)
            sp.dma_start(filt_out, dram["filt_out"]).then_inc(sig("filter_loaded"), 16)
            wait_used(sp, ("branch", 0))

            def load_gate_up(s):
                sp.dma_start(ring[:, s.par, :], dram["w_gu"][s.n].rearrange("p k h n -> p (k h n)"))\
                  .then_inc(sig(f"gu{s.par}_loaded"), 16)

            def load_down(s):
                sp.dma_start(ring[:, 2, s.par * 2048:(s.par + 1) * 2048], dram["w_dn"][s.n].rearrange("p f n -> p (f n)"))\
                  .then_inc(sig(f"dn{s.par}_loaded"), 16)

            load_gate_up(Step(0))
            wait_used(sp, ("branch", 1))
            for name, dst in (("dft_inv", own[:, 2, :]), ("dft_time", own[:, 3, :])):
                sp.dma_start(dst, dram[name].rearrange("p a n -> p (a n)")).then_inc(sig("mix_const_loaded"), 16)
            load_gate_up(Step(1))
            wait_used(sp, ("w_out", 0))
            load_down(Step(0))
            load_down(Step(1))
            with sp.Fori(0, (N_FC - 3) // 2) as i:
                for parity in range(2):
                    s = Step(i=i, parity=parity)
                    nxt = Step(i=i, parity=parity)
                    nxt.n, nxt.par = 2 * i + parity + 2, parity
                    sp.wait_ge(sig("gu_made"), 2 * (2 * i + parity) + 2)
                    load_gate_up(nxt)
                    sp.wait_ge(sig("down_made"), 2 * i + parity + 1)
                    load_down(nxt)
            s = Step(N_FC - 1)
            sp.wait_ge(sig("gu_made"), 2 * (N_FC - 2))
            load_gate_up(s)
            sp.wait_ge(sig("down_made"), N_FC - 2)
            load_down(s)
            wait_used(sp, ("w_out", 1))
            sp.wait_ge(sig("filter_turned"), since("filter_turned", 1))
            for c, slot in enumerate(IN2_SLOTS):
                if c == 3:
                    sp.wait_ge(sig("gu_made"), 2 * (N_FC - 1))
                sp.dma_start(ring[:, slot, :], dram["w_in2"][c].rearrange("p k n -> p (k n)")).then_inc(sig(f"slot{slot}_loaded"), 16)
            for half, slot in enumerate(OUT2_SLOTS):
                sp.wait_ge(sig("gu_made" if half == 0 else "down_made"), 2 * N_FC if half == 0 else N_FC)
                sp.dma_start(ring[:, slot, :], dram["w_out2"][half].rearrange("p k n -> p (k n)")).then_inc(sig(f"slot{slot}_loaded"), 16)
            def load_part(par, expert, n, slot, signal=None):
                src = dram["w_exp"][expert].rearrange("p i n -> p (i n)")[:, n * 4096:(n + 1) * 4096] if isinstance(expert, int) \
                    else dram["w_exp"][bass.ds(expert, 1)].rearrange("e p i n -> p (e i n)")[:, n * 4096:(n + 1) * 4096]
                sp.dma_start(ring[:, slot, :], src).then_inc(sig(signal or f"item{par}_{n}_loaded"), 16)

            def load_item(par, expert, parts=range(3)):
                for n in parts:
                    if n == 0:
                        sp.wait_ge(sig("item_gu_made"), expert - 1)
                    if n == 2:
                        sp.wait_ge(sig("item_down_made"), expert - 1)
                    load_part(par, expert, n, ITEM_SLOTS[par][n])

            def load_spare(n, first, end, to):
                src = dram["w_exp"][SPARE_ITEM].rearrange("p i n -> p (i n)")[:, n * 4096 + first * DE:n * 4096 + end * DE]
                sp.dma_start(to, src).then_inc(sig("spare_loaded"), 16)

            sp.wait_ge(sig("u2_projected"), 6)
            for n, slot in enumerate(FIRST_SLOTS):
                load_part(0, 0, n, slot, "first_down_loaded" if n == 2 else None)
            load_part(1, 1, 0, ITEM_SLOTS[1][0])
            sp.wait_ge(sig("prod_ready"), since("prod_ready", 1))
            load_spare(0, 0, 5, nsa_flat[:, 0:5 * DE])
            load_spare(0, 5, 8, raw_flat[:, 1556:1556 + 3 * DE])
            load_spare(1, 4, 6, gatedT_flat)
            sp.wait_ge(sig("hy_normed"), since("hy_normed", 2))
            load_spare(1, 0, 2, m_unit[1])
            load_spare(1, 2, 4, m_unit[3])
            sp.wait_ge(sig("out2_made"), since("out2_made", 2))
            load_part(1, 1, 1, ITEM_SLOTS[1][1])
            load_part(1, 1, 2, ITEM_SLOTS[1][2])
            load_spare(1, 6, 8, silu_z.rearrange("p b n -> p (b n)"))
            sp.wait_ge(sig("item_gu_made"), 1)
            load_part(0, SPARE_ITEM, 2, ITEM_SLOTS[0][2])
            load_part(0, 4, 0, ITEM_SLOTS[0][0])
            load_item(1, 3)
            load_item(0, 4, (1, 2))
            with sp.Fori(0, (N_EXP - 6) // 2) as i:
                for k in range(2):
                    load_item(1 - k, 2 * i + 5 + k)
            load_item(1, N_EXP - 1)
            sp.wait_ge(sig("table_ready"), since("table_ready", 1))
            sp.wait_ge(sig("item_down_made"), N_EXP)
            n_over = sp.value_load(table_i[0:1, 16:17], min_val=0, max_val=16)
            with sp.If(n_over > 0):
                with sp.Fori(0, n_over) as i:
                    sp.wait_ge(sig("over_next"), i + 1)
                    expert = sp.value_load(table_i[0:1, bass.ds(i, 1)], min_val=0, max_val=N_EXP - 1)
                    for n, slot in enumerate(ITEM_SLOTS[0]):
                        sp.dma_start(ring[:, slot, :], dram["w_exp"][bass.ds(expert, 1)].rearrange("e p i n -> p (e i n)")[:, n * 4096:(n + 1) * 4096])\
                          .then_inc(sig("over_loaded"), 16)
            for b in range(NB):
                sp.wait_ge(sig("out_ready"), b + 1)
                sp.dma_start(dram["out"][:, b, :], merge[:, b, 0, :]).then_inc(sig("out_stored"), 16)
            sp.wait_ge(sig("out_stored"), 16 * NB)

        @block.gpsimd
        def _(pool):
            pool.memset(raw[:, :, 0:TAPS - 1], 0.0).then_inc(sig("raw_padded"), 1)
            pool.wait_ge(sig("const_loaded"), 32)
            for t in (inv, invT):
                pool.tensor_copy(t.rearrange("p b h n -> p (b h) n"), spread(ident, 1, NB * H_GDN)).then_inc(sig("inverse_started"), 1)
            pool.wait_ge(sig("o_normed"), 1)
            pool.memset(u2[:, :, 0:1], 0.0)
            pool.memset(u2[:, :, T + 1:T + 2], 0.0).then_inc(sig("u2_padded"), 1)

        @block.tensor
        def _(pe):
            def transposes(bank, sources, signal):
                for n, s in enumerate(sources):
                    m = pe.transpose(ps[:, bank, n * P:(n + 1) * P], s, ident)
                m.then_inc(sig(signal), 1)

            def turn_rows(tok, ready, signal):
                for b in range(NB):
                    pe.wait_ge(sig(ready), since(ready, b + 1))
                    for half in range(2):
                        transposes(2 * b + half, [tok[:, b, (4 * half + n) * P:(4 * half + n + 1) * P] for n in range(4)], signal)

            def project_block(c, b):
                w = arrived(pe, ("w_in", c)).rearrange("p (k n) -> p k n", n=BANK)
                width = 288 if c == 6 else BANK
                n = 2 * (c - 3) + b
                if n >= 4:
                    pe.wait_ge(sig("projected_out"), n - 3)
                for k in range(KT):
                    m = pe.matmul(ps[:, n % 4, 0:width], hT[:, k, b * P:(b + 1) * P], w[:, k, 0:width],
                                  start=(k == 0), stop=(k == KT - 1))
                m.then_inc(sig("projected"), 1)

            def project(c):
                for b in range(NB):
                    project_block(c, b)

            pe.wait_ge(sig("const_loaded"), 32)
            turn_rows(merge[:, :, 0, :], "x_normed", "x_turned")
            pe.wait_ge(sig("h_ready"), since("h_ready", 4))
            for c in range(3):
                w = arrived(pe, ("w_in", c)).rearrange("p (k n) -> p k n", n=BANK)
                for pr in range(2 * c, 2 * c + 2):
                    if pr >= 4:
                        pe.wait_ge(sig("qkv_out"), pr - 3)
                    for ct in (2 * pr, 2 * pr + 1):
                        for k in range(KT):
                            m = pe.matmul(ps[:, 4 + pr % 4, (ct % 2) * T:(ct % 2 + 1) * T],
                                          w[:, k, (ct % 4) * P:(ct % 4 + 1) * P], hT[:, k, :],
                                          start=(k == 0), stop=(k == KT - 1))
                    m.then_inc(sig("qkv_projected"), 1)
            for c in range(3, 8):
                project(c)

            pe.wait_ge(sig("qkv_out"), 6)
            pe.wait_ge(sig("g_spread"), since("g_spread", 2))
            for b in range(NB):
                for h in range(H_GDN):
                    pe.matmul(pair(4)[:, b, h, :], g_lhs[:, b, h, :], sq(CUM), start=True, stop=True)
                    pe.matmul(pair(6)[:, b, h, :], beta_lhs[:, b, h, :], ident, start=True, stop=True)
            pe.wait_ge(sig("projected_out"), 8)
            gt = g_tok.rearrange("p b h -> p (b h)")
            pe.matmul(ps[:, 2, 0:8], sq(CUM), gt, start=True, stop=True)
            pe.matmul(ps[:, 2, 8:16], sq(SAME), gt, start=True, stop=True).then_inc(sig("gc_ready"), 1)
            pe.wait_ge(sig("gc_out"), since("gc_out", 1))
            project(8)
            pe.wait_ge(sig("gc_out"), since("gc_out", 2))
            pe.wait_ge(sig("beta_used"), since("beta_used", 1))
            pe.wait_ge(sig("qk_squared"), since("qk_squared", 1))
            for n in range(4):
                m = pe.matmul(ps[:, 4 + n, :], sq(ONES), qkT_sq[:, 2 * n:2 * n + 2, :].rearrange("p c t -> p (c t)"),
                              start=True, stop=True)
            m.then_inc(sig("qk_summed"), 1)
            project(9)
            project_block(10, 0)
            pe.wait_ge(sig("kb_ready"), since("kb_ready", 1))
            for b in range(NB):
                for h in range(H_GDN):
                    pe.matmul(pair(4)[:, b, h, :], kT[:, b, h, :], kbT[:, b, h, :], start=True, stop=True)
                    m = pe.matmul(pair(6)[:, b, h, :], kT[:, b, h, :], qT[:, b, h, :], start=True, stop=True)
            m.then_inc(sig("kk_ready"), 1)
            project_block(10, 1)
            for n, (src, done) in enumerate(((kT, "a_ready"), (vT, "qk_ready"))):
                pe.wait_ge(sig(done), since(done, 1))
                for b in range(NB):
                    for h in range(H_GDN):
                        m = pe.transpose(pair(4 + 2 * n)[:, b, h, :], src[:, b, h, :], ident)
                m.then_inc(sig("kv_turned"), 1)
            pe.wait_ge(sig("projected_out"), 16)
            pe.wait_ge(sig("kd_ready"), since("kd_ready", 1))
            pe.wait_ge(sig("inverse_started"), 2)

            def attention_step(t):
                if t == 0:
                    pe.wait_ge(sig("roped"), since("roped", 1))
                    for b in range(NB):
                        transposes(4 + b, [nsa[:, b, 2 * r:2 * r + 2, :].rearrange("p h d -> p (h d)") for r in range(NSA_R)], "nq_turned")
                    transposes(6, [nsa[:, b, h:h + 2, :].rearrange("p h d -> p (h d)") for h in (12, 16) for b in range(NB)], "nk_turned")
                    for s in range(2):
                        for g in range(NSA_G):
                            for b in range(NB):
                                for l2 in range(2):
                                    at = (2 * s + g) * P + b * CHUNK
                                    m = pe.matmul(ps[l2 * NSA_D:(l2 + 1) * NSA_D, 7, at:at + CHUNK], nsa[:, b, 8 + 2 * s + g, :],
                                                  ident[:, l2::2], start=True, stop=True)
                    m.then_inc(sig("pairs_made"), 1)
                elif t == 1:
                    w1 = arrived(pe, ("cmp", 0)).rearrange("p (s a n) -> p s a n", s=2, a=CMP_A)
                    pe.wait_ge(sig("pairs_ready"), since("pairs_ready", 1))
                    pe.wait_ge(sig("nq_ready"), since("nq_ready", 2))
                    for i in range(CMP_A // 2):
                        for j in range(4):
                            s, a = j // 2, 2 * i + j % 2
                            m = pe.matmul(ps[32 * j:32 * (j + 1), 4, 0:P], pairs_all[:, s, a, :], w1[:, s, a, :],
                                          start=(i == 0), stop=(i == CMP_A // 2 - 1))
                    m.then_inc(sig("hid_made"), 1)
                elif t == 2:
                    pe.wait_ge(sig("hid_ready"), since("hid_ready", 1))
                    pe.matmul(ps[:, 5, 0:2 * NSA_G * N_CMP], hid_part, cols[:, C_SUM:C_SUM + 2 * NSA_G * N_CMP], start=True, stop=True)\
                      .then_inc(sig("hid_made"), 1)
                elif t == 3:
                    pe.wait_ge(sig("nsa_const_loaded"), 48)
                    pe.wait_ge(sig("hid_ready"), since("hid_ready", 2))
                    for g in range(NSA_G):
                        pe.matmul(ps[g * NSA_D:(g + 1) * NSA_D, 4, 64:80], cmp_w2[:, 0, :], hid[:, 0, g, :], start=True, stop=True)
                    pe.wait_ge(sig("hid_rep_ready"), since("hid_rep_ready", 1))
                    pe.matmul(ps[:, 4, 128:192], hid_rep.rearrange("p g r n -> p (g r n)"), cmp_w2[:, 1, :], start=True, stop=True)\
                      .then_inc(sig("kv_cmp_made"), 1)
                elif t == 4:
                    pe.wait_ge(sig("kv_cmp_ready"), since("kv_cmp_ready", 1))
                    for b in range(NB):
                        for r in range(NSA_R):
                            at = (b * NSA_R + r) * NSA_G * CMP_STRIDE
                            m = pe.matmul(ps[:, 5, at:at + NSA_G * CMP_STRIDE], nqT[:, r, b * P:(b + 1) * P],
                                          kcT.rearrange("p g n -> p (g n)"), start=True, stop=True)
                    m.then_inc(sig("s_cmp_made"), 1)
                elif t == 6:
                    pe.wait_ge(sig("p_cmp_ready"), 1)
                    transposes(7, [p_cmp[:, b].rearrange("p h n -> p (h n)") for b in range(NB)], "p_cmp_turned")
                elif t == 7:
                    pe.wait_ge(sig("p_cmpT_ready"), 1)
                    for b in range(NB):
                        m = pe.matmul(ps[:, 4 + b, :], p_cmpT[:, b, :], v_cmp.rearrange("p h d -> p (h d)"), start=True, stop=True)
                    m.then_inc(sig("o_cmp_made"), 1)
                elif t in (8, 9):
                    job_scores(t - 8)
                elif t >= FIRST_TURN and (t - FIRST_TURN) % 2 == 0:
                    job_turn((t - FIRST_TURN) // 2)
                elif t > FIRST_TURN:
                    q = (t - FIRST_TURN) // 2
                    job_output(q)
                    if q + 2 < N_JOB:
                        job_scores(q + 2)

            def job_scores(q):
                b, kind, half = JOBS[q]
                nk = (b + 1) * P
                if q:
                    pe.wait_ge(sig("scores_out"), q)
                else:
                    pe.wait_ge(sig("o_cmp_out"), 1)
                    pe.wait_ge(sig("nk_ready"), since("nk_ready", 1))
                for rr in range(2):
                    for g in range(NSA_G):
                        gp = slice(g * NSA_D, (g + 1) * NSA_D)
                        m = pe.matmul(ps[:, 4 + g, rr * nk:(rr + 1) * nk], nqT[gp, 2 * half + rr, b * P:(b + 1) * P],
                                      nkT[gp, kind, 0:nk], start=True, stop=True)
                m.then_inc(sig("scores_made"), 1)

            def job_turn(q):
                b = JOBS[q][0]
                pe.wait_ge(sig("probs_ready"), q + 1)
                if q:
                    pe.wait_ge(sig("o_job_out"), q)
                for n in range(4 * (b + 1)):
                    m = pe.transpose(ps[:, 6 + n // 4, (n % 4) * P:(n % 4 + 1) * P], probs[q % 2][:, n * P:(n + 1) * P], ident)
                m.then_inc(sig("probs_turned"), 1)

            def job_output(q):
                b, kind, half = JOBS[q]
                pe.wait_ge(sig("probsT_ready"), q + 1)
                for h in range(4):
                    for kb in range(b + 1):
                        m = pe.matmul(ps[:, 7, h * NSA_D:(h + 1) * NSA_D], probsT[:, h * (b + 1) + kb, :],
                                      nsa[:, kb, 14 + 4 * kind + h // 2, :], start=(kb == 0), stop=(kb == b))
                m.then_inc(sig("o_job_made"), 1)

            for n in range(N_LEVEL):
                for b in range(NB):
                    pe.wait_ge(sig("off_ready"), NB * n + b + 1)
                    if n:
                        pe.wait_ge(sig("inverse_ready"), NB * (n - 1) + b + 1)
                    for h in range(H_GDN):
                        m = pe.matmul(pair(0)[:, b, h, :], off[:, b, h, :], inv[:, b, h, :], start=True, stop=True)
                    m.then_inc(sig("mid_made" if n else "step_made"), 1)
                attention_step(2 * n)
                for b in range(NB if n else 0):
                    pe.wait_ge(sig("mid_ready"), NB * (n - 1) + b + 1)
                    for h in range(H_GDN):
                        pe.matmul(pair(2)[:, b, h, :], invT[:, b, h, :], mid[:, b, h, :], start=True, stop=True)
                        m = pe.matmul(pair(0)[:, b, h, :], mid[:, b, h, :], invT[:, b, h, :], start=True, stop=True)
                    m.then_inc(sig("step_made"), 1)
                attention_step(2 * n + 1)
            pe.wait_ge(sig("inverse_ready"), NB * N_LEVEL)
            for b in range(NB):
                for h in range(H_GDN):
                    pe.matmul(pair(0)[:, b, h, :], invT[:, b, h, :], vb[:, b, h, :], start=True, stop=True)
                    m = pe.matmul(pair(2)[:, b, h, :], kbg[:, b, h, :], invT[:, b, h, :], start=True, stop=True)
            m.then_inc(sig("uw_made"), 1)
            attention_step(2 * N_LEVEL)
            pe.wait_ge(sig("uw_ready"), 2)
            for c in range(N_CHUNK):
                b, r = c // 2, slice(CHUNK * (c % 2), CHUNK * (c % 2) + CHUNK)
                heads = range(H_GDN)
                if c:
                    pe.wait_ge(sig("state_ready"), c)
                    for h in heads:
                        m = pe.matmul(ps[r, 0, h * P:(h + 1) * P], wT[:, b, h, r], state[:, c % 2, h, :], start=True, stop=True)
                    m.then_inc(sig("ws_made"), 1)
                    attention_step(2 * N_LEVEL + 2 * c)
                pe.wait_ge(sig("vnew_ready"), c + 1)
                if c < N_CHUNK - 1:
                    for h in heads:
                        m = pe.matmul(ps[:, 1, h * P:(h + 1) * P], kd[r, b, h, :], vnew[r, b, h, :], start=True, stop=True)
                    m.then_inc(sig("kv_made"), 1)
                for h in heads:
                    if c:
                        pe.matmul(pair(2)[r, b, h, :], qgT[:, b, h, r], state[:, c % 2, h, :], start=True, stop=False)
                    m = pe.matmul(pair(2)[r, b, h, :], qk_decay[r, b, h, r], vnew[r, b, h, :], start=(c == 0), stop=True)
                m.then_inc(sig("o_made"), 1)
                attention_step(2 * N_LEVEL + 2 * c + 1)
            for t in range(2 * N_LEVEL + 2 * N_CHUNK, OUTPUTS_TURNED):
                attention_step(t)
            pe.wait_ge(sig("o_normed"), 1)
            for b in range(NB):
                for h in range(H_GDN):
                    m = pe.transpose(pair(0)[:, b, h, :], o_gdn[:, b, h, :], ident)
            m.then_inc(sig("o_turned"), 1)
            def project_branch(br, src, b, half):
                w = arrived(pe, ("branch", br)).rearrange("p (k n) -> p k n", n=D)
                for k in range(4):
                    m = pe.matmul(ps[:, 4 * br + 2 * b + half, :], src[:, k, b * P:(b + 1) * P],
                                  w[:, k, half * BANK:(half + 1) * BANK], start=(k == 0), stop=(k == 3))
                if half:
                    m.then_inc(sig("branch_made"), 1)

            attention_step(OUTPUTS_TURNED)
            pe.wait_ge(sig("oa_ready"), 1)
            project_branch(0, oaT, 0, 0)
            project_branch(0, oaT, 0, 1)
            attention_step(OUTPUTS_TURNED + 1)
            project_branch(0, oaT, 1, 0)
            pe.wait_ge(sig("o_nsa_ready"), 1)
            for b in range(NB):
                transposes(4 + b, [o_nsa[:, b, n * P:(n + 1) * P] for n in range(4)], "ob_turned")
            project_branch(0, oaT, 1, 1)
            pe.wait_ge(sig("ob_ready"), NB)
            for b in range(NB):
                for half in range(2):
                    project_branch(1, obT, b, half)

            def turn_merged(b):
                pe.wait_ge(sig("merged"), b + 1)
                for half in range(2):
                    transposes(2 * b + half, [merge[:, b, 0, (4 * half + n) * P:(4 * half + n + 1) * P] for n in range(4)], "merge_turned")

            def project_out(b, half):
                w = arrived(pe, ("w_out", half)).rearrange("p (k n) -> p k n", n=BANK)
                for k in range(KT):
                    m = pe.matmul(ps[:, 4 + 2 * b + half, :], hT[:, k, b * P:(b + 1) * P], w[:, k, :],
                                  start=(k == 0), stop=(k == KT - 1))
                m.then_inc(sig("w_out_made"), 1)

            turn_merged(0)
            pe.wait_ge(sig("mergedT_ready"), since("mergedT_ready", 2))
            pe.wait_ge(sig("filter_small_loaded"), 48)
            pe.matmul(ps[0:64, 0, 0:T], filt_in, emb, start=True, stop=True).then_inc(sig("filt_layer"), 1)
            project_out(0, 0)
            turn_merged(1)
            pe.wait_ge(sig("filt_sin"), since("filt_sin", 1))
            pe.matmul(ps[0:64, 0, 0:T], filt_mid[:, 0:64], act_a, start=True, stop=True).then_inc(sig("filt_layer"), 1)
            project_out(0, 1)
            pe.wait_ge(sig("mergedT_ready"), since("mergedT_ready", 4))
            pe.wait_ge(sig("filt_sin"), since("filt_sin", 2))
            pe.matmul(ps[0:64, 0, 0:T], filt_mid[:, 64:128], act_a, start=True, stop=True).then_inc(sig("filt_layer"), 1)
            project_out(1, 0)
            pe.wait_ge(sig("filt_sin"), since("filt_sin", 3))
            pe.wait_ge(sig("filter_loaded"), 64)
            for b in range(NB):
                for d in range(2):
                    m = pe.matmul(ps[:, 2 * b + d, :], act_a[:, b * P:(b + 1) * P], filt_out[:, d * DH2:(d + 1) * DH2], start=True, stop=True)
            m.then_inc(sig("filt_out_made"), 1)
            project_out(1, 1)
            pe.wait_ge(sig("kern_ready"), since("kern_ready", 1))
            pe.wait_ge(sig("kern_abs_ready"), since("kern_abs_ready", 1))
            for ct in range(NHT):
                for n in range(4):
                    b, d = n // 2, n % 2
                    one = C_ONE + (1 if (b, d) == (0, 1) else 0)
                    m = pe.matmul(ps[:, 3, ct:ct + 1], kern_abs[:, d, b, ct * P:(ct + 1) * P], cols[:, one:one + 1],
                                  start=(n == 0), stop=(n == 3))
            m.then_inc(sig("filter_turned"), 1)
            for b in range(NB):
                pe.wait_ge(sig("x2_normed"), since("x2_normed", b + 1))
                for half in range(2):
                    if (b, half) == (1, 1):
                        pe.wait_ge(sig("filt_norm_ready"), since("filt_norm_ready", 1))
                    transposes(2 * b + half, [merge[:, b, 0, (4 * half + n) * P:(4 * half + n + 1) * P] for n in range(4)], "x2_turned")

            def gate_up(s, first=False):
                pe.wait_ge(sig(f"gu{s.par}_loaded"), 16 * s.turns)
                w = ring[:, s.par, :].rearrange("p (k n) -> p k n", n=BANK)
                if not first:
                    pe.wait_ge(sig("gatedT_ready"), s.n - 1)
                for b in range(NB):
                    if first:
                        pe.wait_ge(sig("h2_ready"), since("h2_ready", 4))
                    for k in range(KT):
                        m = pe.matmul(ps[:, 2 * s.par + b, :], hT[:, k, b * P:(b + 1) * P], w[:, k, :],
                                      start=(k == 0), stop=(k == KT - 1))
                    m.then_inc(sig("gu_made"), 1)

            def down(s, start=False, stop=False):
                pe.wait_ge(sig("gated_ready"), s.n + 1)
                for b in range(NB):
                    for f in range(FC // P):
                        m = pe.transpose(ps[:, 2 * s.par + b, f * P:(f + 1) * P], gated[:, s.par, b, f * P:(f + 1) * P], ident)
                m.then_inc(sig("gated_turned"), 1)
                pe.wait_ge(sig(f"dn{s.par}_loaded"), 16 * s.turns)
                pe.wait_ge(sig("gatedT_ready"), s.n + 1)
                w = ring[:, 2, s.par * 2048:(s.par + 1) * 2048].rearrange("p (f n) -> p f n", n=D)
                for b in range(NB):
                    for half in range(2):
                        for f in range(FC // P):
                            m = pe.matmul(ps[:, 4 + 2 * b + half, :], gatedT[:, s.par, b, f, :], w[:, f, half * BANK:(half + 1) * BANK],
                                          start=start and f == 0, stop=stop and f == FC // P - 1, skip_group_check=True)
                m.then_inc(sig("down_made"), 1)

            gate_up(Step(0), first=True)
            gate_up(Step(1), first=True)
            down(Step(0), start=True)
            with pe.Fori(0, (N_FC - 3) // 2) as i:
                for parity in range(2):
                    s, nxt = Step(i=i, parity=parity), Step(i=i, parity=parity)
                    nxt.n, nxt.par, nxt.turns = 2 * i + parity + 2, parity, i + 2
                    gate_up(nxt)
                    down(s)
            gate_up(Step(N_FC - 1))
            down(Step(N_FC - 2))
            down(Step(N_FC - 1), stop=True)

            def mix_weights(slot):
                pe.wait_ge(sig(f"slot{slot}_loaded"), 16 * (len(stream) // 4 + 1 if slot < 4 else 1))

            pe.wait_ge(sig("filter_loaded"), 64)
            for f in range(4):
                for n, (mat, b, d) in enumerate(((dft_fwd, 0, 0), (dft_fwd, 1, 0), (dft_bwd, 0, 1), (dft_bwd, 1, 1))):
                    m = pe.matmul(ps[:, f, :], mat[:, b, f * P:(f + 1) * P], kern[:, d, b, :], start=(n == 0), stop=(n == 3))
            m.then_inc(sig("kernF_made"), 1)
            for b in range(NB):
                pe.wait_ge(sig("x3_normed"), since("x3_normed", b + 1))
                for half in range(2):
                    transposes(4 + 2 * b + half, [merge[:, b, 1, (4 * half + n) * P:(4 * half + n + 1) * P] for n in range(4)], "x3_turned")
            pe.wait_ge(sig("h3_ready"), since("h3_ready", 4))
            def project_fourier():
                mix_weights(IN2_SLOTS[3])
                w = ring[:, IN2_SLOTS[3], :].rearrange("p (k n) -> p k n", n=BANK)
                for b in range(NB):
                    for k in range(KT):
                        m = pe.matmul(ps[:, b, :], hT[:, k, b * P:(b + 1) * P], w[:, k, :], start=(k == 0), stop=(k == KT - 1))
                    m.then_inc(sig("four_projected"), 1)

            def project_hyena(n):
                pr = HYENA_PAIRS[n]
                slot = IN2_SLOTS[pr // 2]
                mix_weights(slot)
                w = ring[:, slot, :].rearrange("p (k n) -> p k n", n=BANK)
                if n >= 4:
                    pe.wait_ge(sig("u2_out"), n - 3)
                for i in range(2):
                    ct = 2 * pr + i
                    for k in range(KT):
                        m = pe.matmul(ps[:, 4 + n % 4, i * T:(i + 1) * T], w[:, k, (ct % 4) * P:(ct % 4 + 1) * P], hT[:, k, :],
                                      start=(k == 0), stop=(k == KT - 1))
                m.then_inc(sig("u2_projected"), 1)

            def project_mixed(banks, tiles, src, first, last):
                for b, half in banks:
                    mix_weights(OUT2_SLOTS[half])
                    w = ring[:, OUT2_SLOTS[half], :].rearrange("p (k n) -> p k n", n=BANK)
                    for k in tiles:
                        m = pe.matmul(ps[:, 4 + 2 * b + half, :], src[:, k % NHT, b * P:(b + 1) * P], w[:, k, :],
                                      start=first and k == tiles[0], stop=last and k == tiles[-1], skip_group_check=True)
                return m

            pe.wait_ge(sig("kernF_ready"), since("kernF_ready", 1))
            project_fourier()
            project_hyena(0)
            project_hyena(1)
            pe.wait_ge(sig("mix_const_loaded"), 48)
            pe.wait_ge(sig("four_ready"), since("four_ready", NB))
            for ct in range(NHT):
                for b in range(NB):
                    m = pe.matmul(ps[:, ct, :], u_four[:, b, ct * P:(ct + 1) * P], dft_time[:, b, :], start=(b == 0), stop=(b == NB - 1))
                m.then_inc(sig("four1_made"), 1)
            project_hyena(2)
            project_hyena(3)
            pe.wait_ge(sig("four1_ready"), since("four1_ready", NHT))
            for ct in range(NHT):
                at = ps[:, ct // 2, (ct % 2) * T:(ct % 2 + 1) * T]
                pe.matmul(at, sq(DFT_C), four1[:, ct, 0:T], start=True, stop=False)
                m = pe.matmul(at, sq(DFT_S), four1[:, ct, T:2 * T], start=False, stop=True)
            m.then_inc(sig("four2_made"), 1)
            project_hyena(4)
            pe.wait_ge(sig("fo_squared"), since("fo_squared", 1))
            for half in range(2):
                m = pe.matmul(ps[:, 2 + half, :], sq(SAME), y_sq_fo[:, half * BANK:(half + 1) * BANK], start=True, stop=True)
            m.then_inc(sig("fo_summed"), 1)
            project_hyena(5)
            pe.wait_ge(sig("z_ready"), since("z_ready", 1))
            pe.wait_ge(sig("u2_out"), 4)
            for b in range(NB):
                transposes(6 + b, [zT[:, ct, b * P:(b + 1) * P] for ct in range(NHT)], "z_turned")
            pe.wait_ge(sig("z_tok_ready"), since("z_tok_ready", NB))
            pe.wait_ge(sig("fo_mean"), since("fo_mean", 1))
            for f in range(4):
                for b in range(NB):
                    m = pe.matmul(ps[:, f, :], dft_fwd[:, b, f * P:(f + 1) * P], z_tok[:, b, :], start=(b == 0), stop=(b == NB - 1))
                m.then_inc(sig("zF_made"), 1)
            pe.wait_ge(sig("u2_out"), 6)
            pe.wait_ge(sig("fo_normed"), since("fo_normed", 1))
            project_mixed([(0, 0), (0, 1)], range(NHT, KT), y_fo, True, False)
            pe.wait_ge(sig("prod_ready"), since("prod_ready", 1))
            for ct in range(NHT):
                for f in range(4):
                    m = pe.matmul(ps[:, ct // 2, (ct % 2) * T:(ct % 2 + 1) * T], prodF[:, f, ct * P:(ct + 1) * P],
                                  dft_inv[:, f, :], start=(f == 0), stop=(f == 3))
            m.then_inc(sig("conv_made"), 1)
            project_mixed([(1, 0)], range(NHT, KT), y_fo, True, False)
            pe.wait_ge(sig("hy_squared"), since("hy_squared", 1))
            for half in range(2):
                m = pe.matmul(ps[:, 2 + half, :], sq(SAME), y_sq_hy[:, half * BANK:(half + 1) * BANK], start=True, stop=True)
            m.then_inc(sig("hy_summed"), 1)
            project_mixed([(1, 1)], range(NHT, KT), y_fo, True, False)
            every = [(b, half) for b in range(NB) for half in range(2)]
            pe.wait_ge(sig("hy_normed"), since("hy_normed", 1))
            project_mixed(every, range(0, 2), y_hy, False, False)
            pe.wait_ge(sig("hy_normed"), since("hy_normed", 2))
            for b in range(NB):
                project_mixed([(b, 0), (b, 1)], range(2, 4), y_hy, False, True).then_inc(sig("out2_made"), 1)

            for b in range(NB):
                pe.wait_ge(sig("x4_summed"), b + 1)
                for half in range(2):
                    transposes(2 * b + half, [x[:, b, (4 * half + n) * P:(4 * half + n + 1) * P] for n in range(4)], "x4_turned")
            pe.wait_ge(sig("x4_summed"), NB)
            n = N_GRP + N_EXP
            for b in range(NB):
                pe.wait_ge(sig("h4_ready"), since("h4_ready", 2 * b + 2))
                for k in range(KT):
                    m = pe.matmul(ps[:, 4, b * n:(b + 1) * n], hT[:, k, b * P:(b + 1) * P], w_route[:, k, :], start=(k == 0), stop=(k == KT - 1))
            m.then_inc(sig("logits_made"), 1)
            pe.wait_ge(sig("chosen_ready"), since("chosen_ready", 1))
            pe.matmul(ps[:, 3, 0:32], sq(RANK), chosen[:, 0, :], start=True, stop=True)
            pe.matmul(ps[:, 3, 32:64], sq(ONES), chosen[:, 0, :], start=True, stop=False)
            pe.matmul(ps[:, 3, 32:64], sq(RANK), chosen[:, 1, :], start=False, stop=True)
            pe.matmul(ps[:, 3, 64:96], sq(ONES), chosen[:, 0, :], start=True, stop=False)
            pe.matmul(ps[:, 3, 64:96], sq(ONES), chosen[:, 1, :], start=False, stop=True).then_inc(sig("ranks_made"), 1)
            gather, turn_item_rows, item_gate_up, turn_gate_up, item_down, scatter = item_steps(pe)
            pe.wait_ge(sig("zero_ready"), since("zero_ready", 1))
            for bank in range(4, 8):
                pe.matmul(ps[:, bank, :], zero, squares[:, 0:4, :].rearrange("p a n -> p (a n)"), start=True, stop=False, skip_group_check=True)

            pe.wait_ge(sig("picked"), 1)
            pe.wait_ge(sig("xn_ready"), NB)
            gather(0).then_inc(sig("gathered"), 1)
            pe.wait_ge(sig("rows_part_ready"), 1)
            turn_item_rows().then_inc(sig("item_rows_turned"), 1)

            def item(par, n, tiles, gu_loaded, down_slot, down_loaded, first=False, last=False):
                pe.wait_ge(sig("hg_ready"), n + 1)
                for name, count in gu_loaded:
                    pe.wait_ge(sig(name), count)
                item_gate_up(tiles).then_inc(sig("item_gu_made"), 1)
                if not last:
                    if not first:
                        pe.wait_ge(sig("down_scalar"), n)
                    pe.wait_ge(sig("picked"), n + 2)
                    gather(1 - par).then_inc(sig("gathered"), 1)
                pe.wait_ge(sig("gu_part_ready"), n + 1)
                if not first:
                    pe.wait_ge(sig("pickT_ready"), n)
                turn_gate_up(par).then_inc(sig("gate_up_turned"), 1)
                if not last:
                    if not first:
                        pe.wait_ge(sig("down_vector"), n)
                    pe.wait_ge(sig("rows_part_ready"), n + 2)
                    turn_item_rows().then_inc(sig("item_rows_turned"), 1)
                if not first:
                    to_tokens(1 - par, n - 1)
                pe.wait_ge(sig("act_ready"), n + 1)
                if not last:
                    pe.wait_ge(sig("hg_ready"), n + 2)
                pe.wait_ge(sig(down_loaded[0]), down_loaded[1])
                item_down(down_slot).then_inc(sig("item_down_made"), 1)

            def to_tokens(par, n, last=False):
                pe.wait_ge(sig("pickT_ready"), n + 1)
                pe.wait_ge(sig("down_scalar"), n + 1)
                pe.wait_ge(sig("down_vector"), n + 1)
                scatter(par, False, last, "scattered")

            def ring_item(par, n, half, last=False):
                turn = half if par == 0 else half + 1
                item(par, n, gate_up_tiles(ITEM_SLOTS[par]), [(f"item{par}_{k}_loaded", 16 * turn) for k in range(2)],
                     ITEM_SLOTS[par][2], (f"item{par}_2_loaded", 16 * turn), last=last)

            item(0, 0, gate_up_tiles(FIRST_SLOTS), [("item0_0_loaded", 16), ("item0_1_loaded", 16)], FIRST_SLOTS[2],
                 ("first_down_loaded", 16), first=True)
            ring_item(1, 1, 0)
            item(0, SPARE_ITEM, SPARE, [("spare_loaded", 96)], ITEM_SLOTS[0][2], ("item0_2_loaded", 16))
            ring_item(1, 3, 1)
            with pe.Fori(0, N_EXP // 2 - 3) as i:
                for par in range(2):
                    ring_item(par, 2 * i + 4 + par, i + 2)
            ring_item(0, N_EXP - 2, N_EXP // 2 - 1)
            ring_item(1, N_EXP - 1, N_EXP // 2 - 1, last=True)
            to_tokens(1, N_EXP - 1, last=True)
            pe.wait_ge(sig("table_ready"), since("table_ready", 1))
            n_over = pe.value_load(table_i[0:1, 16:17], min_val=0, max_val=16)
            with pe.If(n_over > 0):
                with pe.Fori(0, n_over) as i:
                    pe.wait_ge(sig("over_vector"), 6 * i + 1)
                    gather(0).then_inc(sig("over_tensor"), 1)
                    pe.wait_ge(sig("over_vector"), 6 * i + 2)
                    turn_item_rows().then_inc(sig("over_tensor"), 1)
                    pe.wait_ge(sig("over_vector"), 6 * i + 3)
                    pe.wait_ge(sig("over_loaded"), 48 * i + 48)
                    item_gate_up(gate_up_tiles(ITEM_SLOTS[0])).then_inc(sig("over_tensor"), 1)
                    pe.wait_ge(sig("over_vector"), 6 * i + 4)
                    turn_gate_up(0).then_inc(sig("over_tensor"), 1)
                    pe.wait_ge(sig("over_vector"), 6 * i + 5)
                    item_down(ITEM_SLOTS[0][2]).then_inc(sig("over_tensor"), 1)
                    pe.wait_ge(sig("over_vector"), 6 * i + 6)
                    scatter(0, True, True).then_inc(sig("over_tensor"), 1)

        @block.scalar
        def _(act):
            link = chain(act, "act_chain")

            def root(values, ready, n, done):
                act.wait_ge(sig(ready), since(ready, n))
                act.activation(values, values, ACT.Sqrt).then_inc(sig(done), 1)

            root(stat[:, 0:NB], "row_mean", 1, "row_root")
            act.wait_ge(sig("raw_padded"), 1)
            for pr in range(6):
                act.wait_ge(sig("qkv_projected"), pr + 1)
                act.activation(raw[:, 2 * pr:2 * pr + 2, TAPS - 1:], ps[:, 4 + pr % 4, :].rearrange("p (c t) -> p c t", t=T),
                               ACT.Copy).then_inc(sig("qkv_out"), 1)

            def columns_out(n, out, func):
                act.wait_ge(sig("projected"), n + 1)
                return act.activation(out, ps[:, n % 4, 0:out.free_size()], func)

            for b in range(NB):
                columns_out(b, silu_z[:, b, :], ACT.Silu).then_inc(sig("projected_out"), 1)
            for b in range(NB):
                act.wait_ge(sig("projected"), 3 + b)
                act.activation(nsa[:, b, 0:NSA_H, :].rearrange("p (r g) d -> p g r d", g=NSA_G),
                               ps[:, 2 + b, :].rearrange("p (g r d) -> p g r d", g=NSA_G, d=NSA_D), ACT.Copy)\
                   .then_inc(sig("projected_out"), 1)
            flat = nsa.rearrange("p b h d -> p b (h d)")
            for b in range(NB):
                columns_out(4 + b, flat[:, b, 512:1024], ACT.Copy).then_inc(sig("projected_out"), 1)
            for b in range(NB):
                act.wait_ge(sig("projected"), 7 + b)
                act.activation(flat[:, b, 1024:1280], ps[:, 2 + b, 0:256], ACT.Copy)
                act.activation(ctl[:, b, 0:28], ps[:, 2 + b, 256:284], ACT.Sigmoid)
                act.activation(ctl[:, b, 28:32], ps[:, 2 + b, 284:288], ACT.Copy).then_inc(sig("projected_out"), 1)
            act.wait_ge(sig("y_ready"), since("y_ready", 1))
            link(act.activation(sp_m, sp_y, ACT.Abs))
            link(act.activation(sp_m, sp_m, ACT.Exp, scale=-1.0))
            link(act.activation(sp_m, sp_m, ACT.Ln, bias=1.0))
            act.activation(small[:, 64:68], rows[:, R_ALOG:R_ALOG + 4], ACT.Exp).then_inc(sig("softplus_ready"), 1)
            act.wait_ge(sig("conv_ready"), since("conv_ready", 1))
            link(act.activation(convT.rearrange("p c t -> p (c t)"), convT.rearrange("p c t -> p (c t)"), ACT.Silu))
            act.activation(qkT_sq.rearrange("p c t -> p (c t)"), convT[:, 0:8, :].rearrange("p c t -> p (c t)"),
                           ACT.Square).then_inc(sig("qk_squared"), 1)

            def merge_gates(first, end):
                for n in range(first, end):
                    branch, half, b = (n - 8) // 4, (n - 8) // 2 % 2, n % 2
                    columns_out(n, merge[:, b, branch, half * BANK:(half + 1) * BANK], ACT.Sigmoid).then_inc(sig("projected_out"), 1)

            merge_gates(8, 10)
            act.wait_ge(sig("gc_ready"), since("gc_ready", 1))
            act.activation(exp_gc.rearrange("p b h n -> p b (h n)"), ps[:, 4:6, :], ACT.Exp).then_inc(sig("exp_gc_ready"), 1)
            act.wait_ge(sig("gc_out"), since("gc_out", 2))
            link(act.activation(decayT.rearrange("p b h n -> p (b h n)"), decayT.rearrange("p b h n -> p (b h n)"), ACT.Exp))
            act.activation(e_last, e_last, ACT.Exp)
            act.activation(beta_g, gc, ACT.Exp).then_inc(sig("decays_ready"), 1)
            merge_gates(10, 12)
            act.wait_ge(sig("sums_out"), since("sums_out", 1))
            norms = own[:, 4:6, :]
            act.activation(norms, norms, ACT.Sqrt).then_inc(sig("norms_ready"), 1)
            merge_gates(12, 16)

            def attention_step(t):
                if t == 0:
                    for b in range(NB):
                        act.wait_ge(sig("nq_turned"), since("nq_turned", b + 1))
                        act.activation(nqT[:, :, b * P:(b + 1) * P], ps[:, 4 + b, :].rearrange("p (r t) -> p r t", t=P), ACT.Copy)\
                           .then_inc(sig("nq_ready"), 1)
                    act.wait_ge(sig("nk_turned"), since("nk_turned", 1))
                    act.activation(nkT.rearrange("p s t -> p (s t)"), ps[:, 6, :], ACT.Copy).then_inc(sig("nk_ready"), 1)
                elif t == 1:
                    act.wait_ge(sig("hid_made"), since("hid_made", 1))
                    act.activation(hid_part, ps[:, 4, 0:P], ACT.Copy).then_inc(sig("hid_ready"), 1)
                elif t == 2:
                    act.wait_ge(sig("hid_zeroed"), since("hid_zeroed", 1))
                    act.wait_ge(sig("hid_made"), since("hid_made", 2))
                    act.activation(hid[:, :, :, 0:N_CMP], ps[:, 5, 0:2 * NSA_G * N_CMP].rearrange("p (s g n) -> p s g n", s=2, n=N_CMP),
                                   ACT.Silu).then_inc(sig("hid_ready"), 1)
                elif t == 5:
                    act.wait_ge(sig("s_cmp_ready"), 1)
                    act.activation(p_cmp, p_cmp, ACT.Exp, scale=float(NSA_D) ** -0.5).then_inc(sig("exp_cmp_ready"), 1)
                elif t == 6:
                    act.wait_ge(sig("p_cmp_turned"), 1)
                    act.activation(p_cmpT.rearrange("p b t -> p (b t)"), ps[:, 7, 0:256], ACT.Copy).then_inc(sig("p_cmpT_ready"), 1)
                elif t == 9:
                    job_exp(0)
                elif t >= FIRST_TURN and (t - FIRST_TURN) % 2 == 0:
                    q = (t - FIRST_TURN) // 2
                    n = 4 * (JOBS[q][0] + 1)
                    act.wait_ge(sig("probs_turned"), q + 1)
                    act.activation(probsT[:, 0:n, :].rearrange("p h n -> p (h n)"), ps[:, 6:6 + n // 4, :].rearrange("p b n -> p (b n)"),
                                   ACT.Copy).then_inc(sig("probsT_ready"), 1)
                    if q + 1 < N_JOB:
                        job_exp(q + 1)

            def job_exp(q):
                nk = (JOBS[q][0] + 1) * P
                act.wait_ge(sig("maxima_ready"), q + 1)
                for h in range(4):
                    p = probs[q % 2][:, h * nk:(h + 1) * nk]
                    ins = act.activation(p, p, ACT.Exp, bias=soft[:, 4 * q + h:4 * q + h + 1], scale=float(NSA_D) ** -0.5,
                                         accum_out=soft[:, 32 + 4 * q + h:33 + 4 * q + h])
                ins.then_inc(sig("probs_ready"), 1)

            for n in range(N_LEVEL):
                for b in range(NB if n else 0):
                    act.wait_ge(sig("mid_made"), NB * (n - 1) + b + 1)
                    act.activation(mid[:, b], pair(0)[:, b], ACT.Copy).then_inc(sig("mid_ready"), 1)
                attention_step(2 * n)
                attention_step(2 * n + 1)
            act.wait_ge(sig("uw_made"), 1)
            act.wait_ge(sig("inverse_ready"), NB * N_LEVEL)
            act.activation(uu, pair(0), ACT.Copy).then_inc(sig("uw_ready"), 1)
            act.activation(wT, pair(2), ACT.Copy).then_inc(sig("uw_ready"), 1)
            for t in range(2 * N_LEVEL, 2 * (N_LEVEL + N_CHUNK)):
                attention_step(t)
            act.wait_ge(sig("o_made"), N_CHUNK)
            link(act.activation(o_gdn, pair(2), ACT.Copy))
            act.activation(o_sq, o_gdn, ACT.Square).then_inc(sig("o_squared"), 1)
            attention_step(2 * (N_LEVEL + N_CHUNK))
            root(o_ss, "o_mean", 1, "o_root")
            for t in range(2 * (N_LEVEL + N_CHUNK) + 1, OUTPUTS_TURNED):
                attention_step(t)
            act.wait_ge(sig("o_turned"), 1)
            act.activation(oaT.rearrange("p h (b t) -> p b h t", b=NB), pair(0), ACT.Copy).then_inc(sig("oa_ready"), 1)
            for t in range(OUTPUTS_TURNED, FILL_STEPS):
                attention_step(t)
            for b in range(NB):
                act.wait_ge(sig("ob_turned"), b + 1)
                act.activation(obT[:, :, b * P:(b + 1) * P], ps[:, 4 + b, :].rearrange("p (h t) -> p h t", t=P), ACT.Copy)\
                   .then_inc(sig("ob_ready"), 1)

            def plain_out(signal_in, signal_out):
                for n in range(4):
                    b, half = n // 2, n % 2
                    act.wait_ge(sig(signal_in), since(signal_in, n + 1))
                    act.activation(hT[:, 4 * half:4 * half + 4, b * P:(b + 1) * P],
                                   ps[:, n, :].rearrange("p (k t) -> p k t", t=P), ACT.Copy).then_inc(sig(signal_out), 1)

            plain_out("merge_turned", "mergedT_ready")
            for n in range(3):
                act.wait_ge(sig("arg_ready"), since("arg_ready", n + 1))
                act.activation(act_a, arg, ACT.Sin).then_inc(sig("filt_sin"), 1)
            act.wait_ge(sig("kern_ready"), since("kern_ready", 1))
            act.activation(kern_abs.rearrange("p d b n -> p (d b n)"), kern.rearrange("p d b n -> p (d b n)"), ACT.Abs).then_inc(sig("kern_abs_ready"), 1)
            root(stat[:, 0:NB], "row_mean", 2, "row_root")

            def ffn(s):
                for b in range(NB):
                    act.wait_ge(sig("gu_made"), 2 * s.n + b + 1)
                    act.activation(gated[:, s.par, b, :], ps[:, 2 * s.par + b, 0:FC], ACT.Silu).then_inc(sig("gate_ready"), 1)
                act.wait_ge(sig("gated_turned"), s.n + 1)
                act.activation(gatedT[:, s.par].rearrange("p b f n -> p b (f n)"), ps[:, 2 * s.par:2 * s.par + 2, 0:FC], ACT.Copy)\
                   .then_inc(sig("gatedT_ready"), 1)

            ffn(Step(0))
            with act.Fori(0, (N_FC - 1) // 2) as i:
                for parity in range(2):
                    ffn(Step(i=i, parity=parity))
            for src, ready, total in ((x[:, 0, :], 1, 0), (merge[:, 0, 0, :], 2, 4), (x[:, 1, :], 3, 1)):
                act.wait_ge(sig("x3_step"), ready)
                if ready > 1:
                    act.wait_ge(sig("x3_squared"), ready - 1)
                act.activation(hT_flat[:, 0:1024], src, ACT.Square, accum_out=stat[:, total:total + 1]).then_inc(sig("x3_squared"), 1)
            root(stat[:, 0:NB], "row_mean", 3, "row_root")
            root(stat[:, 4:4 + NB], "row_mean", 4, "row_root")
            act.wait_ge(sig("kernF_made"), since("kernF_made", 1))
            act.activation(kernF.rearrange("p f n -> p (f n)"), ps[:, 0:4, :].rearrange("p f n -> p (f n)"), ACT.Copy).then_inc(sig("kernF_ready"), 1)
            for b in range(NB):
                act.activation(x[:, b, :], merge[:, b, 0, :], ACT.Copy, scale=stat[:, b:b + 1]).then_inc(sig("x3_ready"), 1)
            act.wait_ge(sig("u2_padded"), 1)

            def hyena_out(n):
                pr = HYENA_PAIRS[n]
                act.wait_ge(sig("u2_projected"), n + 1)
                act.activation(u2[:, 2 * pr:2 * pr + 2, 1:T + 1], ps[:, 4 + n % 4, :].rearrange("p (c t) -> p c t", t=T),
                               ACT.Copy).then_inc(sig("u2_out"), 1)

            for b in range(NB):
                act.wait_ge(sig("four_projected"), since("four_projected", b + 1))
                act.activation(u_four[:, b, :], ps[:, b, :], ACT.Copy).then_inc(sig("four_ready"), 1)
            hyena_out(0)
            hyena_out(1)
            for ct in range(NHT):
                act.wait_ge(sig("four1_made"), since("four1_made", ct + 1))
                act.activation(four1[:, ct, :], ps[:, ct, :], ACT.Copy).then_inc(sig("four1_ready"), 1)
            hyena_out(2)
            hyena_out(3)
            act.wait_ge(sig("four2_made"), since("four2_made", 1))
            act.activation(y_fo, ps[:, 0:2, :].rearrange("p b (c t) -> p (b c) t", t=T), ACT.Copy).then_inc(sig("y_fo_ready"), 1)
            act.wait_ge(sig("y_fo_ready"), since("y_fo_ready", 1))
            act.activation(y_sq_fo, y_fo.rearrange("p c t -> p (c t)"), ACT.Square).then_inc(sig("fo_squared"), 1)
            hyena_out(4)
            act.wait_ge(sig("fo_mean"), since("fo_mean", 1))
            act.activation(root_fo, root_fo, ACT.Sqrt).then_inc(sig("fo_root"), 1)
            hyena_out(5)
            for b in range(NB):
                act.wait_ge(sig("z_turned"), since("z_turned", b + 1))
                act.activation(z_tok[:, b, :], ps[:, 6 + b, :], ACT.Copy).then_inc(sig("z_tok_ready"), 1)
            for f in range(4):
                act.wait_ge(sig("zF_made"), since("zF_made", f + 1))
                act.activation(zF[:, f, :], ps[:, f, :], ACT.Copy).then_inc(sig("zF_ready"), 1)
            act.wait_ge(sig("y_hy_ready"), since("y_hy_ready", 1))
            act.activation(y_sq_hy, y_hy.rearrange("p c t -> p (c t)"), ACT.Square).then_inc(sig("hy_squared"), 1)
            for n in range(2):
                part = root_hy[:, n * BANK:(n + 1) * BANK]
                act.wait_ge(sig("hy_mean"), since("hy_mean", n + 1))
                act.activation(part, part, ACT.Sqrt).then_inc(sig("hy_root"), 1)
            root(stat[:, 0:NB], "row_mean", 5, "row_root")
            act.wait_ge(sig("ex_ready"), since("ex_ready", 1))
            act.activation(ex, ex, ACT.Exp).then_inc(sig("ex_out"), 1)
            for b in range(NB):
                act.activation(xn[:, b, :], x[:, b, :], ACT.Copy, scale=stat[:, b:b + 1]).then_inc(sig("xn_ready"), 1)

            def silu_gate():
                return act.activation(silu_g.rearrange("p (c h s) -> p c h s", c=2, h=2), by_tile(ps[:, 3, 0:256])[:, :, 0:2, :], ACT.Silu)

            def rows_part_out(n):
                act.wait_ge(sig("gathered"), n + 1)
                act.activation(rows_part, ps[:, 0, 0:256], ACT.Copy).then_inc(sig("rows_part_ready"), 1)

            def item_out(n, last=False):
                act.wait_ge(sig("item_gu_made"), n + 1)
                act.activation(gu_part, ps[:, 2, 0:256], ACT.Copy).then_inc(sig("gu_part_ready"), 1)
                if not last:
                    rows_part_out(n + 1)
                act.wait_ge(sig("gate_up_turned"), n + 1)
                silu_gate().then_inc(sig("silu_g_ready"), 1)
                act.wait_ge(sig("item_down_made"), n + 1)
                act.activation(down_part[:, 0:BANK], ps[:, 0, :], ACT.Copy).then_inc(sig("down_scalar"), 1)

            rows_part_out(0)
            with act.Fori(0, N_EXP - 1) as n:
                item_out(n)
            item_out(N_EXP - 1, last=True)
            act.wait_ge(sig("table_ready"), since("table_ready", 1))
            n_over = act.value_load(table_i[0:1, 16:17], min_val=0, max_val=16)
            with act.If(n_over > 0):
                with act.Fori(0, n_over) as i:
                    act.wait_ge(sig("over_tensor"), 6 * i + 4)
                    silu_gate().then_inc(sig("over_scalar"), 1)
            root(stat[:, 0:NB], "row_mean", 6, "row_root")

        @block.vector
        def _(dve):
            link = chain(dve, "dve_chain")

            rows_scaled = [0]

            def row_scales(src, junk, ready=None):
                for b in range(NB):
                    if ready:
                        dve.wait_ge(sig(ready[b][0]), ready[b][1])
                    link(dve.tensor_tensor_reduce(junk, src[:, b, :], src[:, b, :], 1.0, 0.0, ALU.mult, ALU.add, stat[:, b:b + 1]))
                dve.tensor_scalar(stat[:, 0:NB], stat[:, 0:NB], 1.0 / D, EPS, ALU.mult, ALU.add).then_inc(sig("row_mean"), 1)
                rows_scaled[0] += 1
                dve.wait_ge(sig("row_root"), rows_scaled[0])
                link(dve.reciprocal(stat[:, 0:NB], stat[:, 0:NB]))

            def turned_out(first_bank, signal_in, signal_out, gains):
                for n in range(4):
                    b, half = n // 2, n % 2
                    dve.wait_ge(sig(signal_in), since(signal_in, n + 1))
                    dve.tensor_tensor(hT[:, 4 * half:4 * half + 4, b * P:(b + 1) * P],
                                      ps[:, first_bank + n, :].rearrange("p (k t) -> p k t", t=P),
                                      spread(cols[:, gains + 4 * half:gains + 4 * half + 4], 2, P), ALU.mult)\
                       .then_inc(sig(signal_out), 1)

            row_scales(x, merge[:, 0, 1, :], (("x0_loaded", 16), ("x1_loaded", 16)))
            for b in range(NB):
                dve.tensor_scalar(merge[:, b, 0, :], x[:, b, :], stat[:, b:b + 1], None, ALU.mult).then_inc(sig("x_normed"), 1)
            dve.wait_ge(sig("const_loaded"), 32)
            turned_out(0, "x_turned", "h_ready", C_MIX)

            dve.wait_ge(sig("qkv_out"), 6)
            for k in range(TAPS):
                for ct in range(CT):
                    tap = cols[:, C_CONV + k * CT + ct:C_CONV + k * CT + ct + 1]
                    src = raw[:, ct, k:k + T]
                    if k == 0:
                        ins = dve.tensor_scalar(convT[:, ct, :], src, tap, None, ALU.mult)
                    else:
                        ins = dve.scalar_tensor_tensor(convT[:, ct, :], src, tap, convT[:, ct, :], ALU.mult, ALU.add)
                if k < TAPS - 1:
                    link(ins)
            ins.then_inc(sig("conv_ready"), 1)
            dve.wait_ge(sig("projected_out"), 8)
            dve.wait_ge(sig("rows_loaded"), 16)
            dve.tensor_tensor(sp_y, ctl[:, :, 28:32], spread(rows[:, R_DT:R_DT + 4], 1, NB), ALU.add).then_inc(sig("y_ready"), 1)
            dve.wait_ge(sig("y_ready"), since("y_ready", 1))
            dve.wait_ge(sig("softplus_ready"), since("softplus_ready", 1))
            link(dve.scalar_tensor_tensor(sp_y, sp_y, 0.0, sp_m, ALU.max, ALU.add))
            link(dve.scalar_tensor_tensor(g_tok, sp_y, -1.0, spread(small[:, 64:68], 1, NB), ALU.mult, ALU.mult))
            dve.tensor_copy(g_lhs, spread(g_tok, 3, P)).then_inc(sig("g_spread"), 1)
            beta = ctl[:, :, 24:28]
            dve.tensor_copy(beta_lhs, spread(beta, 3, P)).then_inc(sig("g_spread"), 1)
            dve.wait_ge(sig("gc_ready"), since("gc_ready", 1))
            link(dve.tensor_copy(small[:, 24:40], ps[:, 2, 0:16]))
            dve.tensor_tensor(e_last, gl, gc, ALU.subtract).then_inc(sig("gc_out"), 1)
            dve.wait_ge(sig("exp_gc_ready"), since("exp_gc_ready", 1))
            for b in range(NB):
                for h in range(H_GDN):
                    ins = dve.tensor_scalar(decayT[:, b, h, :], pair(4)[:, b, h, :], gc[:, b, h:h + 1], 0.0,
                                            ALU.subtract, ALU.min)
            ins.then_inc(sig("gc_out"), 1)
            dve.wait_ge(sig("nsa_const_loaded"), 48)
            dve.wait_ge(sig("projected_out"), 8)
            tmp = [own[:, 4:6, :].rearrange("p u n -> p (u n)")[:, 320 * n:320 * n + 320]
                   .rearrange("p (b h d) -> p b h d", b=NB, h=N_HEADS64) for n in range(4)]
            for b in range(NB):
                x1, x2 = nsa[:, b, :, 0:ROPE_HALF], nsa[:, b, :, ROPE_HALF:2 * ROPE_HALF]
                dve.tensor_tensor(tmp[0][:, b], x1, rope[:, 0, b], ALU.mult)
                dve.tensor_tensor(tmp[1][:, b], x2, rope[:, 1, b], ALU.mult)
                dve.tensor_tensor(tmp[2][:, b], x2, rope[:, 0, b], ALU.mult)
                link(dve.tensor_tensor(tmp[3][:, b], x1, rope[:, 1, b], ALU.mult))
                dve.tensor_tensor(x1, tmp[0][:, b], tmp[1][:, b], ALU.subtract)
                ins = dve.tensor_tensor(x2, tmp[2][:, b], tmp[3][:, b], ALU.add)
            ins.then_inc(sig("roped"), 1)
            dve.wait_ge(sig("qk_squared"), since("qk_squared", 1))
            dve.tensor_tensor(kbT, kT, pair(6), ALU.mult).then_inc(sig("beta_used"), 1)
            dve.wait_ge(sig("qk_summed"), since("qk_summed", 1))
            sums = ps[:, 4:8, :].rearrange("p u (c t) -> p (u c) t", t=T)
            rs = own[:, 4:6, :].rearrange("p u (c t) -> p (u c) t", t=T)
            dve.tensor_scalar(rs, sums, EPS, None, ALU.add).then_inc(sig("sums_out"), 1)
            dve.wait_ge(sig("norms_ready"), since("norms_ready", 1))
            link(dve.reciprocal(rs, rs))
            dve.wait_ge(sig("beta_used"), since("beta_used", 1))
            link(dve.scalar_tensor_tensor(convT[:, 0:4, :], convT[:, 0:4, :], float(DH_GDN) ** -0.5, rs[:, 0:4, :], ALU.mult, ALU.mult))
            link(dve.tensor_tensor(convT[:, 4:8, :], convT[:, 4:8, :], rs[:, 4:8, :], ALU.mult))
            rk = own[:, 5, :].rearrange("p (h b t) -> p b h t", h=H_GDN, b=NB)
            dve.tensor_tensor(kbT, kbT, rk, ALU.mult).then_inc(sig("kb_ready"), 1)
            dve.wait_ge(sig("decays_ready"), since("decays_ready", 1))
            dve.wait_ge(sig("qk_summed"), since("qk_summed", 1))
            dve.tensor_tensor(qgT, qT, exp_gc, ALU.mult)
            flat = lambda u: u.rearrange("p b h n -> p (b h) n")
            link(dve.tensor_tensor(flat(decayT), flat(decayT), spread(sq(CUM), 1, NB * H_GDN), ALU.mult))
            link(dve.tensor_tensor(flat(decay_strict), flat(decayT), spread(sq(STRICT), 1, NB * H_GDN), ALU.mult))
            dve.wait_ge(sig("kk_ready"), since("kk_ready", 1))
            dve.tensor_tensor(aT, pair(4), decay_strict, ALU.mult).then_inc(sig("a_ready"), 1)
            dve.tensor_tensor(qk_decay, pair(6), decayT, ALU.mult).then_inc(sig("qk_ready"), 1)
            link(dve.tensor_tensor(beta_g, beta_g, beta, ALU.mult))
            dve.wait_ge(sig("kv_turned"), since("kv_turned", 1))
            for b in range(NB):
                dve.tensor_tensor(kbg[:, b], pair(4)[:, b], spread(beta_g[:, b], 2, P), ALU.mult)
                dve.tensor_tensor(kd[:, b], pair(4)[:, b], spread(e_last[:, b], 2, P), ALU.mult)
            dve.wait_ge(sig("kv_turned"), since("kv_turned", 2))
            for b in range(NB):
                ins = dve.tensor_tensor(vb[:, b], pair(6)[:, b], spread(beta[:, b], 2, P), ALU.mult)
            ins.then_inc(sig("kd_ready"), 1)
            dve.wait_ge(sig("a_ready"), since("a_ready", 1))
            dve.wait_ge(sig("inverse_started"), 2)

            gates = lambda b, kind: ctl[:, b, 0:24].rearrange("p (h k) -> p h k", k=3)[:, :, kind]
            mx, total = (soft[:, n:n + 16].rearrange("p (b h) -> p b h", b=NB) for n in (64, 80))

            def attention_step(t):
                if t == 0:
                    dve.wait_ge(sig("pairs_made"), since("pairs_made", 1))
                    made = ps[:, 7, :].rearrange("p (s g n a) -> p s g n a", s=2, g=NSA_G, a=CMP_A // 2)
                    dve.memset(pairs_all[:, :, :, NSA_G * N_CMP:], 0.0)
                    for s in range(2):
                        for ah in range(2):
                            pos = cols[:, C_POS + s * CMP_A + 8 * ah:C_POS + s * CMP_A + 8 * ah + 8]
                            ins = dve.tensor_tensor(pairs[:, s, 8 * ah:8 * ah + 8, :, :].rearrange("p a g n -> p g n a"),
                                                    made[:, s, :, ah:ah + N_CMP, :], spread(spread(pos, 1, N_CMP), 1, NSA_G), ALU.add)
                    ins.then_inc(sig("pairs_ready"), 1)
                    dve.memset(kcT, 0.0)
                    dve.memset(unit[7][:, 0:64], 0.0).then_inc(sig("hid_zeroed"), 1)
                elif t == 2:
                    dve.wait_ge(sig("hid_ready"), since("hid_ready", 2))
                    dve.tensor_copy(hid_rep, spread(hid[:, 1, :, :], 2, NSA_R)).then_inc(sig("hid_rep_ready"), 1)
                elif t == 3:
                    dve.wait_ge(sig("kv_cmp_made"), since("kv_cmp_made", 1))
                    for g in range(NSA_G):
                        gp = slice(g * NSA_D, (g + 1) * NSA_D)
                        dve.tensor_copy(kcT[gp, g, :], ps[gp, 4, 64:80])
                    dve.tensor_tensor(v_cmp, spread(ps[:, 4, 128:192], 1, NSA_H), spread(cols[:, C_BLK:C_BLK + NSA_H], 2, NSA_D), ALU.mult)\
                       .then_inc(sig("kv_cmp_ready"), 1)
                elif t == 4:
                    dve.wait_ge(sig("s_cmp_made"), 1)
                    made = ps[:, 5, 0:256].rearrange("p (b r g n) -> p b r g n", b=NB, r=NSA_R, g=NSA_G)
                    for b in range(NB):
                        ins = dve.tensor_tensor(p_cmp[:, b].rearrange("p (g r) n -> p r g n", g=NSA_G), made[:, b],
                                                spread(spread(vis[:, 1, b], 1, NSA_G), 1, NSA_R), ALU.add)
                    link(ins)
                    link(dve.tensor_reduce(mx, p_cmp, AX_X, ALU.max))
                    dve.tensor_tensor(p_cmp, p_cmp, spread(mx, 3, CMP_STRIDE), ALU.subtract).then_inc(sig("s_cmp_ready"), 1)
                elif t == 5:
                    dve.wait_ge(sig("exp_cmp_ready"), 1)
                    link(dve.tensor_reduce(total, p_cmp, AX_X, ALU.add))
                    dve.tensor_tensor(p_cmp, p_cmp, spread(vis[:, 0], 2, NSA_H), ALU.mult).then_inc(sig("p_cmp_ready"), 1)
                    link(dve.reciprocal(total, total))
                    for b in range(NB):
                        ins = dve.tensor_tensor(total[:, b], total[:, b], gates(b, 0), ALU.mult)
                    link(ins)
                elif t == 7:
                    dve.wait_ge(sig("o_cmp_made"), 1)
                    dve.tensor_tensor(o_nsa.rearrange("p b (h d) -> p b h d", d=NSA_D),
                                      ps[:, 4:6, :].rearrange("p b (h d) -> p b h d", d=NSA_D), spread(total, 3, NSA_D), ALU.mult)\
                       .then_inc(sig("o_cmp_out"), 1)
                elif t in (8, 9):
                    job_maxima(t - 8)
                elif t > FIRST_TURN and (t - FIRST_TURN) % 2:
                    q = (t - FIRST_TURN) // 2
                    job_out(q)
                    if q + 2 < N_JOB:
                        job_maxima(q + 2)

            def job_maxima(q):
                b = JOBS[q][0]
                nk = (b + 1) * P
                p = probs[q % 2][:, 0:4 * nk].rearrange("p (g r n) -> p g r n", g=NSA_G, n=nk)
                got = ps[:, 4:6, 0:2 * nk].rearrange("p g (r n) -> p g r n", n=nk)
                mine = soft[:, 4 * q:4 * q + 4]
                dve.wait_ge(sig("scores_made"), q + 1)
                if b:
                    dve.tensor_copy(p[:, :, :, 0:P], got[:, :, :, 0:P])
                dve.tensor_tensor(p[:, :, :, nk - P:nk], got[:, :, :, nk - P:nk], spread(spread(sq(CAUSAL), 1, 2), 1, NSA_G), ALU.add)\
                   .then_inc(sig("scores_out"), 1)
                dve.wait_ge(sig("scores_out"), q + 1)
                link(dve.tensor_reduce(mine, probs[q % 2][:, 0:4 * nk].rearrange("p (h n) -> p h n", n=nk), AX_X, ALU.max))
                dve.tensor_scalar(mine, mine, -float(NSA_D) ** -0.5, None, ALU.mult).then_inc(sig("maxima_ready"), 1)

            def job_out(q):
                b, kind, half = JOBS[q]
                sums = soft[:, 32 + 4 * q:36 + 4 * q]
                by_group = sums.rearrange("p (g r) -> p g r", g=NSA_G)
                gate = gates(b, 1 + kind).rearrange("p (g r) -> p g r", g=NSA_G)[:, :, 2 * half:2 * half + 2]
                dve.wait_ge(sig("probs_ready"), q + 1)
                link(dve.reciprocal(sums, sums))
                link(dve.tensor_tensor(by_group, by_group, gate, ALU.mult))
                dve.wait_ge(sig("o_job_made"), q + 1)
                dve.tensor_tensor(o_part, ps[:, 7, 0:256].rearrange("p (g r d) -> p g r d", g=NSA_G, d=NSA_D), spread(by_group, 3, NSA_D), ALU.mult)\
                   .then_inc(sig("o_job_out"), 1)
                dve.wait_ge(sig("o_job_out"), q + 1)
                into = job_heads(o_nsa[:, b, :], half)
                ins = dve.tensor_tensor(into, into, o_part, ALU.add)
                if q == N_JOB - 1:
                    ins.then_inc(sig("o_nsa_ready"), 1)
                else:
                    link(ins)

            def level_off(n, b):
                dve.tensor_tensor(off[:, b], aT[:, b], spread(sq(LEVEL0 + n), 1, H_GDN), ALU.mult).then_inc(sig("off_ready"), 1)

            for b in range(NB):
                level_off(0, b)
            for n in range(N_LEVEL):
                attention_step(2 * n)
                for b in range(NB):
                    dve.wait_ge(sig("step_made"), NB * n + b + 1)
                    if n:
                        dve.wait_ge(sig("inverse_ready"), NB * (n - 1) + b + 1)
                    dve.tensor_tensor(inv[:, b], inv[:, b], pair(2 if n else 0)[:, b], ALU.subtract)
                    dve.tensor_tensor(invT[:, b], invT[:, b], pair(0)[:, b] if n else off[:, b], ALU.subtract).then_inc(sig("inverse_ready"), 1)
                    if n == 0:
                        dve.wait_ge(sig("inverse_ready"), b + 1)
                    if n < N_LEVEL - 1:
                        level_off(n + 1, b)
                attention_step(2 * n + 1)
            for c in range(N_CHUNK):
                b, r = c // 2, slice(CHUNK * (c % 2), CHUNK * (c % 2) + CHUNK)
                if c == 0:
                    dve.wait_ge(sig("uw_ready"), 1)
                    dve.tensor_copy(vnew[r, b], uu[r, b]).then_inc(sig("vnew_ready"), 1)
                else:
                    dve.wait_ge(sig("ws_made"), c)
                    dve.tensor_tensor(vnew[r, b], uu[r, b], ps[r, 0, :].rearrange("p (h n) -> p h n", h=H_GDN),
                                      ALU.subtract).then_inc(sig("vnew_ready"), 1)
                attention_step(2 * N_LEVEL + 2 * c)
                if c < N_CHUNK - 1:
                    dve.wait_ge(sig("kv_made"), c + 1)
                    if c >= 1:
                        dve.wait_ge(sig("o_made"), c)
                    for h in range(H_GDN):
                        new, add = state[:, (c + 1) % 2, h, :], ps[:, 1, h * P:(h + 1) * P]
                        if c == 0:
                            ins = dve.tensor_copy(new, add)
                        else:
                            last = exp_gc[:, b, h, r.stop - 1:r.stop]
                            ins = dve.scalar_tensor_tensor(new, state[:, c % 2, h, :], last, add, ALU.mult, ALU.add)
                    ins.then_inc(sig("state_ready"), 1)
                    dve.wait_ge(sig("state_ready"), c + 1)
                attention_step(2 * N_LEVEL + 2 * c + 1)
            attention_step(2 * (N_LEVEL + N_CHUNK))
            dve.wait_ge(sig("o_squared"), 1)
            link(dve.tensor_reduce(o_ss, o_sq, AX_X, ALU.add))
            dve.tensor_scalar(o_ss, o_ss, 1.0 / DH_GDN, EPS, ALU.mult, ALU.add).then_inc(sig("o_mean"), 1)
            attention_step(2 * (N_LEVEL + N_CHUNK) + 1)
            dve.wait_ge(sig("o_root"), 1)
            link(dve.reciprocal(o_ss, o_ss))
            link(dve.tensor_tensor(o_gdn, o_gdn, spread(o_ss, 3, P), ALU.mult))
            link(dve.tensor_tensor(flat(o_gdn), flat(o_gdn), spread(rows[:, R_ONORM:R_ONORM + P], 1, NB * H_GDN), ALU.mult))
            dve.tensor_tensor(o_gdn, o_gdn, silu_z.rearrange("p b (h n) -> p b h n", h=H_GDN), ALU.mult).then_inc(sig("o_normed"), 1)
            for t in range(2 * (N_LEVEL + N_CHUNK) + 2, FILL_STEPS):
                attention_step(t)
            halves = lambda n: ps[:, n:n + 2, :].rearrange("p h n -> p (h n)")
            for b in range(NB):
                dve.wait_ge(sig("branch_made"), b + 1)
                link(dve.tensor_tensor(merge[:, b, 0, :], merge[:, b, 0, :], halves(2 * b), ALU.mult))
            for b in range(NB):
                dve.wait_ge(sig("branch_made"), NB + b + 1)
                link(dve.tensor_tensor(merge[:, b, 1, :], merge[:, b, 1, :], halves(4 + 2 * b), ALU.mult))
                dve.tensor_tensor(merge[:, b, 0, :], merge[:, b, 0, :], merge[:, b, 1, :], ALU.add).then_inc(sig("merged"), 1)
            for n in range(3):
                dve.wait_ge(sig("filt_layer"), since("filt_layer", n + 1))
                link(dve.tensor_scalar(arg, ps[0:64, 0, 0:T], cols[0:64, C_FB + n:C_FB + n + 1], cols[0:64, C_FREQ + n:C_FREQ + n + 1],
                                       ALU.add, ALU.mult))
                link(dve.tensor_scalar(turns_, arg, 1.0 / TWO_PI, ROUND_MAGIC, ALU.mult, ALU.add))
                link(dve.tensor_scalar(turns_, turns_, ROUND_MAGIC, None, ALU.subtract))
                for part in (TWO_PI_HI, TWO_PI_MID, TWO_PI_LO):
                    link(dve.scalar_tensor_tensor(arg, turns_, -part, arg, ALU.mult, ALU.add))
                dve.tensor_scalar(arg, arg, 3.1415925, -3.1415925, ALU.min, ALU.max).then_inc(sig("arg_ready"), 1)
                dve.wait_ge(sig("arg_ready"), since("arg_ready", n + 1))
                if n == 1:
                    dve.wait_ge(sig("w_out_made"), 2)
                    link(dve.tensor_tensor(x[:, 0, :], x[:, 0, :], halves(4), ALU.add))
            dve.wait_ge(sig("filt_out_made"), since("filt_out_made", 1))
            made = ps[:, 0:4, :].rearrange("p (b d) n -> p d b n", d=2)
            link(dve.tensor_tensor(kern[:, 1], made[:, 1], decay2, ALU.mult))
            dve.tensor_tensor(kern[:, 0], made[:, 0], decay2, ALU.mult).then_inc(sig("kern_ready"), 1)
            dve.wait_ge(sig("w_out_made"), 4)
            link(dve.tensor_tensor(x[:, 1, :], x[:, 1, :], halves(6), ALU.add))
            dve.wait_ge(sig("merged"), 2)
            row_scales(x, merge[:, 0, 1, :])
            dve.wait_ge(sig("merge_turned"), since("merge_turned", 4))
            for b in range(NB):
                dve.tensor_scalar(merge[:, b, 0, :], x[:, b, :], stat[:, b:b + 1], None, ALU.mult).then_inc(sig("x2_normed"), 1)
            dve.wait_ge(sig("filter_turned"), since("filter_turned", 1))
            dve.reciprocal(filt_norm, ps[:, 3, 0:NHT]).then_inc(sig("filt_norm_ready"), 1)
            turned_out(0, "x2_turned", "h2_ready", C_FFN)

            def ffn(s):
                for b in range(NB):
                    dve.wait_ge(sig("gate_ready"), 2 * s.n + b + 1)
                    ins = dve.tensor_tensor(gated[:, s.par, b, :], gated[:, s.par, b, :], ps[:, 2 * s.par + b, FC:2 * FC], ALU.mult)
                ins.then_inc(sig("gated_ready"), 1)

            ffn(Step(0))
            with dve.Fori(0, (N_FC - 1) // 2) as i:
                for parity in range(2):
                    ffn(Step(i=i, parity=parity))
            dve.wait_ge(sig("down_made"), N_FC)
            for b in range(NB):
                dve.tensor_tensor(x[:, b, :], x[:, b, :], halves(4 + 2 * b), ALU.add).then_inc(sig("x3_step"), 1)
                dve.wait_ge(sig("x3_step"), 2 * b + 1)
                dve.tensor_tensor(merge[:, b, 0, :], x[:, b, :], rows[:, R_FIN1:R_FIN1 + D], ALU.mult).then_inc(sig("x3_step"), 1)
            dve.wait_ge(sig("x3_step"), 4)
            link(dve.tensor_tensor_reduce(hT_flat[:, 1024:2048], merge[:, 1, 0, :], merge[:, 1, 0, :], 1.0, 0.0, ALU.mult, ALU.add, stat[:, 5:6]))
            dve.wait_ge(sig("x3_squared"), 3)
            root1, root2, scale = stat[:, 0:NB], stat[:, 4:4 + NB], stat[:, 8:8 + NB]
            dve.tensor_scalar(root1, root1, 1.0 / D, EPS, ALU.mult, ALU.add).then_inc(sig("row_mean"), 1)
            rows_scaled[0] += 1
            dve.wait_ge(sig("row_root"), rows_scaled[0])
            link(dve.reciprocal(root1, root1))
            link(dve.tensor_tensor(root2, root2, root1, ALU.mult))
            link(dve.scalar_tensor_tensor(root2, root2, 1.0 / D, root1, ALU.mult, ALU.mult))
            dve.tensor_scalar(root2, root2, EPS, None, ALU.add).then_inc(sig("row_mean"), 1)
            rows_scaled[0] += 1
            dve.wait_ge(sig("row_root"), rows_scaled[0])
            link(dve.reciprocal(root2, root2))
            link(dve.tensor_tensor(scale, root1, root2, ALU.mult))
            for b in range(NB):
                dve.tensor_scalar(merge[:, b, 1, :], merge[:, b, 0, :], scale[:, b:b + 1], None, ALU.mult).then_inc(sig("x3_normed"), 1)
            turned_out(4, "x3_turned", "h3_ready", C_N1)
            def short_conv(first, n):
                for k in range(3):
                    for ct in range(first, first + n):
                        tap = cols[:, C_CONV2 + k * CT + ct:C_CONV2 + k * CT + ct + 1]
                        if k == 0:
                            ins = dve.tensor_scalar(conv2[:, ct, :], u2[:, ct, 0:T], tap, cols[:, C_CONVB2 + ct:C_CONVB2 + ct + 1],
                                                    ALU.mult, ALU.add)
                        else:
                            ins = dve.scalar_tensor_tensor(conv2[:, ct, :], u2[:, ct, k:k + T], tap, conv2[:, ct, :], ALU.mult, ALU.add)
                    link(ins)

            def head_norms(y, part, gains):
                link(dve.reciprocal(part, part))
                for ct in range(y.shape[1]):
                    ins = dve.scalar_tensor_tensor(y[:, ct, :], y[:, ct, :], cols[:, gains + ct:gains + ct + 1], part[:, ct * T:(ct + 1) * T],
                                                   ALU.mult, ALU.mult)
                return ins

            dve.wait_ge(sig("u2_out"), 2)
            short_conv(NHT, NHT)
            dve.wait_ge(sig("u2_out"), 4)
            short_conv(2 * NHT, NHT)
            dve.tensor_tensor(zT, zT, conv2[:, 2 * NHT:3 * NHT, :], ALU.mult).then_inc(sig("z_ready"), 1)
            dve.wait_ge(sig("fo_summed"), since("fo_summed", 1))
            dve.tensor_scalar(root_fo, ps[:, 2:4, :].rearrange("p f n -> p (f n)"), 1.0 / NSA_D, EPS, ALU.mult, ALU.add).then_inc(sig("fo_mean"), 1)
            dve.wait_ge(sig("fo_root"), since("fo_root", 1))
            head_norms(y_fo, root_fo, C_MIXG + NHT).then_inc(sig("fo_normed"), 1)
            dve.wait_ge(sig("u2_out"), 6)
            short_conv(0, NHT)
            dve.wait_ge(sig("z_turned"), since("z_turned", 2))
            for ct in range(NHT):
                ins = dve.tensor_scalar(zT[:, ct, :], zT[:, ct, :], cols[:, C_FBIAS + ct:C_FBIAS + ct + 1], None, ALU.mult)
            link(ins)
            dve.wait_ge(sig("zF_ready"), since("zF_ready", 4))
            re, im = slice(0, 2), slice(2, 4)
            dve.tensor_tensor(cross, zF[:, im, :], kernF[:, im, :], ALU.mult)
            link(dve.tensor_tensor(prodF[:, re, :], zF[:, re, :], kernF[:, re, :], ALU.mult))
            link(dve.tensor_tensor(prodF[:, re, :], prodF[:, re, :], cross, ALU.subtract))
            dve.tensor_tensor(cross, zF[:, im, :], kernF[:, re, :], ALU.mult)
            link(dve.tensor_tensor(prodF[:, im, :], zF[:, re, :], kernF[:, im, :], ALU.mult))
            dve.tensor_tensor(prodF[:, im, :], prodF[:, im, :], cross, ALU.add).then_inc(sig("prod_ready"), 1)
            dve.wait_ge(sig("conv_made"), since("conv_made", 1))
            for ct in range(NHT):
                ins = dve.scalar_tensor_tensor(y_hy[:, ct, :], ps[:, ct // 2, (ct % 2) * T:(ct % 2 + 1) * T], filt_norm[:, ct:ct + 1],
                                               zT[:, ct, :], ALU.mult, ALU.add)
            link(ins)
            dve.tensor_tensor(y_hy, y_hy, conv2[:, 0:NHT, :], ALU.mult).then_inc(sig("y_hy_ready"), 1)
            dve.wait_ge(sig("hy_summed"), since("hy_summed", 1))
            for n in range(2):
                part = root_hy[:, n * BANK:(n + 1) * BANK]
                dve.tensor_scalar(part, ps[:, 2 + n, :], 1.0 / NSA_D, EPS, ALU.mult, ALU.add).then_inc(sig("hy_mean"), 1)
            for n in range(2):
                dve.wait_ge(sig("hy_root"), since("hy_root", n + 1))
                head_norms(y_hy[:, 2 * n:2 * n + 2], root_hy[:, n * BANK:(n + 1) * BANK], C_MIXG + 2 * n).then_inc(sig("hy_normed"), 1)
            dve.wait_ge(sig("x3_ready"), NB)
            for b in range(NB):
                dve.wait_ge(sig("out2_made"), since("out2_made", b + 1))
                dve.tensor_tensor(x[:, b, :], x[:, b, :], halves(4 + 2 * b), ALU.add).then_inc(sig("x4_summed"), 1)
            dve.wait_ge(sig("x4_summed"), NB)
            turned_out(0, "x4_turned", "h4_ready", C_N2)
            row_scales(x, own[:, 5, :])
            dve.memset(zero, 0.0).then_inc(sig("zero_ready"), 1)

            def first_best(values, n, tmp, out):
                big = spread(rows[:, R_BIG:R_BIG + n], 1, NB)
                wide = lambda v: v.broadcast_to([P, NB, n])
                link(dve.tensor_reduce(best, values, AX_X, ALU.max))
                link(dve.tensor_tensor(tmp, values, wide(best), ALU.is_equal))
                link(dve.tensor_tensor(tmp, tmp, big, ALU.mult))
                link(dve.tensor_reduce(first, tmp, AX_X, ALU.min))
                link(dve.tensor_tensor(out, big, wide(first), ALU.is_equal))

            dve.wait_ge(sig("logits_made"), since("logits_made", 1))
            n = N_GRP + N_EXP
            for b in range(NB):
                ins = dve.scalar_tensor_tensor(logits[:, b, :], ps[:, 4, b * n:(b + 1) * n], stat[:, b:b + 1], rows[:, R_BIAS:R_BIAS + n],
                                               ALU.mult, ALU.add)
            link(ins)
            first_best(l_grp, N_GRP, eq4, one_grp)
            link(dve.tensor_tensor(ex[:, :, 0:N_GRP], l_grp, best.broadcast_to([P, NB, N_GRP]), ALU.subtract))
            in_group = lambda b: spread(one_grp[:, b, :], 2, EPG)
            by_group = lambda v, b: v[:, b, :].rearrange("p (g e) -> p g e", e=EPG)
            link(dve.tensor_scalar(eq4, one_grp, -1.0, -NEG, ALU.add, ALU.mult))
            for b in range(NB):
                link(dve.tensor_tensor(by_group(l_exp, b), by_group(l_exp, b), in_group(b), ALU.mult))
                link(dve.tensor_tensor(by_group(l_exp, b), by_group(l_exp, b), spread(eq4[:, b, :], 2, EPG), ALU.add))
            first_best(l_exp, N_EXP, eq, one1)
            link(dve.tensor_copy(second, best))
            link(dve.scalar_tensor_tensor(l_exp, one1, 2 * NEG, l_exp, ALU.mult, ALU.add))
            first_best(l_exp, N_EXP, eq, one2)
            dve.tensor_tensor(chosen, one1, one2, ALU.add).then_inc(sig("chosen_ready"), 1)
            dve.tensor_tensor(ex[:, :, N_GRP:N_GRP + 1], best, second, ALU.subtract).then_inc(sig("ex_ready"), 1)
            dve.wait_ge(sig("ex_out"), 1)
            link(dve.tensor_reduce(best, ex[:, :, 0:N_GRP], AX_X, ALU.add))
            link(dve.scalar_tensor_tensor(first, ex[:, :, N_GRP:N_GRP + 1], 1.0, best, ALU.add, ALU.mult))
            w1 = weights[:, 0:NB].rearrange("p (b e) -> p b e", e=1)
            w2 = weights[:, NB:2 * NB].rearrange("p (b e) -> p b e", e=1)
            link(dve.reciprocal(w1, first))
            link(dve.tensor_tensor(w2, w1, ex[:, :, N_GRP:N_GRP + 1], ALU.mult))
            iota = rows[:, R_IOTA:R_IOTA + N_EXP]
            link(dve.tensor_scalar(base, iota, float(CAP), None, ALU.mult))
            dve.wait_ge(sig("ranks_made"), since("ranks_made", 1))
            link(dve.tensor_copy(rank_count, ps[:, 3, 0:96]))
            rank = rank_count[:, 0:64].rearrange("p (b e) -> p b e", b=NB)
            link(dve.tensor_scalar(shift, rank, float(CAP), FAR, ALU.is_ge, ALU.mult))
            link(dve.tensor_tensor(slot_of, rank, spread(base, 1, NB), ALU.add))
            link(dve.tensor_tensor(shift, shift, slot_of, ALU.add))

            def places(source, out):
                for n, one in enumerate((one1, one2)):
                    link(dve.tensor_tensor(eq, one, source, ALU.mult))
                    link(dve.tensor_reduce(out[:, n * NB:(n + 1) * NB], eq, AX_X, ALU.add))

            places(shift, slots_of)

            def places_beyond():
                link(dve.tensor_scalar(counts, rank_count[:, 64:96], 1.0 / CAP, None, ALU.mult))
                link(dve.tensor_tensor(steps, spread(counts, 2, 7), spread(rows[:, R_IOTA + 1:R_IOTA + 8], 1, N_EXP), ALU.is_gt))
                link(dve.tensor_reduce(more, steps, AX_X, ALU.add))
                link(dve.tensor_copy(over_ends[0], more))
                for k in range(5):
                    a, b, s = over_ends[k % 2], over_ends[(k + 1) % 2], 1 << k
                    dve.tensor_copy(b[:, 0:s], a[:, 0:s])
                    link(dve.tensor_tensor(b[:, s:], a[:, s:], a[:, 0:N_EXP - s], ALU.add))
                ends = over_ends[1]
                link(dve.tensor_tensor(base, ends, more, ALU.subtract))
                link(dve.tensor_tensor(base, base, iota, ALU.subtract))
                link(dve.tensor_scalar(base, base, float(CAP), float(CAP * (N_EXP - 1)), ALU.mult, ALU.add))
                link(dve.tensor_scalar(shift, rank, float(CAP), None, ALU.is_ge))
                link(dve.tensor_tensor(shift, shift, spread(base, 1, NB), ALU.mult))
                link(dve.scalar_tensor_tensor(slot_of, slot_of, -float(CAP * N_EXP), shift, ALU.add, ALU.add))
                places(slot_of, slots_beyond)
                link(dve.tensor_tensor(table_cmp, spread(ends, 1, 16), spread(rows[:, R_IOTA:R_IOTA + 16], 2, N_EXP), ALU.is_le))
                link(dve.tensor_reduce(table[:, 0:16], table_cmp, AX_X, ALU.add))
                link(dve.tensor_scalar(table[:, 0:16], table[:, 0:16], float(N_EXP - 1), None, ALU.min))
                link(dve.tensor_copy(table[:, 16:17], ends[:, N_EXP - 1:N_EXP]))
                dve.tensor_copy(table_i, table).then_inc(sig("table_ready"), 1)

            def rows_out():
                return dve.tensor_tensor(hgT.rearrange("p (j c) s -> p c j s", j=4), by_tile(ps[:, 1, 0:256]),
                                         spread(cols[:, C_N2:C_N2 + KT].rearrange("p (j c) -> p c j", j=4), 3, CAP), ALU.mult)

            def activation_out():
                return dve.tensor_tensor(actT.rearrange("p (h c) s -> p c h s", h=2),
                                         silu_g.rearrange("p (c h s) -> p c h s", c=2, h=2), by_tile(ps[:, 3, 0:256])[:, :, 2:4, :], ALU.mult)

            def weights_out(par):
                return dve.tensor_copy(pickT[par].rearrange("p b t -> p (b t)"), ps[:, 3, 256:512])

            def item_rows_out(n):
                dve.wait_ge(sig("item_rows_turned"), n + 1)
                rows_out().then_inc(sig("hg_ready"), 1)

            def item_vector(par, n, picks=True, last=False):
                dve.wait_ge(sig("silu_g_ready"), n + 1)
                activation_out().then_inc(sig("act_ready"), 1)
                weights_out(par).then_inc(sig("pickT_ready"), 1)
                if not last:
                    item_rows_out(n + 1)
                dve.wait_ge(sig("item_down_made"), n + 1)
                dve.tensor_copy(down_part[:, BANK:], ps[:, 1, :]).then_inc(sig("down_vector"), 1)
                if picks:
                    dve.wait_ge(sig("picked"), n + 2)
                    item_picks(dve, pick_link, par).then_inc(sig("picked"), 1)

            PICK_LINKS = 3 * NB

            class Links:

                def __init__(self):
                    self.n = 0

                def __call__(self, ins):
                    self.n += 1
                    ins.then_inc(sig("pick_chain"), 1)
                    dve.wait_ge(sig("pick_chain"), self.n)

            pick_link = Links()
            item_picks(dve, pick_link, 0).then_inc(sig("picked"), 1)
            dve.wait_ge(sig("picked"), 1)
            item_picks(dve, pick_link, 1).then_inc(sig("picked"), 1)
            item_rows_out(0)
            places_beyond()
            with dve.Fori(0, N_EXP // 2 - 1) as i:
                pick_link.n = i * (2 * PICK_LINKS) + 2 * PICK_LINKS
                for par in range(2):
                    item_vector(par, 2 * i + par)
            item_vector(0, N_EXP - 2, picks=False)
            item_vector(1, N_EXP - 1, picks=False, last=True)
            for b in range(NB):
                dve.wait_ge(sig("scattered"), NB * (N_EXP - 1) + b + 1)
                ins = dve.tensor_tensor(x[:, b, :], x[:, b, :], halves(4 + 2 * b), ALU.add)
            link(ins)
            dve.wait_ge(sig("picked"), N_EXP)
            link(dve.tensor_copy(slots_of, slots_beyond))
            dve.sem_inc(sig("over_next"), 1)
            n_over = dve.value_load(table_i[0:1, 16:17], min_val=0, max_val=16)
            over_link = Links()
            with dve.If(n_over > 0):
                with dve.Fori(0, n_over) as i:
                    over_link.n = i * PICK_LINKS + N_EXP * PICK_LINKS
                    item_picks(dve, over_link, 0).then_inc(sig("over_vector"), 1)
                    dve.wait_ge(sig("over_tensor"), 6 * i + 1)
                    dve.tensor_copy(rows_part, ps[:, 0, 0:256]).then_inc(sig("over_vector"), 1)
                    dve.wait_ge(sig("over_tensor"), 6 * i + 2)
                    rows_out().then_inc(sig("over_vector"), 1)
                    dve.wait_ge(sig("over_tensor"), 6 * i + 3)
                    dve.tensor_copy(gu_part, ps[:, 2, 0:256]).then_inc(sig("over_vector"), 1)
                    dve.wait_ge(sig("over_scalar"), i + 1)
                    weights_out(0)
                    activation_out().then_inc(sig("over_vector"), 1)
                    dve.wait_ge(sig("over_tensor"), 6 * i + 5)
                    dve.tensor_copy(down_part, halves(0)).then_inc(sig("over_vector"), 1)
                    dve.wait_ge(sig("over_tensor"), 6 * i + 6)
                    for b in range(NB):
                        ins = dve.tensor_tensor(x[:, b, :], x[:, b, :], halves(4 + 2 * b), ALU.add)
                    ins.then_inc(sig("over_next"), 1)
                    dve.wait_ge(sig("over_next"), i + 2)
            row_scales(x, merge[:, 0, 1, :])
            for b in range(NB):
                dve.scalar_tensor_tensor(merge[:, b, 0, :], x[:, b, :], stat[:, b:b + 1], rows[:, R_FIN2:R_FIN2 + D], ALU.mult, ALU.mult)\
                   .then_inc(sig("out_ready"), 1)


def _constants(np):
    i = np.arange(P)
    sq = np.zeros((N_SQ, P, P), np.float32)
    same = i[:, None] // CHUNK == i[None, :] // CHUNK
    sq[IDENT] = np.eye(P)
    sq[CUM] = same & (i[:, None] <= i[None, :])
    sq[SAME] = same
    sq[STRICT] = same & (i[:, None] < i[None, :])
    for n in range(N_LEVEL):
        b = 1 << n
        sq[LEVEL0 + n] = (i[:, None] // (2 * b) == i[None, :] // (2 * b)) & (i[:, None] // b % 2 == 0) & (i[None, :] // b % 2 == 1)
    sq[ONES] = 1
    d = np.arange(NSA_D)
    ang = 2 * np.pi * np.outer(d, d) / NSA_D
    for j in range(2):
        s = slice(j * NSA_D, (j + 1) * NSA_D)
        sq[DFT_C, s, s] = np.cos(ang)
        sq[DFT_S, s, s] = -np.sin(ang)
    sq[CAUSAL] = np.where(i[None, :] <= i[:, None], 0, NEG)
    sq[RANK] = i[:, None] < i[None, :]
    out = {"squares": sq.transpose(1, 0, 2)}
    t = np.arange(T, dtype=np.float64)
    w = 2 * np.pi * (t + 0.5) / (2 * T)
    wt = np.outer(t, w)
    out["dft_fwd"] = np.concatenate([np.cos(wt), -np.sin(wt)], 1).reshape(NB, P, 2 * T).transpose(1, 0, 2)
    back = np.concatenate([np.cos(wt), np.sin(wt)], 1)
    back[0] = 0
    out["dft_bwd"] = back.reshape(NB, P, 2 * T).transpose(1, 0, 2)
    inv = np.concatenate([np.cos(wt).T, -np.sin(wt).T], 0) / T
    out["dft_inv"] = inv.reshape(2 * NB, P, T).transpose(1, 0, 2)
    wt = 2 * np.pi * np.outer(t, t) / T
    both = np.concatenate([np.cos(wt), np.sin(wt)], 1) / np.sqrt(T * NSA_D)
    out["dft_time"] = both.reshape(NB, P, 2 * T).transpose(1, 0, 2)
    f32 = np.float32
    ts = np.linspace(0, 1, T, dtype=f32)[:, None]
    ww = (f32(2 * np.pi / T) * np.arange(T, dtype=f32))[:, None]
    f = np.linspace(1e-4, 15, 16, dtype=f32)[None]
    out["emb"] = np.concatenate([ts, np.cos(f * ww), -np.sin(f * ww)], 1).T
    lo, hi = np.log(1e-2) / 1.5, np.log(1e-2) / 0.3
    deltas = np.abs(np.linspace(lo, hi, DH2, dtype=f32))
    out["decay"] = np.exp(-ts * deltas).reshape(NB, P, DH2).transpose(1, 0, 2)
    freq = f32(500000.0) ** (-np.arange(ROPE_HALF, dtype=f32) / ROPE_HALF)
    a = np.arange(T, dtype=f32)[:, None] * freq
    rope = np.zeros((2, T, N_HEADS64, ROPE_HALF), f32)
    rope[0] = 1
    for h in list(range(NSA_H)) + [8, 9, 12, 13, 16, 17]:
        rope[0, :, h], rope[1, :, h] = np.cos(a), np.sin(a)
    out["rope"] = rope.reshape(2, NB, P, N_HEADS64, ROPE_HALF).transpose(2, 0, 1, 3, 4)
    vis = np.zeros((T, CMP_STRIDE), f32)
    vis[:, :N_CMP] = np.arange(N_CMP)[None] * CMP_STRIDE + CMP_BLOCK - 1 <= np.arange(T)[:, None]
    add = np.where(vis > 0, 0, NEG)
    add[:, N_CMP:] = 3 * NEG
    out["vis"] = np.stack([vis, add]).reshape(2, NB, P, CMP_STRIDE).transpose(2, 0, 1, 3)
    return {k: np.ascontiguousarray(v, np.float32) for k, v in out.items()}


def _layout(np, x):
    f = lambda n: np.asarray(x[n], np.float32)
    feat = lambda v: v.reshape(-1, P).T
    tiles = lambda w: w.reshape(w.shape[0] // P, P, w.shape[1]).transpose(1, 0, 2)
    w = f("w_in")[0]
    a = 4 * H_GDN * DH_GDN
    ctl = 2 * H_GDN
    kv = a + ctl + (NSA_H + 6 * NSA_G) * NSA_D
    cols = np.concatenate([w[:, :a], w[:, a + ctl:kv], w[:, kv:kv + 3 * NSA_H], w[:, a:a + ctl],
                           np.zeros((D, 224), np.float32), w[:, kv + 3 * NSA_H:]], 1)
    out = {"w_in": cols.reshape(KT, P, -1, BANK).transpose(2, 1, 0, 3)}
    w1 = [f(n)[0].reshape(CMP_A, 2 * NSA_D, P).transpose(1, 0, 2) for n in ("cmp_w1_k", "cmp_w1_v")]
    out["cmp_w1"] = np.stack(w1, 1)
    out["cmp_w2"] = np.stack([f("cmp_w2_k")[0], f("cmp_w2_v")[0]], 1)
    out["w_branch"] = np.stack([tiles(f("w_branch_gdn")[0]), tiles(f("w_branch_nsa")[0])])
    out["w_out"] = f("w_out")[0].reshape(KT, P, 2, BANK).transpose(2, 1, 0, 3)
    gu = f("w_gate_up")[0].reshape(KT, P, 2, N_FC, FC)
    out["w_gu"] = gu.transpose(3, 1, 0, 2, 4)
    out["w_dn"] = f("w_down")[0].reshape(N_FC, FC // P, P, D).transpose(0, 2, 1, 3)
    out["w_in2"] = f("w_in_2")[0].reshape(KT, P, -1, BANK).transpose(2, 1, 0, 3)
    out["w_out2"] = f("w_out_2")[0].reshape(KT, P, 2, BANK).transpose(2, 1, 0, 3)
    pad = lambda v: np.concatenate([v, np.zeros((P - v.shape[0],) + v.shape[1:], np.float32)])
    i = np.arange(P)
    head = (i[:, None] // CMP_STRIDE == np.arange(NSA_H)[None]).astype(np.float32)
    n_blocks = NSA_G * N_CMP
    to = np.arange(2 * n_blocks)[None]
    add = ((i[:, None] // 64 == to // n_blocks) & (i[:, None] % 32 == to % n_blocks)).astype(np.float32)
    pos = [f(n)[0].reshape(CMP_A, P).T for n in ("cmp_pos_k", "cmp_pos_v")]
    one = np.ones((P, 2), np.float32)
    one[0, 1] = 0
    out["cols"] = np.concatenate(
        [feat(f(n)[0]) for n in ("mix_norm_gain", "ffn_norm_gain", "norm1_g_2", "norm2_g_2", "mix_g_2")]
        + [feat(f("gdn_conv_w")[0].reshape(-1)), feat(f("conv_w_2")[0].reshape(-1)), feat(f("conv_b_2")[0]),
           feat(f("f_bias_2")[0]), pad(np.stack([f("f_b_in_2")[0], f("f_b_mid_2")[0, 0], f("f_b_mid_2")[0, 1]], 1)),
           pad(f("f_freq_2")[0].T)] + pos + [one, head, add], 1)
    row = np.concatenate([f("gdn_a_log")[0], f("gdn_dt_bias")[0], f("gdn_out_norm_gain")[0], f("final_norm_gain"),
                          f("final_g_2"), f("b_group_2")[0], f("b_router_2")[0].reshape(-1),
                          np.arange(64, dtype=np.float32), np.arange(N_EXP, dtype=np.float32) - 1000])
    out["rows"] = np.broadcast_to(row, (P, row.size))
    out["filt_in"] = f("f_w_in_2")[0]
    out["filt_mid"] = f("f_w_mid_2")[0].transpose(1, 0, 2)
    out["filt_out"] = f("f_w_out_2")[0]
    router = np.concatenate([f("w_group_2")[0], f("w_router_2")[0].transpose(1, 0, 2).reshape(D, N_EXP)], 1)
    out["w_route"] = tiles(router)
    gate, up = (f(n)[0].reshape(N_EXP, KT, P, DE).transpose(0, 2, 1, 3) for n in ("w_gate_2", "w_up_2"))
    down = f("w_down_2")[0].reshape(N_EXP, DE // P, P, D).transpose(0, 2, 1, 3)
    out["w_exp"] = np.stack([gate.reshape(N_EXP, P, -1), up.reshape(N_EXP, P, -1), down.reshape(N_EXP, P, -1)], 2)
    out["x"] = f("x")[0].reshape(NB, P, D).transpose(1, 0, 2)
    return {k: np.ascontiguousarray(v, np.float32) for k, v in out.items()}


def kernel(**inputs):
    import numpy as np
    import concourse.bacc as bacc
    from concourse.bass_utils import run_bass_kernel_spmd as run

    arrays = {**_constants(np), **_layout(np, inputs)}
    nc = bacc.Bacc("TRN2", target_bir_lowering=False, num_devices=1)
    dram = {k: nc.dram_tensor(k, a.shape, F32, kind="ExternalInput").ap() for k, a in arrays.items()}
    dram["out"] = nc.dram_tensor("out", (P, NB, D), F32, kind="ExternalOutput").ap()
    two_layer_program(nc, dram)
    r = run(nc, [arrays], core_ids=[0])
    return r.results[0]["out"].transpose(1, 0, 2).reshape(1, T, D)
```
